# Optimizing a Trainium2 kernel written in Bass

```python
import math
import jax, jax.numpy as jnp
from jax import lax
import numpy as np

D_MODEL = 1024
BATCH = 1
SEQ = 2048
DEPTH = 1
DEC_BATCH = 8
DEC_SEQ = 8
PAST_LEN = 8192
PAGE_SIZE = 128

MIX_DIM = D_MODEL
SSD_D_INNER = MIX_DIM // 2
SSD_HEAD_DIM = 64
SSD_HEADS = SSD_D_INNER // SSD_HEAD_DIM
SSD_GROUPS = 2
SSD_HEADS_PER_GROUP = SSD_HEADS // SSD_GROUPS
D_STATE = 128
CONV_K = 4
CONV_DIM = SSD_D_INNER + 2 * SSD_GROUPS * D_STATE
CHUNK = 128
ATTN_DIM = MIX_DIM - SSD_D_INNER
ATTN_HEAD_DIM = 64
N_HEADS = ATTN_DIM // ATTN_HEAD_DIM
N_KV_HEADS = 2
Q_PER_KV = N_HEADS // N_KV_HEADS
KV_DIM = N_KV_HEADS * ATTN_HEAD_DIM
WINDOW = 128
N_BUCKETS = 32
MAX_EXACT = N_BUCKETS // 2
MAX_DISTANCE = 128
N_MEM = 256
CA_HEADS = 4
CA_HEAD_DIM = 128
CA_DIM = CA_HEADS * CA_HEAD_DIM
D_FF = -(-8 * D_MODEL // (3 * 256)) * 256
IN_DIM = SSD_D_INNER + CONV_DIM + SSD_HEADS + ATTN_DIM + 2 * KV_DIM
SPLITS = (SSD_D_INNER, SSD_D_INNER + CONV_DIM, SSD_D_INNER + CONV_DIM + SSD_HEADS,
          SSD_D_INNER + CONV_DIM + SSD_HEADS + ATTN_DIM,
          SSD_D_INNER + CONV_DIM + SSD_HEADS + ATTN_DIM + KV_DIM)
EPS = 1e-6

kernel_name = 'hymba_ssd_swa_sink_t5_xattn_step'

def rmsnorm(x, g):
    xf = x.astype(jnp.float32)
    y = xf * lax.rsqrt(jnp.mean(xf * xf, axis=-1, keepdims=True) + EPS)
    return (y * g.astype(jnp.float32)).astype(x.dtype)

def gated_group_rmsnorm(y, z, g):
    yf = y.astype(jnp.float32) * jax.nn.silu(z.astype(jnp.float32))
    yg = yf.reshape(yf.shape[:-1] + (SSD_GROUPS, SSD_D_INNER // SSD_GROUPS))
    yg = yg * lax.rsqrt(jnp.mean(yg * yg, axis=-1, keepdims=True) + EPS)
    return (yg.reshape(yf.shape) * g.astype(jnp.float32)).astype(z.dtype)

def ssd_scan(x, dt, A, B, C, h0):
    b, L = x.shape[:2]
    Q = CHUNK if L % CHUNK == 0 else L
    nc = L // Q
    G, Hg, P, N = SSD_GROUPS, SSD_HEADS_PER_GROUP, SSD_HEAD_DIM, D_STATE
    x = x.reshape(b, nc, Q, G, Hg, P)
    dt = dt.reshape(b, nc, Q, G, Hg)
    B = B.reshape(b, nc, Q, G, N)
    C = C.reshape(b, nc, Q, G, N)
    cs = jnp.cumsum(dt * A.reshape(G, Hg), axis=2)
    xdt = x * dt[..., None]
    causal = jnp.tril(jnp.ones((Q, Q), dtype=bool))[:, :, None, None]
    diff = cs[:, :, :, None] - cs[:, :, None, :]
    decay_qs = jnp.exp(jnp.where(causal, diff, -jnp.inf))
    cb = jnp.einsum('bcqgn,bcsgn->bcqsg', C, B)
    y_diag = jnp.einsum('bcqsgh,bcsghp->bcqghp', cb[..., None] * decay_qs, xdt)
    decay_end = jnp.exp(cs[:, :, -1:] - cs)
    st = jnp.einsum('bcsgn,bcsghp->bcghpn', B, xdt * decay_end[..., None])
    chunk_decay = jnp.exp(cs[:, :, -1])

    def step(h, inp):
        dec, s = inp
        return dec[..., None, None] * h + s, h

    h_final, h_starts = lax.scan(step, h0.reshape(b, G, Hg, P, N),
                                 (jnp.moveaxis(chunk_decay, 1, 0), jnp.moveaxis(st, 1, 0)))
    h_starts = jnp.moveaxis(h_starts, 0, 1)
    y_off = jnp.einsum('bcqgn,bcghpn->bcqghp', C, h_starts) * jnp.exp(cs)[..., None]
    y = (y_diag + y_off).reshape(b, L, SSD_HEADS, P)
    return y, h_final.reshape(b, SSD_HEADS, P, N)

def ssd_branch(z, xbc, dt_raw, conv_prev, ssm_prev, conv_w, conv_b, dt_bias, a_log, d_skip, g_norm):
    b, L, _ = xbc.shape
    xp = jnp.concatenate([conv_prev.astype(xbc.dtype), xbc], axis=1)
    conv = conv_b.astype(jnp.float32)
    for k in range(CONV_K):
        conv = conv + xp[:, k:k + L].astype(jnp.float32) * conv_w[k].astype(jnp.float32)
    conv = jax.nn.silu(conv)
    new_conv = xp[:, L:].astype(conv_prev.dtype)
    xs, Bm, Cm = jnp.split(conv, [SSD_D_INNER, SSD_D_INNER + SSD_GROUPS * D_STATE], axis=-1)
    xs = xs.reshape(b, L, SSD_HEADS, SSD_HEAD_DIM)
    Bm = Bm.reshape(b, L, SSD_GROUPS, D_STATE)
    Cm = Cm.reshape(b, L, SSD_GROUPS, D_STATE)
    dt = jax.nn.softplus(dt_raw.astype(jnp.float32) + dt_bias.astype(jnp.float32))
    A = -jnp.exp(a_log.astype(jnp.float32))
    y, new_ssm = ssd_scan(xs, dt, A, Bm, Cm, ssm_prev.astype(jnp.float32))
    y = y + d_skip.astype(jnp.float32)[:, None] * xs
    y = gated_group_rmsnorm(y.reshape(b, L, SSD_D_INNER), z, g_norm)
    return y, new_conv, new_ssm.astype(ssm_prev.dtype)

def t5_bucket(dist):
    n = jnp.maximum(dist, 0)
    large = MAX_EXACT + (jnp.log(jnp.maximum(n, 1).astype(jnp.float32) / MAX_EXACT)
                         / math.log(MAX_DISTANCE / MAX_EXACT) * (N_BUCKETS - MAX_EXACT)).astype(jnp.int32)
    large = jnp.minimum(large, N_BUCKETS - 1)
    return jnp.where(n < MAX_EXACT, n, large)

def rel_bias_logits(rel_bias, dist):
    bias = rel_bias.astype(jnp.float32)[t5_bucket(dist)]
    q_len, s_len = dist.shape
    return jnp.transpose(bias, (2, 0, 1)).reshape(N_KV_HEADS, Q_PER_KV, q_len, s_len)

def sink_attention(q, k, v, bias, mask, sinks):
    s = jnp.einsum('...qkgd,...skd->...kgqs', q, k).astype(jnp.float32) * (ATTN_HEAD_DIM ** -0.5) + bias
    s = jnp.where(mask, s, -jnp.inf)
    sk = sinks.astype(jnp.float32)[:, :, None, None]
    m = jnp.maximum(jnp.max(s, axis=-1, keepdims=True), sk)
    p = jnp.exp(s - m)
    p = p / (jnp.sum(p, axis=-1, keepdims=True) + jnp.exp(sk - m))
    return jnp.einsum('...kgqs,...skd->...qkgd', p.astype(v.dtype), v)

def swa_banded(q, k, v, sinks, rel_bias):
    b, L = q.shape[:2]
    nb = L // WINDOW
    qb = q.reshape(b, nb, WINDOW, N_KV_HEADS, Q_PER_KV, ATTN_HEAD_DIM)

    def band(t):
        tp = jnp.concatenate([jnp.zeros((b, WINDOW) + t.shape[2:], t.dtype), t], axis=1)
        tp = tp.reshape(b, nb + 1, WINDOW, N_KV_HEADS, ATTN_HEAD_DIM)
        return jnp.concatenate([tp[:, :-1], tp[:, 1:]], axis=2)

    kb, vb = band(k), band(v)
    j = jnp.arange(2 * WINDOW)
    dist = jnp.arange(WINDOW)[:, None] + WINDOW - j[None, :]
    inband = (dist >= 0) & (dist < WINDOW)
    key_pos = jnp.arange(nb)[:, None] * WINDOW - WINDOW + j[None, :]
    mask = inband[None] & (key_pos >= 0)[:, None, :]
    out = sink_attention(qb, kb, vb, rel_bias_logits(rel_bias, dist), mask[:, None, None], sinks)
    return out.reshape(b, L, ATTN_DIM)

def swa_with_buffer(q, k, v, k_buf, v_buf, sinks, rel_bias):
    b, T = q.shape[:2]
    lb = k_buf.shape[1]
    kk = jnp.concatenate([k_buf.astype(k.dtype), k], axis=1)
    vv = jnp.concatenate([v_buf.astype(v.dtype), v], axis=1)
    dist = jnp.arange(T)[:, None] + lb - jnp.arange(lb + T)[None, :]
    mask = (dist >= 0) & (dist < WINDOW)
    out = sink_attention(q, kk, vv, rel_bias_logits(rel_bias, dist), mask, sinks)
    return out.reshape(b, T, ATTN_DIM), kk[:, T:].astype(k_buf.dtype), vv[:, T:].astype(v_buf.dtype)

def memory_kv(mem, g_mem, w_ck, w_cv):
    b, m, _ = mem.shape
    mn = rmsnorm(mem, g_mem)
    return ((mn @ w_ck).reshape(b, m, CA_HEADS, CA_HEAD_DIM),
            (mn @ w_cv).reshape(b, m, CA_HEADS, CA_HEAD_DIM))

def cross_attention(hn, mem_k, mem_v, w_cq, w_co):
    b, L, _ = hn.shape
    q = (hn @ w_cq).reshape(b, L, CA_HEADS, CA_HEAD_DIM)
    s = jnp.einsum('blhd,bmhd->bhlm', q, mem_k.astype(q.dtype)).astype(jnp.float32) * (CA_HEAD_DIM ** -0.5)
    p = jax.nn.softmax(s, axis=-1).astype(q.dtype)
    o = jnp.einsum('bhlm,bmhd->blhd', p, mem_v.astype(q.dtype))
    return o.reshape(b, L, CA_DIM) @ w_co

def decoder_layer(h, mem_k, mem_v, conv_prev, ssm_prev, k_buf, v_buf, rel_bias,
                  g_mix, w_in, conv_w, conv_b, dt_bias, a_log, d_skip, g_ssd_norm, sinks, w_out,
                  g_cross, w_cq, w_co, g_ffn, w_gate, w_up, w_down):
    b, L, _ = h.shape
    xn = rmsnorm(h, g_mix)
    z, xbc, dt_raw, q, k, v = jnp.split(xn @ w_in, SPLITS, axis=-1)
    y_ssd, new_conv, new_ssm = ssd_branch(z, xbc, dt_raw, conv_prev, ssm_prev, conv_w, conv_b,
                                          dt_bias, a_log, d_skip, g_ssd_norm)
    q = q.reshape(b, L, N_KV_HEADS, Q_PER_KV, ATTN_HEAD_DIM)
    k = k.reshape(b, L, N_KV_HEADS, ATTN_HEAD_DIM)
    v = v.reshape(b, L, N_KV_HEADS, ATTN_HEAD_DIM)
    sk = sinks.reshape(N_KV_HEADS, Q_PER_KV)
    if k_buf is None:
        y_att = swa_banded(q, k, v, sk, rel_bias)
        keep = min(WINDOW, L)
        new_k, new_v = k[:, L - keep:], v[:, L - keep:]
    else:
        y_att, new_k, new_v = swa_with_buffer(q, k, v, k_buf, v_buf, sk, rel_bias)
    mix = jnp.concatenate([y_ssd.astype(h.dtype), y_att.astype(h.dtype)], axis=-1)
    h = h + mix @ w_out
    h = h + cross_attention(rmsnorm(h, g_cross), mem_k, mem_v, w_cq, w_co)
    hn = rmsnorm(h, g_ffn)
    h = h + (jax.nn.silu(hn @ w_gate) * (hn @ w_up)) @ w_down
    return h, new_conv, new_ssm, new_k, new_v

def setup_inputs(seed: int = 0) -> dict:
    key = jax.random.key(seed)
    ks = iter(jax.random.split(key, 40))
    f32 = jnp.float32

    def nrm(shape, scale):
        return jax.random.normal(next(ks), shape, f32) * scale

    def gain(shape):
        return 1.0 + nrm(shape, 0.02)

    swa_buf = min(WINDOW, PAST_LEN)
    u = jax.random.uniform(next(ks), (DEPTH, SSD_HEADS), f32)
    dt0 = jnp.exp(u * (math.log(0.1) - math.log(0.001)) + math.log(0.001))
    dt_bias = dt0 + jnp.log(-jnp.expm1(-dt0))
    a_log = jnp.log(jax.random.uniform(next(ks), (DEPTH, SSD_HEADS), f32, minval=1.0, maxval=16.0))
    return {
        'x_prompt': nrm((BATCH, SEQ, D_MODEL), 1.0),
        'x_sample': nrm((DEC_BATCH, DEC_SEQ, D_MODEL), 1.0),
        'mem_prompt': nrm((BATCH, N_MEM, D_MODEL), 1.0),
        'state_conv': nrm((DEPTH, DEC_BATCH, CONV_K - 1, CONV_DIM), 1.0),
        'state_ssm': nrm((DEPTH, DEC_BATCH, SSD_HEADS, SSD_HEAD_DIM, D_STATE), 0.1),
        'cache_swa_k': nrm((DEPTH, DEC_BATCH, swa_buf, N_KV_HEADS, ATTN_HEAD_DIM), 1.0),
        'cache_swa_v': nrm((DEPTH, DEC_BATCH, swa_buf, N_KV_HEADS, ATTN_HEAD_DIM), 1.0),
        'cache_mem_k': nrm((DEPTH, DEC_BATCH, N_MEM, CA_HEADS, CA_HEAD_DIM), 1.0),
        'cache_mem_v': nrm((DEPTH, DEC_BATCH, N_MEM, CA_HEADS, CA_HEAD_DIM), 1.0),
        'rel_bias': nrm((N_BUCKETS, N_HEADS), 0.5),
        'g_mix': gain((DEPTH, D_MODEL)),
        'w_in': nrm((DEPTH, D_MODEL, IN_DIM), D_MODEL ** -0.5),
        'conv_w': nrm((DEPTH, CONV_K, CONV_DIM), CONV_K ** -0.5),
        'conv_b': nrm((DEPTH, CONV_DIM), 0.02),
        'dt_bias': dt_bias,
        'a_log': a_log,
        'd_skip': 1.0 + nrm((DEPTH, SSD_HEADS), 0.1),
        'g_ssd_norm': gain((DEPTH, SSD_D_INNER)),
        'sinks': nrm((DEPTH, N_HEADS), 0.5),
        'w_out': nrm((DEPTH, MIX_DIM, D_MODEL), MIX_DIM ** -0.5),
        'g_cross': gain((DEPTH, D_MODEL)),
        'g_mem': gain((DEPTH, D_MODEL)),
        'w_cq': nrm((DEPTH, D_MODEL, CA_DIM), D_MODEL ** -0.5),
        'w_ck': nrm((DEPTH, D_MODEL, CA_DIM), D_MODEL ** -0.5),
        'w_cv': nrm((DEPTH, D_MODEL, CA_DIM), D_MODEL ** -0.5),
        'w_co': nrm((DEPTH, CA_DIM, D_MODEL), CA_DIM ** -0.5),
        'g_ffn': gain((DEPTH, D_MODEL)),
        'w_gate': nrm((DEPTH, D_MODEL, D_FF), D_MODEL ** -0.5),
        'w_up': nrm((DEPTH, D_MODEL, D_FF), D_MODEL ** -0.5),
        'w_down': nrm((DEPTH, D_FF, D_MODEL), D_FF ** -0.5),
        'g_final': gain((D_MODEL,)),
    }

def reference(x_prompt, x_sample, mem_prompt, state_conv, state_ssm, cache_swa_k, cache_swa_v,
              cache_mem_k, cache_mem_v, rel_bias, g_mix, w_in, conv_w, conv_b, dt_bias, a_log,
              d_skip, g_ssd_norm, sinks, w_out, g_cross, g_mem, w_cq, w_ck, w_cv, w_co, g_ffn,
              w_gate, w_up, w_down, g_final):
    bp = x_prompt.shape[0]
    hp, hs = x_prompt, x_sample
    p_conv, p_ssm, p_k, p_v, p_mk, p_mv = [], [], [], [], [], []
    s_conv, s_ssm, s_k, s_v = [], [], [], []
    for l in range(DEPTH):
        lw = (g_mix[l], w_in[l], conv_w[l], conv_b[l], dt_bias[l], a_log[l], d_skip[l], g_ssd_norm[l],
              sinks[l], w_out[l], g_cross[l], w_cq[l], w_co[l], g_ffn[l], w_gate[l], w_up[l], w_down[l])
        mk, mv = memory_kv(mem_prompt, g_mem[l], w_ck[l], w_cv[l])
        conv0 = jnp.zeros((bp, CONV_K - 1, CONV_DIM), x_prompt.dtype)
        ssm0 = jnp.zeros((bp, SSD_HEADS, SSD_HEAD_DIM, D_STATE), jnp.float32)
        hp, c_new, h_new, k_new, v_new = decoder_layer(hp, mk, mv, conv0, ssm0, None, None, rel_bias, *lw)
        p_conv.append(c_new); p_ssm.append(h_new); p_k.append(k_new); p_v.append(v_new)
        p_mk.append(mk); p_mv.append(mv)
        hs, c_new, h_new, k_new, v_new = decoder_layer(hs, cache_mem_k[l], cache_mem_v[l], state_conv[l],
                                                       state_ssm[l], cache_swa_k[l], cache_swa_v[l],
                                                       rel_bias, *lw)
        s_conv.append(c_new); s_ssm.append(h_new); s_k.append(k_new); s_v.append(v_new)
    y_prompt = rmsnorm(hp, g_final)
    y_sample = rmsnorm(hs, g_final)
    return (y_prompt, y_sample,
            jnp.stack(p_conv), jnp.stack(p_ssm), jnp.stack(p_k), jnp.stack(p_v),
            jnp.stack(p_mk), jnp.stack(p_mv),
            jnp.stack(s_conv), jnp.stack(s_ssm), jnp.stack(s_k), jnp.stack(s_v))


_drawn_inputs = setup_inputs


def setup_inputs(seed=0):
    import zlib

    import numpy as np

    out = dict(_drawn_inputs(seed))
    spreads = {}
    factors = {'g_ssd_norm': 4.676,
     'sinks': 8.0,
     'g_cross': 8.0,
     'g_mem': 2.75,
     'g_ffn': 4.476,
     'g_final': 2.764}
    for name, (base, spread) in spreads.items():
        noise = np.random.default_rng([zlib.crc32(name.encode()), seed]).standard_normal(out[name].shape)
        drawn = base * np.exp(spread * noise) if base else spread * noise
        out[name] = __import__('jax').numpy.asarray(drawn.astype(out[name].dtype))
    for name, factor in factors.items():
        out[name] = (out[name] * factor).astype(out[name].dtype)
    return out
```

```python
from contextlib import ExitStack

import concourse.bass as bass
from concourse import mybir

F32 = mybir.dt.float32
F32R = mybir.dt.float32r
I32 = mybir.dt.int32
ALU = mybir.AluOpType
ACT = mybir.ActivationFunctionType
AX_X = mybir.AxisListType.X

P = 128
D = 1024
KT = D // P
SEQ = 2048
TB = 512
NBLK = SEQ // TB
C = TB // P
NB, TS = 8, 8
S = NB * TS
HS = 8
HP = 64
NST = 128
CONVD = 1024
KV = 2
QJ = 4
WIN = 128
NMEM = 256
CH = 4
DFF = 2816
FT = DFF // P
EPS = 1e-6
NEG = -1e30
COL_Z, COL_X, COL_DT, COL_Q, COL_K, COL_V = 0, 512, 1536, 1544, 2056, 2184
RING = 3
AHEAD = 2
FGROUPS = [(0, 8), (8, 16), (16, 22)]
RLEN = 383

PV_MIX, PV_CROSS, PV_FFN, PV_FINAL, PV_MEM, PV_CB, PV_CW, PV_SSD = 0, 8, 16, 24, 32, 40, 48, 80
PV_ROWS = 84


def weight_panels(w_in, w_out, w_cq, w_co, w_gate, w_up, w_down):
    def cols(w, c, n=P):
        return w[:, c:c + n].rearrange("(k p) n -> p k n", p=P)

    panels = []
    for i in range(8):
        panels.append(([(0, KT, 0, P, cols(w_in, COL_X + i * P))], KT, 1))
    panels.append(([(0, KT, 0, P, cols(w_in, COL_K))], KT, 1))
    panels.append(([(0, KT, 0, P, cols(w_in, COL_V))], KT, 1))
    for j in range(QJ):
        panels.append(([(0, KT, 0, 64, cols(w_in, COL_Q + 64 * j, 64)),
                        (0, KT, 64, 64, cols(w_in, COL_Q + 256 + 64 * j, 64))], KT, 1))
    for i in range(4):
        panels.append(([(0, KT, 0, P, cols(w_in, COL_Z + i * P))], KT, 1))
    for n in range(KT):
        c = slice(n * P, n * P + P)
        top = w_out[0:512, c].rearrange("(k p) n -> p k n", p=P)
        att = w_out[512:1024, c].rearrange("(v j d) n -> v d j n", v=KV, j=QJ)
        panels.append(([(0, 4, 0, P, top), ("kv", att)], KT, 1))
    for n in range(CH):
        panels.append(([(0, KT, 0, P, cols(w_cq, n * P))], KT, 1))
    for n in range(4):
        panels.append(([("wide", w_co[:, n * 256:n * 256 + 256].rearrange("(k p) n -> p k n", p=P))], 4, 2))
    for f0, f1 in FGROUPS:
        for f in range(f0, f1):
            panels.append(([(0, KT, 0, P, cols(w_gate, f * P))], KT, 1))
            panels.append(([(0, KT, 0, P, cols(w_up, f * P))], KT, 1))
        for n in range(KT):
            src = w_down[f0 * P:f1 * P, n * P:n * P + P].rearrange("(k p) n -> p k n", p=P)
            panels.append(([(0, f1 - f0, 0, P, src)], f1 - f0, 1))
    return panels


def panel_slices(slot, parts):
    tiles = slot.rearrange("p (k n) -> p k n", n=P)
    out = []
    for part in parts:
        if part[0] == "kv":
            for v in range(KV):
                out.append((tiles[64 * v:64 * v + 64, 4:8, :], part[1][v]))
        elif part[0] == "wide":
            out.append((slot.rearrange("p (k n) -> p k n", n=256), part[1]))
        else:
            k0, kn, c0, cn, src = part
            out.append((tiles[:, k0:k0 + kn, c0:c0 + cn], src))
    return out


def rsqrt(dve, v, r, t):
    dve.tensor_scalar(r.bitcast(I32), v.bitcast(I32), 1, None, ALU.arith_shift_right)
    dve.drain()
    dve.tensor_scalar(r.bitcast(I32), r.bitcast(I32), -1.0, float(0x5F3759DF), ALU.mult, ALU.add)
    dve.drain()
    for _ in range(3):
        dve.scalar_tensor_tensor(t, r, -0.5, r, ALU.mult, ALU.mult)
        dve.drain()
        dve.tensor_tensor(t, t, v, ALU.mult)
        dve.drain()
        dve.scalar_tensor_tensor(r, t, 1.5, r, ALU.add, ALU.mult)
        dve.drain()


def build(nc, x_prompt, x_sample, mem_prompt, state_conv, state_ssm, cache_swa_k, cache_swa_v,
          cache_mem_k, cache_mem_v, rel_bias, g_mix, w_in, conv_w, conv_b, dt_bias, a_log, d_skip,
          g_ssd_norm, sinks, w_out, g_cross, g_mem, w_cq, w_ck, w_cv, w_co, g_ffn, w_gate, w_up, w_down,
          g_final, bucket_onehot, row_mask,
          y_prompt, y_sample, p_conv, p_ssm, p_swa_k, p_swa_v, p_mem_k, p_mem_v,
          s_conv, s_ssm, s_swa_k, s_swa_v):
    w_in, w_out, w_cq, w_ck, w_cv, w_co = (w[0] for w in (w_in, w_out, w_cq, w_ck, w_cv, w_co))
    w_gate, w_up, w_down = w_gate[0], w_up[0], w_down[0]
    bias_rows = nc.dram_tensor("bias_rows", [HS, RLEN], F32)
    panels = weight_panels(w_in, w_out, w_cq, w_co, w_gate, w_up, w_down)
    NPAN = len(panels)
    first_out = [sum(p[2] for p in panels[:n]) for n in range(NPAN + 1)]
    first_dma = {}
    on_slot = [0] * RING
    for n, (parts, _, _) in enumerate(panels):
        on_slot[n % RING] += sum(KV if part[0] == "kv" else 1 for part in parts)
        first_dma[n] = on_slot[n % RING]
    PAN_XBC, PAN_K, PAN_V, PAN_Q, PAN_Z, PAN_OUT = 0, 8, 9, 10, 14, 18
    PAN_CQ, PAN_CO, PAN_FFN = 26, 30, 34

    with ExitStack() as whole:
        def sb(name, shape, dt=F32, scope=whole):
            return scope.enter_context(nc.sbuf_tensor(name, shape, dt))

        G = whole.enter_context(nc.psum_tensor("G", [P, 6, 512], F32))
        L = whole.enter_context(nc.psum_tensor("L", [P, 2, 512], F32))

        ident = sb("ident", [P, P])
        ones = sb("ones", [P, P])
        tri_le = sb("tri_le", [P, P])
        tri_gt = sb("tri_gt", [P, P])
        pv = sb("pv", [P, PV_ROWS])
        dtb = sb("dtb", [P, HS])
        nega = sb("nega", [P, HS])
        dsk = sb("dsk", [P, HS])
        snk = sb("snk", [P, HS])
        wdt = sb("wdt", [P, KT, HS])
        wdt_h = sb("wdt_h", [P, KT, HS], F32R)
        wdt_l = sb("wdt_l", [P, KT, HS], F32R)
        small = sb("small", [P, 12, 16])
        diag = sb("diag", [P, TB])

        def g_of(row, i):
            return pv[:, row + i:row + i + 1]

        phase_count = [0]

        def clear(sems):
            nums = sorted(x.num for x in sems)
            cuts = [0] + [i for i in range(1, len(nums)) if nums[i] != nums[i - 1] + 1] + [len(nums)]
            runs = [range(nums[a], nums[b - 1] + 1) for a, b in zip(cuts, cuts[1:])]
            for run in runs[:-1]:
                nc.gpsimd.sem_clear(run)
            nc.all_engine_barrier(sems_to_clear=runs[-1])

        class Phase:

            def __init__(self, names):
                phase_count[0] += 1
                self.stack = ExitStack()
                self.names = names

            def __enter__(self):
                tag = f"_{phase_count[0]}"
                sems = [self.stack.enter_context(nc.semaphore(n + tag)) for n in self.names]
                self.sems = sems
                self.of = dict(zip(self.names, sems))
                self.block = nc.Block(no_gpsimd_drain=True)
                self.blk = self.block.__enter__()
                return self.blk, self.of

            def __exit__(self, *exc):
                self.block.__exit__(*exc)
                clear(self.sems)
                self.stack.close()

        prompt = whole.enter_context(ExitStack())
        bias_prev = sb("bias_prev", [P, HS, WIN], scope=prompt)
        bias_first = sb("bias_first", [P, HS, WIN], scope=prompt)
        bias_cur = sb("bias_cur", [P, HS, WIN], scope=prompt)
        kmT = sb("kmT", [P, CH, NMEM], scope=prompt)
        vm = sb("vm", [P, 2, CH * P], scope=prompt)
        kbuf = sb("kbuf", [P, WIN + TB], scope=prompt)
        vtok = sb("vtok", [P, 1 + C, P], scope=prompt)
        carry = sb("carry", [P, 8, 3], scope=prompt)
        state = sb("state", [P, HS * HP], scope=prompt)

        with ExitStack() as tmp:
            pvrow = sb("pvrow", [PV_ROWS, P], scope=tmp)
            alog = sb("alog", [P, HS], scope=tmp)
            table = sb("table", [32, HS], scope=tmp)
            onehot = sb("onehot", [32, RLEN], scope=tmp)
            rmask = sb("rmask", [HS, RLEN], scope=tmp)
            rrow = sb("rrow", [HS, RLEN], scope=tmp)
            mem = sb("mem", [P, 2, D], scope=tmp)
            memn = sb("memn", [P, 2, D], scope=tmp)
            mnT = sb("mnT", [P, KT, NMEM], scope=tmp)
            wck_sb = sb("wck_sb", [P, KT, CH * P], scope=tmp)
            wcv_sb = sb("wcv_sb", [P, KT, CH * P], scope=tmp)
            kmtok = sb("kmtok", [P, 2, CH * P], scope=tmp)
            toep = sb("toep", [P, HS, 2 * WIN], scope=tmp)
            flip = sb("flip", [P, P], scope=tmp)
            with Phase(["par_in", "mem_in", "wck_in", "wcv_in", "bias_in", "rows_out", "made", "consts",
                        "params", "ssq", "normed", "mt", "mtsb", "kps", "kev", "vps", "vev", "ktp", "ktev",
                        "rps", "rsb", "out_done", "bias_done", "flipped"]) as (b, s):
                par = 0

                @b.sync
                def _(sp):
                    loads = [(pvrow[PV_MIX:PV_MIX + 8, :], g_mix[0].rearrange("(t p) -> t p", p=P)),
                             (pvrow[PV_CROSS:PV_CROSS + 8, :], g_cross[0].rearrange("(t p) -> t p", p=P)),
                             (pvrow[PV_FFN:PV_FFN + 8, :], g_ffn[0].rearrange("(t p) -> t p", p=P)),
                             (pvrow[PV_FINAL:PV_FINAL + 8, :], g_final.rearrange("(t p) -> t p", p=P)),
                             (pvrow[PV_MEM:PV_MEM + 8, :], g_mem[0].rearrange("(t p) -> t p", p=P)),
                             (pvrow[PV_CB:PV_CB + 8, :], conv_b[0].rearrange("(t p) -> t p", p=P)),
                             (pvrow[PV_CW:PV_CW + 32, :], conv_w[0].rearrange("k (t p) -> (k t) p", p=P)),
                             (pvrow[PV_SSD:PV_SSD + 4, :], g_ssd_norm[0].rearrange("(t p) -> t p", p=P)),
                             (dtb[:], dt_bias.to_broadcast([P, HS])),
                             (alog[:], a_log.to_broadcast([P, HS])),
                             (dsk[:], d_skip.to_broadcast([P, HS])),
                             (snk[:], sinks.to_broadcast([P, HS])),
                             (wdt[:], w_in[:, COL_DT:COL_DT + HS].rearrange("(k p) n -> p k n", p=P)),
                             (table[:], rel_bias), (onehot[:], bucket_onehot), (rmask[:], row_mask)]
                    assert len(loads) == 16
                    for dst, src in loads:
                        sp.dma_start(dst, src).then_inc(s["par_in"], 16)
                    sp.dma_start(mem[:], mem_prompt[0].rearrange("(c p) d -> p c d", p=P)).then_inc(s["mem_in"], 16)
                    sp.dma_start(wck_sb[:], w_ck.rearrange("(k p) n -> p k n", p=P)).then_inc(s["wck_in"], 16)
                    sp.dma_start(wcv_sb[:], w_cv.rearrange("(k p) n -> p k n", p=P)).then_inc(s["wcv_in"], 16)
                    sp.wait_ge(s["rsb"], 1)
                    sp.dma_start(bias_rows.ap(), rrow[:]).then_inc(s["rows_out"], 16)
                    sp.wait_ge(s["rows_out"], 16)
                    sp.dma_start(toep[:], bass.AP(tensor=bias_rows, offset=0,
                                                  ap=[[1, P], [RLEN, HS], [1, 2 * WIN]])).then_inc(s["bias_in"], 16)
                    sp.wait_ge(s["vev"], 2)
                    sp.dma_start(p_mem_v[0, 0].rearrange("(c p) h d -> p c (h d)", p=P), vm[:])\
                      .then_inc(s["out_done"], 16)
                    sp.wait_ge(s["ktev"], 2)
                    sp.dma_start(p_mem_k[0, 0].rearrange("(c p) h d -> p c (h d)", p=P), kmtok[:])\
                      .then_inc(s["out_done"], 16)
                    sp.wait_ge(s["out_done"], 32)

                @b.gpsimd
                def _(pool):
                    pool.memset(ones[:], 1.0).then_inc(s["made"], 1)
                    pool.memset(ident[:], 0.0).then_inc(s["made"], 1)
                    pool.memset(flip[:], 0.0).then_inc(s["made"], 1)
                    pool.memset(bias_first[:], NEG)
                    pool.memset(kbuf[:, 0:WIN], 0.0)
                    pool.memset(vtok[:, 0, :], 0.0)
                    pool.memset(carry[:], 0.0)
                    pool.memset(state[:], 0.0)
                    pool.wait_ge(s["made"], 3)
                    pool.affine_select(out=ident[:], in_=ident[:], compare_op=ALU.not_equal, fill=1.0, base=0,
                                       pattern=[[-1, P]], channel_multiplier=1)
                    pool.affine_select(out=flip[:], in_=flip[:], compare_op=ALU.not_equal, fill=1.0, base=1 - P,
                                       pattern=[[1, P]], channel_multiplier=1)
                    pool.affine_select(out=tri_le[:], in_=ones[:], compare_op=ALU.is_ge, fill=0.0, base=0,
                                       pattern=[[1, P]], channel_multiplier=-1)
                    pool.affine_select(out=tri_gt[:], in_=ones[:], compare_op=ALU.is_ge, fill=0.0, base=-1,
                                       pattern=[[-1, P]], channel_multiplier=1).then_inc(s["consts"], 1)

                @b.scalar
                def _(act):
                    act.wait_ge(s["par_in"], 256)
                    act.activation(alog[:], alog[:], ACT.Exp).then_inc(s["params"], 1)
                    act.wait_ge(s["mem_in"], 16)
                    for c in range(2):
                        act.activation(memn[:, c, :], mem[:, c, :], ACT.Square, accum_out=small[:, 0, c:c + 1])\
                           .then_inc(s["ssq"], 1)
                    for i in range(KT):
                        act.wait_ge(s["mt"], i + 1)
                        act.activation(mnT[:, i, :], G[:, i % 2, 0:NMEM], ACT.Copy, scale=g_of(PV_MEM, i))\
                           .then_inc(s["mtsb"], 1)
                    for h in range(CH):
                        act.wait_ge(s["kps"], h + 1)
                        act.activation(kmT[:, h, :], G[:, 2 + h % 2, 0:NMEM], ACT.Copy).then_inc(s["kev"], 1)
                    for c in range(2):
                        act.wait_ge(s["vps"], c + 1)
                        act.activation(vm[:, c, :], G[:, 4 + c, :], ACT.Copy).then_inc(s["vev"], 1)

                @b.vector
                def _(dve):
                    dve.wait_ge(s["par_in"], 256)
                    dve.tensor_copy(wdt_h[:], wdt[:])
                    dve.drain()
                    dve.tensor_tensor(wdt_l[:], wdt[:], wdt_h[:].bitcast(F32), ALU.subtract)
                    dve.wait_ge(s["params"], 1)
                    dve.tensor_scalar(nega[:], alog[:], -1.0, None, ALU.mult)
                    dve.wait_ge(s["rps"], 1)
                    dve.tensor_tensor(rrow[:], L[0:HS, 0, 0:RLEN], rmask[:], ALU.add).then_inc(s["rsb"], 1)
                    dve.wait_ge(s["rps"], 2)
                    dve.tensor_copy(pv[:], L[:, 1, 0:PV_ROWS]).then_inc(s["rsb"], 1)
                    dve.wait_ge(s["ssq"], 2)
                    v, r, t = small[:, 1, 0:2], small[:, 2, 0:2], small[:, 3, 0:2]
                    dve.tensor_scalar(v, small[:, 0, 0:2], 1.0 / D, EPS, ALU.mult, ALU.add)
                    dve.drain()
                    rsqrt(dve, v, r, t)
                    for c in range(2):
                        dve.tensor_scalar(memn[:, c, :], mem[:, c, :], r[:, c:c + 1], None, ALU.mult)\
                           .then_inc(s["normed"], 1)
                    for c in range(2):
                        dve.wait_ge(s["ktp"], c + 1)
                        dve.tensor_copy(kmtok[:, c, :], L[:, c, :]).then_inc(s["ktev"], 1)
                    for n in range(4):
                        dve.wait_ge(s["flipped"], n + 1)
                        src = G[:, n % 2, :].rearrange("p (h k) -> p h k", h=2)
                        dve.tensor_copy(bias_prev[:, 2 * n:2 * n + 2, :], src[:, :, 0:WIN])
                        dve.tensor_copy(bias_cur[:, 2 * n:2 * n + 2, :], src[:, :, WIN:2 * WIN])\
                           .then_inc(s["bias_done"], 1)

                @b.tensor
                def _(pe):
                    pe.wait_ge(s["par_in"], 256)
                    pe.wait_ge(s["consts"], 1)
                    pe.matmul(L[0:HS, 0, 0:RLEN], table[:], onehot[:], start=True, stop=True)\
                      .then_inc(s["rps"], 1)
                    pe.transpose(L[:, 1, 0:PV_ROWS], pvrow[:], ident[0:PV_ROWS, 0:PV_ROWS]).then_inc(s["rps"], 1)
                    pe.wait_ge(s["normed"], 2)
                    pe.wait_ge(s["rsb"], 2)
                    for i in range(KT):
                        if i >= 2:
                            pe.wait_ge(s["mtsb"], i - 1)
                        for c in range(2):
                            last = pe.transpose(G[:, i % 2, c * P:c * P + P], memn[:, c, i * P:i * P + P], ident[:])
                        last.then_inc(s["mt"], 1)
                    pe.wait_ge(s["mtsb"], KT)
                    pe.wait_ge(s["wck_in"], 16)
                    for h in range(CH):
                        if h >= 2:
                            pe.wait_ge(s["kev"], h - 1)
                        for k in range(KT):
                            last = pe.matmul(G[:, 2 + h % 2, 0:NMEM], wck_sb[:, k, h * P:h * P + P], mnT[:, k, :],
                                             start=(k == 0), stop=(k == KT - 1))
                        last.then_inc(s["kps"], 1)
                    pe.wait_ge(s["wcv_in"], 16)
                    for c in range(2):
                        for k in range(KT):
                            last = pe.matmul(G[:, 4 + c, :], mnT[:, k, c * P:c * P + P], wcv_sb[:, k, :],
                                             start=(k == 0), stop=(k == KT - 1))
                        last.then_inc(s["vps"], 1)
                    pe.wait_ge(s["kev"], CH)
                    for c in range(2):
                        for h in range(CH):
                            last = pe.transpose(L[:, c, h * P:h * P + P], kmT[:, h, c * P:c * P + P], ident[:])
                        last.then_inc(s["ktp"], 1)
                    pe.wait_ge(s["bias_in"], 16)
                    for n in range(4):
                        if n >= 2:
                            pe.wait_ge(s["bias_done"], n - 1)
                        pe.matmul(G[:, n % 2, :], flip[:], toep[:, 2 * n:2 * n + 2, :], start=True, stop=True)\
                          .then_inc(s["flipped"], 1)

        with nc.Fori(0, NBLK) as blk, ExitStack() as body:
            hT = sb("hT", [P, KT, TB], scope=body)
            xh = sb("xh", [P, KT, TB], F32R, scope=body)
            xl = sb("xl", [P, KT, TB], F32R, scope=body)
            w_raw = sb("w_raw", [P, RING, D], scope=body)
            w_hi = sb("w_hi", [P, RING, D], F32R, scope=body)
            w_lo = sb("w_lo", [P, RING, D], F32R, scope=body)
            ntmp = sb("ntmp", [P, 2, TB], scope=body)
            sq = sb("sq", [P, 2, TB], scope=body)
            sqsum = sb("sqsum", [P, TB], scope=body)

            stream_names = [f"w_in_slot{r}" for r in range(RING)] + ["hi_ready", "lo_ready", "lin_out"]
            stream = {n: body.enter_context(nc.semaphore(n)) for n in stream_names}

            def load_panels(sp, a, z):
                for n in range(a, min(z, NPAN)):
                    if n >= RING:
                        sp.wait_ge(stream["lo_ready"], n - RING + 1)
                    for dst, src in panel_slices(w_raw[:, n % RING, :], panels[n][0]):
                        sp.dma_start(dst, src).then_inc(stream[f"w_in_slot{n % RING}"], 16)

            def panel_width(n):
                return panels[n][1] * panels[n][2] * P

            def round_panel(act, n):
                if n >= NPAN:
                    return
                act.wait_ge(stream[f"w_in_slot{n % RING}"], 16 * first_dma[n])
                if n >= RING:
                    act.wait_ge(stream["lin_out"], first_out[n - RING + 1])
                w = panel_width(n)
                act.activation(w_hi[:, n % RING, 0:w], w_raw[:, n % RING, 0:w], ACT.Copy)\
                   .then_inc(stream["hi_ready"], 1)

            def rest_panels(pool, a, z):
                for n in range(a, min(z, NPAN)):
                    pool.wait_ge(stream["hi_ready"], n + 1)
                    w = panel_width(n)
                    pool.tensor_tensor(w_lo[:, n % RING, 0:w], w_raw[:, n % RING, 0:w],
                                       w_hi[:, n % RING, 0:w].bitcast(F32), ALU.subtract)\
                        .then_inc(stream["lo_ready"], 1)

            def multiply_panel(pe, n, rh, rl, each_k=None, free=None):
                pe.wait_ge(stream["lo_ready"], n + 1)
                kn, outs = panels[n][1], panels[n][2]
                for m in range(outs):
                    o = first_out[n] + m
                    if free:
                        free(o)
                    bank = L[:, o % 2, :]
                    for k in range(kn):
                        if each_k:
                            each_k(k)
                        c0 = (k * outs + m) * P
                        wh = w_hi[:, n % RING, c0:c0 + P]
                        wl = w_lo[:, n % RING, c0:c0 + P]
                        pe.matmul(bank, wh, rh[:, k, :], start=(k == 0), stop=False)
                        pe.matmul(bank, wl, rh[:, k, :], start=False, stop=False)
                        last = pe.matmul(bank, wh, rl[:, k, :], start=False, stop=(k == kn - 1))
                    last.then_inc(stream["lin_out"], 1)

            def norm_rows_dve(dve, s, tag, sums, n=C):
                v, r, t = small[:, 1, 0:n], small[:, 2, 0:n], small[:, 3, 0:n]
                dve.tensor_scalar(v, sums, 1.0 / D, EPS, ALU.mult, ALU.add)
                dve.drain()
                rsqrt(dve, v, r, t)
                for c in range(n):
                    last = dve.tensor_scalar(diag[:, c * P:c * P + P], ident[:], r[:, c:c + 1], None, ALU.mult)
                last.then_inc(s[tag + "diag"], 1)

            def norm_rows_pe(pe, s, tag):
                pe.wait_ge(s[tag + "diag"], 1)
                pe.matmul(G[:, 4, :], ones[:], diag[:], start=True, stop=True).then_inc(s[tag + "rb"], 1)

            def norm_split_dve(dve, s, tag, row):
                dve.wait_ge(s[tag + "rb"], 1)

                def rest(i):
                    dve.wait_ge(s[tag + "xh"], i + 1)
                    dve.tensor_tensor(xl[:, i, :], ntmp[:, i % 2, :], xh[:, i, :].bitcast(F32), ALU.subtract)\
                       .then_inc(s[tag + "xl"], 1)

                for i in range(KT):
                    if i >= 2:
                        dve.wait_ge(s[tag + "xl"], i - 1)
                    dve.scalar_tensor_tensor(ntmp[:, i % 2, :], hT[:, i, :], g_of(row, i), G[:, 4, :],
                                             ALU.mult, ALU.mult).then_inc(s[tag + "nt"], 1)
                    if i >= 1:
                        rest(i - 1)
                rest(KT - 1)

            def norm_split_act(act, s, tag):
                for i in range(KT):
                    act.wait_ge(s[tag + "nt"], i + 1)
                    act.activation(xh[:, i, :], ntmp[:, i % 2, :], ACT.Copy).then_inc(s[tag + "xh"], 1)

            def residual_dve(dve, s, tag, o0, n, square):
                dve.wait_ge(stream["lin_out"], o0 + n + 1)
                dve.tensor_tensor(hT[:, n, :], L[:, (o0 + n) % 2, :], hT[:, n, :], ALU.add)\
                   .then_inc(s[tag + "h"], 1)
                if square and n >= 1:
                    sum_squares_dve(dve, s, tag, n - 1)

            def sum_squares_dve(dve, s, tag, n):
                dve.wait_ge(s[tag + "sq"], n + 1)
                if n == 0:
                    ins = dve.tensor_copy(sqsum[:], sq[:, 0, :])
                else:
                    dve.wait_ge(s[tag + "sqs"], n)
                    ins = dve.tensor_tensor(sqsum[:], sqsum[:], sq[:, n % 2, :], ALU.add)
                ins.then_inc(s[tag + "sqs"], 1)

            def square_act(act, s, tag, n, done=None):
                act.wait_ge(s[tag + "h"], (n if done is None else done) + 1)
                if n >= 2:
                    act.wait_ge(s[tag + "sqs"], n - 1)
                act.activation(sq[:, n % 2, :], hT[:, n, :], ACT.Square).then_inc(s[tag + "sq"], 1)

            def token_sums_pe(pe, s, tag):
                pe.wait_ge(s[tag + "sqs"], KT)
                for c in range(C):
                    last = pe.matmul(G[:, 5, c:c + 1], sqsum[:, c * P:c * P + P], ones[:, 0:1],
                                     start=True, stop=True)
                last.then_inc(s[tag + "tok"], 1)

            NORM = ["diag", "rb", "nt", "xh", "xl"]
            RESID = ["h", "sq", "sqs", "tok"]

            mixer = ExitStack()
            xbc = sb("xbc", [P, 8, TB], scope=mixer)
            zs = sb("zs", [P, 4, TB], scope=mixer)
            qT = sb("qT", [P, QJ, TB], scope=mixer)
            vT = sb("vT", [P, TB], scope=mixer)

            with ExitStack() as tmp:
                xin = sb("xin", [P, C, D], scope=tmp)
                raw = sb("raw", [P, 2, 3 + TB], scope=tmp)
                cacc = sb("cacc", [P, 2, TB], scope=tmp)
                junk1 = sb("junk1", [P, D], scope=tmp)
                with Phase([f"x_in{c}" for c in range(C)] + ["xt", "hev", "ssq", "lin_free", "raw_ready",
                            "conv_done", "silu_done"] + ["n1" + n for n in NORM]) as (b, s):

                    @b.sync
                    def _(sp):
                        for c in range(C):
                            sp.dma_start(xin[:, c, :], x_prompt[0, bass.ds(blk * TB + c * P, P), :])\
                              .then_inc(s[f"x_in{c}"], 16)
                        load_panels(sp, 0, PAN_OUT + RING)

                    @b.gpsimd
                    def _(pool):
                        rest_panels(pool, 0, PAN_OUT + AHEAD)

                    @b.scalar
                    def _(act):
                        for c in range(C):
                            act.wait_ge(s[f"x_in{c}"], 16)
                            act.activation(junk1[:], xin[:, c, :], ACT.Square, accum_out=small[:, 0, c:c + 1])\
                               .then_inc(s["ssq"], 1)
                            act.drain()
                        for n in range(AHEAD):
                            round_panel(act, n)
                        norm_split_act(act, s, "n1")

                        def silu(i):
                            act.wait_ge(s["conv_done"], i + 1)
                            act.activation(xbc[:, i, :], cacc[:, i % 2, :], ACT.Silu).then_inc(s["silu_done"], 1)

                        for o in range(PAN_OUT):
                            round_panel(act, o + AHEAD)
                            act.wait_ge(stream["lin_out"], o + 1)
                            src = L[:, o % 2, :]
                            if o < PAN_K:
                                if o >= 2:
                                    act.wait_ge(s["conv_done"], o - 1)
                                act.activation(raw[:, o % 2, 3:3 + TB], src, ACT.Copy).then_inc(s["lin_free"], 1)
                                if o >= 1:
                                    silu(o - 1)
                            elif o == PAN_K:
                                act.activation(kbuf[:, WIN:WIN + TB], src, ACT.Copy).then_inc(s["lin_free"], 1)
                                silu(7)
                            elif o == PAN_V:
                                act.activation(vT[:], src, ACT.Copy).then_inc(s["lin_free"], 1)
                            elif o < PAN_Z:
                                act.activation(qT[:, o - PAN_Q, :], src, ACT.Copy, scale=64 ** -0.5)\
                                   .then_inc(s["lin_free"], 1)
                            else:
                                act.activation(zs[:, o - PAN_Z, :], src, ACT.Silu).then_inc(s["lin_free"], 1)

                    @b.vector
                    def _(dve):
                        for c in range(C):
                            dve.wait_ge(s["xt"], c + 1)
                            g0 = 2 * (c % 2)
                            dve.tensor_copy(hT[:, :, c * P:c * P + P],
                                            G[:, g0:g0 + 2, :].rearrange("p a (i t) -> p (a i) t", t=P))\
                               .then_inc(s["hev"], 1)
                        dve.wait_ge(s["ssq"], C)
                        norm_rows_dve(dve, s, "n1", small[:, 0, 0:C])
                        norm_split_dve(dve, s, "n1", PV_MIX)
                        for i in range(8):
                            sl = i % 2
                            if i >= 2:
                                dve.wait_ge(s["silu_done"], i - 1)
                            dve.tensor_copy(raw[:, sl, 0:3], carry[:, i, :])
                            dve.drain()
                            dve.wait_ge(s["lin_free"], i + 1)
                            dve.tensor_scalar(cacc[:, sl, :], raw[:, sl, 0:TB], g_of(PV_CW, i), g_of(PV_CB, i),
                                              ALU.mult, ALU.add)
                            for k in range(1, 4):
                                dve.drain()
                                last = dve.scalar_tensor_tensor(cacc[:, sl, :], raw[:, sl, k:k + TB],
                                                                g_of(PV_CW + 8 * k, i), cacc[:, sl, :],
                                                                ALU.mult, ALU.add)
                                if k == 2:
                                    dve.tensor_copy(carry[:, i, :], raw[:, sl, TB:TB + 3])
                            last.then_inc(s["conv_done"], 1)

                    @b.tensor
                    def _(pe):
                        for c in range(C):
                            pe.wait_ge(s[f"x_in{c}"], 16)
                            if c >= 2:
                                pe.wait_ge(s["hev"], c - 1)
                            for i in range(KT):
                                g = 2 * (c % 2) + i // 4
                                last = pe.transpose(G[:, g, (i % 4) * P:(i % 4) * P + P],
                                                    xin[:, c, i * P:i * P + P], ident[:])
                            last.then_inc(s["xt"], 1)
                        norm_rows_pe(pe, s, "n1")
                        for n in range(PAN_OUT):
                            multiply_panel(
                                pe, n, xh, xl,
                                each_k=(lambda k: pe.wait_ge(s["n1xl"], k + 1)) if n == 0 else None,
                                free=(lambda o: pe.wait_ge(s["lin_free"], o - 1)) if n >= 2 else None)
                        for c in range(C):
                            for k in range(KT):
                                lh = xh[:, k, c * P:c * P + P]
                                ll = xl[:, k, c * P:c * P + P]
                                o = G[:, 5, c * HS:c * HS + HS]
                                pe.matmul(o, lh, wdt_h[:, k, :], start=(k == 0), stop=False)
                                pe.matmul(o, lh, wdt_l[:, k, :], start=False, stop=False)
                                pe.matmul(o, ll, wdt_h[:, k, :], start=False, stop=(k == KT - 1))

            with ExitStack() as tmp:
                ymix = sb("ymix", [P, C, D], scope=tmp)
                CHN = C * HS
                dts = sb("dts", [P, 8, CHN], scope=tmp)
                dt, da = dts[:, 0, :], dts[:, 1, :]
                ex = sb("ex", [P, 3 * CHN], scope=tmp)
                rda = sb("rda", [P, HS * P], scope=tmp)
                E = sb("E", [P, HS * P], scope=tmp)
                M = E
                cbm = sb("cbm", [P, 2 * P], scope=tmp)
                btok = sb("btok", [P, 2 * P], scope=tmp)
                xdt = sb("xdt", [P, 512], scope=tmp)
                xdd = sb("xdd", [P, 512], scope=tmp)
                yD = sb("yD", [P, 512], scope=tmp)
                yac = sb("yac", [P, 512], scope=tmp)
                ssg = sb("ssg", [P, 5, 8], scope=tmp)
                junk2 = sb("junk2", [P, 256], scope=tmp)
                SC = sb("SC", [P, 2, 4, 256], scope=tmp)
                PT = rda
                sm = sb("sm", [P, 3, 8, 4], scope=tmp)
                NU = 2 * C

                def heads(ap, w):
                    return ap.unsqueeze(2).to_broadcast([P, ap.shape[1], w])

                def bank(i):
                    return G[:, i, :] if i < 6 else L[:, i - 6, :]

                with Phase(["dtr", "dte", "dtu", "dtl", "da", "cum", "ex", "rda", "xtok", "btok", "cb", "ztok",
                            "diff", "E", "yoff", "xdd", "st", "M", "yd", "ssd_done", "ssum", "ynorm",
                            "vps", "vev", "scores", "s_free", "nmax", "prob", "pt", "ptsb", "pv", "att",
                            "mixt", "mixh", "mixl"]) as (b, s):

                    @b.scalar
                    def _(act):
                        act.wait_ge(s["vps"], 1)
                        act.activation(vtok[:, 1:1 + C, :], bank(7).rearrange("p (c t) -> p c t", t=P), ACT.Copy)\
                           .then_inc(s["vev"], 1)
                        act.wait_ge(s["dtr"], 1)
                        act.activation(dts[:, 3, :], dts[:, 2, :], ACT.Exp).then_inc(s["dte"], 1)
                        act.wait_ge(s["dtu"], 1)
                        act.activation(dts[:, 5, :], dts[:, 4, :], ACT.Ln).then_inc(s["dtl"], 1)
                        act.wait_ge(s["cum"], 1)
                        act.activation(ex[:], bank(4)[:, 0:3 * CHN], ACT.Exp).then_inc(s["ex"], 1)
                        for c in range(C):
                            act.wait_ge(s["xtok"], c + 1)
                            act.activation(btok[:], bank(1)[:, 0:256], ACT.Copy).then_inc(s["btok"], 1)
                            for g in range(2):
                                act.wait_ge(s["diff"], 2 * c + g + 1)
                                act.activation(E[:, g * 512:g * 512 + 512], bank(2 + g), ACT.Exp)\
                                   .then_inc(s["E"], 1)
                            act.wait_ge(s["ssd_done"], c + 1)
                            for g in range(2):
                                act.activation(junk2[:], ymix[:, c, g * 256:g * 256 + 256], ACT.Square,
                                               accum_out=ssg[:, 0, 2 * c + g:2 * c + g + 1]).then_inc(s["ssum"], 1)
                                act.drain()

                        def transposed(u):
                            act.wait_ge(s["pt"], u + 1)
                            if u >= 1:
                                act.wait_ge(s["pv"], u)
                            act.activation(PT[:], G[:, 2:4, :], ACT.Copy).then_inc(s["ptsb"], 1)

                        for u in range(NU):
                            act.wait_ge(s["nmax"], u + 1)
                            for a in range(4):
                                act.activation(SC[:, u % 2, a, :], SC[:, u % 2, a, :], ACT.Exp,
                                               bias=sm[:, u % 3, 2, a:a + 1],
                                               accum_out=sm[:, u % 3, 4, a:a + 1])
                            act.activation(sm[:, u % 3, 5, :], sm[:, u % 3, 3, :], ACT.Exp).then_inc(s["prob"], 1)
                            if u >= 1:
                                transposed(u - 1)
                        transposed(NU - 1)
                        for i in range(KT):
                            act.wait_ge(s["mixt"], i + 1)
                            scale = g_of(PV_SSD, i) if i < 4 else 1.0
                            act.activation(xh[:, i, :], bank(6 + i % 2), ACT.Copy, scale=scale)\
                               .then_inc(s["mixh"], 1)

                    @b.vector
                    def _(dve):
                        d, na, e, u, ln, q, r = (dts[:, i, :] for i in (1, 2, 3, 4, 5, 6, 7))
                        dve.tensor_tensor(d.rearrange("p (c h) -> p c h", h=HS),
                                          bank(5)[:, 0:CHN].rearrange("p (c h) -> p c h", h=HS),
                                          dtb[:].unsqueeze(1).to_broadcast([P, C, HS]), ALU.add)
                        dve.drain()
                        dve.scalar_tensor_tensor(na, d, -1.0, d, ALU.mult, ALU.min).then_inc(s["dtr"], 1)
                        dve.wait_ge(s["dte"], 1)
                        dve.tensor_scalar(u, e, 1.0, None, ALU.add).then_inc(s["dtu"], 1)
                        dve.wait_ge(s["dtu"], 1)
                        dve.tensor_scalar(q, u, -1.0, None, ALU.add)
                        dve.drain()
                        dve.tensor_scalar(r, q, 1e-30, None, ALU.max)
                        dve.drain()
                        dve.reciprocal(r, r)
                        dve.tensor_scalar(q, q, 0.0, None, ALU.is_equal)
                        dve.wait_ge(s["dtl"], 1)
                        dve.drain()
                        dve.tensor_tensor(r, r, ln, ALU.mult)
                        dve.drain()
                        dve.tensor_tensor(r, r, q, ALU.add)
                        dve.drain()
                        dve.tensor_tensor(r, r, e, ALU.mult)
                        dve.drain()
                        dve.scalar_tensor_tensor(dt, d, 0.0, r, ALU.max, ALU.add)
                        dve.drain()
                        dve.tensor_tensor(da.rearrange("p (c h) -> p c h", h=HS),
                                          dt.rearrange("p (c h) -> p c h", h=HS),
                                          nega[:].unsqueeze(1).to_broadcast([P, C, HS]), ALU.mult)\
                           .then_inc(s["da"], 1)
                        dve.wait_ge(s["da"], 1)
                        v3 = lambda t: t.rearrange("p (h w) -> p h w", h=HS)
                        for c in range(C):
                            hc = slice(c * HS, c * HS + HS)
                            if c >= 1:
                                dve.wait_ge(s["diff"], 2 * c)
                            dve.tensor_tensor(v3(rda[:]), tri_le[:].unsqueeze(1).to_broadcast([P, HS, P]),
                                              heads(da[:, hc], P), ALU.mult).then_inc(s["rda"], 1)
                            dve.wait_ge(s["xtok"], c + 1)
                            if c == 0:
                                dve.wait_ge(s["ex"], 1)
                            dve.tensor_tensor(v3(xdt[:]), v3(bank(0)), heads(dt[:, hc], HP), ALU.mult)
                            if c >= 1:
                                dve.wait_ge(s["ssd_done"], c)
                            dve.tensor_tensor(v3(yD[:]), v3(bank(0)), heads(dsk[:], HP), ALU.mult)
                            dve.drain()
                            dve.tensor_tensor(v3(xdd[:]), v3(xdt[:]),
                                              heads(ex[:, CHN + c * HS:CHN + c * HS + HS], HP), ALU.mult)\
                               .then_inc(s["xdd"], 1)
                            dve.wait_ge(s["cb"], c + 1)
                            dve.tensor_tensor(cbm[:].rearrange("p (g q) -> p g q", g=2),
                                              bank(1)[:, 256:512].rearrange("p (g q) -> p g q", g=2),
                                              tri_le[:].unsqueeze(1).to_broadcast([P, 2, P]), ALU.mult)
                            dve.drain()
                            for g in range(2):
                                dve.wait_ge(s["E"], 2 * c + g + 1)
                                last = dve.tensor_tensor(
                                    M[:, g * 512:g * 512 + 512].rearrange("p (h q) -> p h q", h=4),
                                    E[:, g * 512:g * 512 + 512].rearrange("p (h q) -> p h q", h=4),
                                    cbm[:, g * P:g * P + P].unsqueeze(1).to_broadcast([P, 4, P]), ALU.mult)
                            last.then_inc(s["M"], 1)
                            dve.wait_ge(s["yoff"], c + 1)
                            dve.tensor_tensor(v3(yac[:]), v3(bank(5)), heads(ex[:, hc], HP), ALU.mult)
                            dve.drain()
                            dve.tensor_tensor(yac[:], yac[:], yD[:], ALU.add)
                            dve.wait_ge(s["st"], c + 1)
                            dve.tensor_tensor(v3(state[:]), v3(state[:]),
                                              heads(ex[:, 2 * CHN + c * HS:2 * CHN + c * HS + HS], HP), ALU.mult)
                            dve.drain()
                            dve.tensor_tensor(state[:], state[:], bank(6), ALU.add)
                            dve.wait_ge(s["yd"], c + 1)
                            dve.tensor_tensor(yac[:], yac[:], bank(4), ALU.add)
                            dve.drain()
                            dve.wait_ge(s["ztok"], c + 1)
                            dve.tensor_tensor(ymix[:, c, 0:512], yac[:], bank(7), ALU.mult)\
                               .then_inc(s["ssd_done"], 1)
                        dve.wait_ge(s["ssum"], 2 * C)
                        dve.tensor_scalar(ssg[:, 1, :], ssg[:, 0, :], 1.0 / 256, EPS, ALU.mult, ALU.add)
                        dve.drain()
                        rsqrt(dve, ssg[:, 1, :], ssg[:, 2, :], ssg[:, 3, :])
                        for c in range(C):
                            yv = ymix[:, c, 0:512].rearrange("p (g w) -> p g w", g=2)
                            last = dve.tensor_tensor(yv, yv, heads(ssg[:, 2, 2 * c:2 * c + 2], 256), ALU.mult)
                        last.then_inc(s["ynorm"], 1)

                        def finish(u):
                            c, jp = u // 2, u % 2
                            st = sm[:, u % 3]
                            dve.wait_ge(s["prob"], u + 1)
                            dve.tensor_tensor(st[:, 6, :], st[:, 4, :], st[:, 5, :], ALU.add)
                            dve.drain()
                            dve.reciprocal(st[:, 7, :], st[:, 6, :])
                            dve.drain()
                            dve.wait_ge(s["pv"], u + 1)
                            o = ymix[:, c, 512 + jp * 256:512 + jp * 256 + 256]
                            dve.tensor_tensor(o.rearrange("p (j v d) -> p j v d", j=2, v=KV),
                                              bank(4)[:, 0:256].rearrange("p (j v d) -> p j v d", j=2, v=KV),
                                              st[:, 7, :].rearrange("p (v j) -> p j v", v=KV).unsqueeze(3)
                                              .to_broadcast([P, 2, KV, 64]), ALU.mult).then_inc(s["att"], 1)

                        for u in range(NU):
                            c, jp = u // 2, u % 2
                            st = sm[:, u % 3]
                            sc = SC[:, u % 2].rearrange("p (v j) k -> p v j k", v=KV)
                            ps = G[:, 0:2, :].rearrange("p v (j k) -> p v j k", j=2)
                            hj = slice(2 * jp, 2 * jp + 2)
                            dve.wait_ge(s["scores"], u + 1)
                            if u >= 2:
                                dve.wait_ge(s["pt"], u - 1)
                            for half, bias in ((0, bias_first if c == 0 else bias_prev), (1, bias_cur)):
                                ks = slice(half * WIN, half * WIN + WIN)
                                bv = bias[:].rearrange("p (v j) k -> p v j k", v=KV)
                                for v in range(KV):
                                    last = dve.tensor_tensor(sc[:, v, :, ks], ps[:, v, :, ks], bv[:, v, hj, :],
                                                             ALU.add)
                            last.then_inc(s["s_free"], 1)
                            dve.wait_ge(s["s_free"], u + 1)
                            dve.tensor_reduce(st[:, 0, :], SC[:, u % 2], AX_X, ALU.max)
                            dve.drain()
                            snk_u = snk[:].rearrange("p (v j) -> p v j", v=KV)[:, :, hj]
                            vj = lambda t: t.rearrange("p (v j) -> p v j", v=KV)
                            dve.tensor_tensor(vj(st[:, 1, :]), vj(st[:, 0, :]), snk_u, ALU.max)
                            dve.drain()
                            dve.tensor_scalar(st[:, 2, :], st[:, 1, :], -1.0, None, ALU.mult)
                            dve.tensor_tensor(vj(st[:, 3, :]), snk_u, vj(st[:, 1, :]), ALU.subtract)\
                               .then_inc(s["nmax"], 1)
                            if u >= 2:
                                finish(u - 2)
                        finish(NU - 2)
                        finish(NU - 1)
                        dve.tensor_copy(kbuf[:, 0:WIN], kbuf[:, TB:TB + WIN])
                        dve.tensor_copy(vtok[:, 0, :], vtok[:, C, :])
                        dve.tensor_copy(bias_first[:], bias_prev[:])
                        for i in range(KT):
                            dve.wait_ge(s["mixh"], i + 1)
                            src, hi = bank(6 + i % 2), xh[:, i, :].bitcast(F32)
                            if i < 4:
                                ins = dve.scalar_tensor_tensor(xl[:, i, :], src, g_of(PV_SSD, i), hi,
                                                               ALU.mult, ALU.subtract)
                            else:
                                ins = dve.tensor_tensor(xl[:, i, :], src, hi, ALU.subtract)
                            ins.then_inc(s["mixl"], 1)

                    @b.tensor
                    def _(pe):
                        for c in range(C):
                            last = pe.transpose(bank(7)[:, c * P:c * P + P], vT[:, c * P:c * P + P], ident[:])
                        last.then_inc(s["vps"], 1)
                        pe.wait_ge(s["da"], 1)
                        for i, left in enumerate((tri_le, tri_gt, ones)):
                            last = pe.matmul(bank(4)[:, i * CHN:(i + 1) * CHN], left[:], da, start=True, stop=True)
                        last.then_inc(s["cum"], 1)
                        pe.wait_ge(s["vev"], 1)
                        for c in range(C):
                            t = slice(c * P, c * P + P)
                            if c >= 1:
                                pe.wait_ge(s["ssd_done"], c)
                                pe.wait_ge(s["btok"], c)
                            for i in range(4):
                                pe.transpose(bank(0)[:, i * P:i * P + P], xbc[:, i, t], ident[:])
                            for g in range(2):
                                last = pe.transpose(bank(1)[:, g * P:g * P + P], xbc[:, 4 + g, t], ident[:])
                            last.then_inc(s["xtok"], 1)
                            pe.wait_ge(s["rda"], c + 1)
                            for g in range(2):
                                pe.matmul(bank(2 + g), tri_gt[:], rda[:, g * 512:g * 512 + 512],
                                          start=True, stop=True).then_inc(s["diff"], 1)
                            for g in range(2):
                                last = pe.matmul(bank(5)[:, g * 256:g * 256 + 256], xbc[:, 6 + g, t],
                                                 state[:, g * 256:g * 256 + 256], start=True, stop=True)
                            last.then_inc(s["yoff"], 1)
                            pe.wait_ge(s["btok"], c + 1)
                            for g in range(2):
                                last = pe.matmul(bank(1)[:, 256 + g * P:256 + g * P + P], xbc[:, 4 + g, t],
                                                 xbc[:, 6 + g, t], start=True, stop=True)
                            last.then_inc(s["cb"], 1)
                            pe.wait_ge(s["xdd"], c + 1)
                            for g in range(2):
                                last = pe.matmul(bank(6)[:, g * 256:g * 256 + 256], btok[:, g * P:g * P + P],
                                                 xdd[:, g * 256:g * 256 + 256], start=True, stop=True)
                            last.then_inc(s["st"], 1)
                            for i in range(4):
                                last = pe.transpose(bank(7)[:, i * P:i * P + P], zs[:, i, t], ident[:])
                            last.then_inc(s["ztok"], 1)
                            if c == 0:
                                pe.wait_ge(s["ex"], 1)
                            pe.wait_ge(s["M"], c + 1)
                            for h in range(HS):
                                last = pe.matmul(bank(4)[:, h * HP:h * HP + HP], M[:, h * P:h * P + P],
                                                 xdt[:, h * HP:h * HP + HP], start=True, stop=True)
                            last.then_inc(s["yd"], 1)

                        def scores(u):
                            c, jp = u // 2, u % 2
                            if u >= 1:
                                pe.wait_ge(s["s_free"], u)
                            for v in range(KV):
                                for jj in range(2):
                                    r = slice(64 * v, 64 * v + 64)
                                    last = pe.matmul(G[:, v, jj * 256:jj * 256 + 256],
                                                     qT[r, 2 * jp + jj, c * P:c * P + P],
                                                     kbuf[r, c * P:c * P + 256], start=True, stop=True)
                            last.then_inc(s["scores"], 1)

                        def weigh(u):
                            c = u // 2
                            pe.wait_ge(s["prob"], u + 1)
                            if u >= 1:
                                pe.wait_ge(s["ptsb"], u)
                            for a in range(4):
                                for half in range(2):
                                    i = 2 * a + half
                                    last = pe.transpose(G[:, 2 + i // 4, (i % 4) * P:(i % 4) * P + P],
                                                        SC[:, u % 2, a, half * P:half * P + P], ident[:])
                            last.then_inc(s["pt"], 1)

                        def values(u):
                            c = u // 2
                            pe.wait_ge(s["ptsb"], u + 1)
                            if u >= 1:
                                pe.wait_ge(s["att"], u)
                            for a in range(4):
                                v, jj = a // 2, a % 2
                                for half in range(2):
                                    i = 2 * a + half
                                    last = pe.matmul(bank(4)[:, jj * P + v * 64:jj * P + v * 64 + 64],
                                                     PT[:, i * P:i * P + P], vtok[:, c + half, v * 64:v * 64 + 64],
                                                     start=(half == 0), stop=(half == 1))
                            last.then_inc(s["pv"], 1)

                        pe.wait_ge(s["ssd_done"], C)
                        scores(0)
                        for u in range(NU):
                            if u + 1 < NU:
                                scores(u + 1)
                            weigh(u)
                            if u >= 1:
                                values(u - 1)
                        values(NU - 1)
                        pe.wait_ge(s["ynorm"], 1)
                        pe.wait_ge(s["att"], NU)
                        for i in range(KT):
                            if i >= 2:
                                pe.wait_ge(s["mixl"], i - 1)
                            for c in range(C):
                                last = pe.transpose(bank(6 + i % 2)[:, c * P:c * P + P],
                                                    ymix[:, c, i * P:i * P + P], ident[:])
                            last.then_inc(s["mixt"], 1)
            mixer.close()

            with ExitStack() as tmp:
                cq = sb("cq", [P, CH, TB], scope=tmp)
                PC = sb("PC", [P, 2, CH, NMEM], scope=tmp)
                PTc = sb("PTc", [P, 2 * CH, TB], scope=tmp)
                cs_ = sb("cs_", [P, 2, 3, CH], scope=tmp)
                O_OUT, O_CQ, O_CO = first_out[PAN_OUT], first_out[PAN_CQ], first_out[PAN_CO]
                with Phase(["r1" + n for n in RESID] + ["n2" + n for n in NORM] + ["r2" + n for n in RESID]
                           + ["n3" + n for n in NORM]
                           + ["cqev", "scores", "cmax", "cexp", "cprob", "pt", "ptsb", "ov", "oh", "ol"]) as (b, s):

                    @b.sync
                    def _(sp):
                        load_panels(sp, PAN_OUT + RING, PAN_FFN + RING)

                    @b.gpsimd
                    def _(pool):
                        rest_panels(pool, PAN_OUT + AHEAD, PAN_FFN + AHEAD)

                    @b.scalar
                    def _(act):
                        for n in range(KT):
                            round_panel(act, PAN_OUT + n + AHEAD)
                            if n >= 1:
                                square_act(act, s, "r1", n - 1)
                        square_act(act, s, "r1", KT - 1)
                        norm_split_act(act, s, "n2")
                        for n in range(CH):
                            round_panel(act, PAN_CQ + n + AHEAD)

                        def transposed(c):
                            act.wait_ge(s["pt"], c + 1)
                            act.activation(PTc[:, :, c * P:c * P + P],
                                           G[:, 2:4, :].rearrange("p a (i t) -> p (a i) t", t=P), ACT.Copy)\
                               .then_inc(s["ptsb"], 1)

                        for c in range(C):
                            act.wait_ge(s["cmax"], c + 1)
                            for h in range(CH):
                                act.activation(PC[:, c % 2, h, :],
                                                      G[:, h // 2, (h % 2) * 256:(h % 2) * 256 + 256], ACT.Exp,
                                                      bias=cs_[:, c % 2, 0, h:h + 1],
                                                      accum_out=cs_[:, c % 2, 1, h:h + 1]).then_inc(s["cexp"], 1)
                            if c >= 1:
                                transposed(c - 1)
                        transposed(C - 1)
                        for h in range(CH):
                            act.wait_ge(s["ov"], h + 1)
                            act.activation(xh[:, h, :], G[:, 4 + h % 2, :], ACT.Copy).then_inc(s["oh"], 1)
                        for n in range(KT):
                            if n % 2 == 0:
                                round_panel(act, PAN_CO + n // 2 + AHEAD)
                            if n >= 1:
                                square_act(act, s, "r2", n - 1)
                        square_act(act, s, "r2", KT - 1)
                        norm_split_act(act, s, "n3")

                    @b.vector
                    def _(dve):
                        for n in range(KT):
                            residual_dve(dve, s, "r1", O_OUT, n, True)
                        sum_squares_dve(dve, s, "r1", KT - 1)
                        dve.wait_ge(s["r1tok"], 1)
                        norm_rows_dve(dve, s, "n2", G[:, 5, 0:C])
                        norm_split_dve(dve, s, "n2", PV_CROSS)
                        for n in range(CH):
                            dve.wait_ge(stream["lin_out"], O_CQ + n + 1)
                            dve.tensor_scalar(cq[:, n, :], L[:, (O_CQ + n) % 2, :], P ** -0.5, None, ALU.mult)\
                               .then_inc(s["cqev"], 1)

                        def normalise(c):
                            dve.wait_ge(s["cexp"], CH * (c + 1))
                            dve.reciprocal(cs_[:, c % 2, 2, :], cs_[:, c % 2, 1, :])
                            dve.drain()
                            for h in range(CH):
                                last = dve.tensor_scalar(PC[:, c % 2, h, :], PC[:, c % 2, h, :],
                                                         cs_[:, c % 2, 2, h:h + 1], None, ALU.mult)
                            last.then_inc(s["cprob"], 1)

                        for c in range(C):
                            dve.wait_ge(s["scores"], c + 1)
                            dve.tensor_reduce(cs_[:, c % 2, 0, :],
                                              G[:, 0:2, :].rearrange("p a (h m) -> p (a h) m", h=2), AX_X, ALU.max,
                                              negate=True).then_inc(s["cmax"], 1)
                            normalise(c)
                        for h in range(CH):
                            dve.wait_ge(s["oh"], h + 1)
                            dve.tensor_tensor(xl[:, h, :], G[:, 4 + h % 2, :], xh[:, h, :].bitcast(F32),
                                              ALU.subtract).then_inc(s["ol"], 1)
                        for n in range(KT):
                            residual_dve(dve, s, "r2", O_CO, n, True)
                        sum_squares_dve(dve, s, "r2", KT - 1)
                        dve.wait_ge(s["r2tok"], 1)
                        norm_rows_dve(dve, s, "n3", G[:, 5, 0:C])
                        norm_split_dve(dve, s, "n3", PV_FFN)

                    @b.tensor
                    def _(pe):
                        for n in range(KT):
                            multiply_panel(pe, PAN_OUT + n, xh, xl,
                                           free=(lambda o: pe.wait_ge(s["r1h"], o - O_OUT - 1)) if n >= 2 else None)
                        token_sums_pe(pe, s, "r1")
                        norm_rows_pe(pe, s, "n2")
                        for n in range(CH):
                            multiply_panel(pe, PAN_CQ + n, xh, xl,
                                           each_k=(lambda k: pe.wait_ge(s["n2xl"], k + 1)) if n == 0 else None,
                                           free=(lambda o: pe.wait_ge(s["cqev"], o - O_CQ - 1)) if n >= 2 else None)
                        pe.wait_ge(s["cqev"], CH)

                        def scores(c):
                            if c >= 1:
                                pe.wait_ge(s["cexp"], CH * c)
                            for h in range(CH):
                                last = pe.matmul(G[:, h // 2, (h % 2) * 256:(h % 2) * 256 + 256],
                                                 cq[:, h, c * P:c * P + P], kmT[:, h, :], start=True, stop=True)
                            last.then_inc(s["scores"], 1)

                        scores(0)
                        for c in range(C):
                            if c + 1 < C:
                                scores(c + 1)
                            pe.wait_ge(s["cprob"], c + 1)
                            if c >= 1:
                                pe.wait_ge(s["ptsb"], c)
                            for i in range(2 * CH):
                                last = pe.transpose(G[:, 2 + i // 4, (i % 4) * P:(i % 4) * P + P],
                                                    PC[:, c % 2, i // 2, (i % 2) * P:(i % 2) * P + P], ident[:])
                            last.then_inc(s["pt"], 1)
                        pe.wait_ge(s["ptsb"], C)
                        for h in range(CH):
                            if h >= 2:
                                pe.wait_ge(s["ol"], h - 1)
                            for m in range(2):
                                last = pe.matmul(G[:, 4 + h % 2, :], vm[:, m, h * P:h * P + P],
                                                 PTc[:, 2 * h + m, :], start=(m == 0), stop=(m == 1))
                            last.then_inc(s["ov"], 1)
                        pe.wait_ge(s["ol"], CH)
                        for n in range(4):
                            multiply_panel(pe, PAN_CO + n, xh, xl,
                                           free=(lambda o: pe.wait_ge(s["r2h"], o - O_CO - 1)) if n >= 1 else None)
                        token_sums_pe(pe, s, "r2")
                        norm_rows_pe(pe, s, "n3")

            with ExitStack() as tmp:
                hid_h = sb("hid_h", [P, 8, TB], F32R, scope=tmp)
                hid_l = sb("hid_l", [P, 8, TB], F32R, scope=tmp)
                sg = sb("sg", [P, 2, TB], scope=tmp)
                gu = sb("gu", [P, 2, TB], scope=tmp)
                yout = sb("yout", [P, C, D], scope=tmp)
                steps = []
                for g, (f0, f1) in enumerate(FGROUPS):
                    for f in range(f0, f1):
                        steps += [("gate", f, g), ("up", f, g)]
                    steps += [("down", n, g) for n in range(KT)]
                O_FFN = first_out[PAN_FFN]
                assert O_FFN % 2 == 0 and len(steps) == NPAN - PAN_FFN
                LASTG = len(FGROUPS) - 1
                with Phase(["gate", "up", "hh", "hl"] + ["rf" + n for n in RESID] + ["nf" + n for n in NORM]
                           + ["yt", "yev", "out_done"]) as (b, s):

                    @b.sync
                    def _(sp):
                        load_panels(sp, PAN_FFN + RING, NPAN)
                        sp.wait_ge(s["yev"], KT)
                        sp.dma_start(y_prompt[0, bass.ds(blk * TB, TB), :].rearrange("(c p) d -> p c d", p=P),
                                     yout[:]).then_inc(s["out_done"], 16)
                        sp.wait_ge(s["out_done"], 16)

                    @b.gpsimd
                    def _(pool):
                        rest_panels(pool, PAN_FFN + AHEAD, NPAN)

                    @b.scalar
                    def _(act):
                        def round_hidden(f):
                            act.wait_ge(s["up"], f + 1)
                            act.activation(hid_h[:, f % 8, :], gu[:, f % 2, :], ACT.Copy).then_inc(s["hh"], 1)

                        for o, (kind, i, g) in enumerate(steps):
                            round_panel(act, PAN_FFN + o + AHEAD)
                            if kind == "gate":
                                act.wait_ge(stream["lin_out"], O_FFN + o + 1)
                                if i >= 2:
                                    act.wait_ge(s["up"], i - 1)
                                act.activation(sg[:, i % 2, :], L[:, o % 2, :], ACT.Silu).then_inc(s["gate"], 1)
                                if i > FGROUPS[g][0]:
                                    round_hidden(i - 1)
                            elif kind == "down":
                                if i == 0:
                                    round_hidden(FGROUPS[g][1] - 1)
                                if g == LASTG and i >= 1:
                                    square_act(act, s, "rf", i - 1, done=g * KT + i - 1)
                        square_act(act, s, "rf", KT - 1, done=LASTG * KT + KT - 1)
                        for i in range(KT):
                            act.wait_ge(s["yt"], i + 1)
                            act.activation(yout[:, :, i * P:i * P + P],
                                           G[:, i % 2, :].rearrange("p (c t) -> p c t", t=P), ACT.Copy)\
                               .then_inc(s["yev"], 1)

                    @b.vector
                    def _(dve):
                        def rest_hidden(f):
                            dve.wait_ge(s["hh"], f + 1)
                            dve.tensor_tensor(hid_l[:, f % 8, :], gu[:, f % 2, :], hid_h[:, f % 8, :].bitcast(F32),
                                              ALU.subtract).then_inc(s["hl"], 1)

                        for o, (kind, i, g) in enumerate(steps):
                            if kind == "up":
                                dve.wait_ge(s["gate"], i + 1)
                                dve.wait_ge(stream["lin_out"], O_FFN + o + 1)
                                if i >= 2:
                                    dve.wait_ge(s["hl"], i - 1)
                                dve.tensor_tensor(gu[:, i % 2, :], sg[:, i % 2, :], L[:, o % 2, :], ALU.mult)\
                                   .then_inc(s["up"], 1)
                                if i > FGROUPS[g][0]:
                                    rest_hidden(i - 1)
                            elif kind == "down":
                                if i == 0:
                                    rest_hidden(FGROUPS[g][1] - 1)
                                dve.wait_ge(stream["lin_out"], O_FFN + o + 1)
                                if g >= 1:
                                    dve.wait_ge(s["rfh"], (g - 1) * KT + i + 1)
                                dve.tensor_tensor(hT[:, i, :], L[:, o % 2, :], hT[:, i, :], ALU.add)\
                                   .then_inc(s["rfh"], 1)
                                if g == LASTG and i >= 1:
                                    sum_squares_dve(dve, s, "rf", i - 1)
                        sum_squares_dve(dve, s, "rf", KT - 1)
                        dve.wait_ge(s["rftok"], 1)
                        norm_rows_dve(dve, s, "nf", G[:, 5, 0:C])
                        dve.wait_ge(s["nfrb"], 1)
                        for i in range(KT):
                            if i >= 2:
                                dve.wait_ge(s["yt"], i - 1)
                            dve.scalar_tensor_tensor(ntmp[:, i % 2, :], hT[:, i, :], g_of(PV_FINAL, i), G[:, 4, :],
                                                     ALU.mult, ALU.mult).then_inc(s["nfnt"], 1)

                    @b.tensor
                    def _(pe):
                        done_h = 0
                        for o, (kind, i, g) in enumerate(steps):
                            f0, f1 = FGROUPS[g]

                            def free(_, o=o):
                                if o < 2:
                                    return
                                kind2, i2, g2 = steps[o - 2]
                                if kind2 == "down":
                                    pe.wait_ge(s["rfh"], g2 * KT + i2 + 1)
                                else:
                                    pe.wait_ge(s[kind2], i2 + 1)

                            if kind == "down":
                                each = (lambda k, f0=f0: pe.wait_ge(s["hl"], f0 + k + 1)) if i == 0 else None
                                multiply_panel(pe, PAN_FFN + o, hid_h, hid_l, each_k=each, free=free)
                            else:
                                multiply_panel(pe, PAN_FFN + o, xh, xl, free=free)
                        token_sums_pe(pe, s, "rf")
                        norm_rows_pe(pe, s, "nf")
                        for i in range(KT):
                            pe.wait_ge(s["nfnt"], i + 1)
                            if i >= 2:
                                pe.wait_ge(s["yev"], i - 1)
                            for c in range(C):
                                last = pe.transpose(G[:, i % 2, c * P:c * P + P],
                                                    ntmp[:, i % 2, c * P:c * P + P], ident[:])
                            last.then_inc(s["yt"], 1)

            clear(stream.values())

        with ExitStack() as tmp:
            ktail = sb("ktail", [P, P], scope=tmp)
            ctail = sb("ctail", [3, D], scope=tmp)
            stail = sb("stail", [P, 4, P], scope=tmp)
            with Phase(["kt", "ct", "stt", "ktsb", "ctsb", "stsb", "out_done"]) as (b, s):

                @b.tensor
                def _(pe):
                    pe.transpose(G[:, 0, 0:P], kbuf[:, 0:P], ident[:]).then_inc(s["kt"], 1)
                    for i in range(KT):
                        last = pe.transpose(G[0:3, 1 + i // 4, (i % 4) * P:(i % 4) * P + P], carry[:, i, :], ident[:])
                    last.then_inc(s["ct"], 1)
                    for i in range(4):
                        last = pe.transpose(G[:, 3, i * P:i * P + P], state[:, i * P:i * P + P], ident[:])
                    last.then_inc(s["stt"], 1)

                @b.vector
                def _(dve):
                    dve.wait_ge(s["kt"], 1)
                    dve.tensor_copy(ktail[:], G[:, 0, 0:P]).then_inc(s["ktsb"], 1)
                    dve.wait_ge(s["ct"], 1)
                    dve.tensor_copy(ctail[:], G[0:3, 1:3, :].rearrange("p a n -> p (a n)")).then_inc(s["ctsb"], 1)
                    dve.wait_ge(s["stt"], 1)
                    dve.tensor_copy(stail[:], G[:, 3, :].rearrange("p (i n) -> p i n", n=P)).then_inc(s["stsb"], 1)

                @b.sync
                def _(sp):
                    sp.dma_start(p_swa_v[0, 0].rearrange("t v d -> t (v d)"), vtok[:, 0, :]).then_inc(s["out_done"], 16)
                    for src, dst in ((cache_swa_k, s_swa_k), (cache_swa_v, s_swa_v)):
                        sp.dma_start(dst[0, :, 0:WIN - TS].rearrange("b t v d -> b (t v d)"),
                                     src[0, :, TS:WIN].rearrange("b t v d -> b (t v d)")).then_inc(s["out_done"], 16)
                    sp.wait_ge(s["ktsb"], 1)
                    sp.dma_start(p_swa_k[0, 0].rearrange("t v d -> t (v d)"), ktail[:]).then_inc(s["out_done"], 16)
                    sp.wait_ge(s["ctsb"], 1)
                    sp.dma_start(p_conv[0, 0], ctail[:]).then_inc(s["out_done"], 16)
                    sp.wait_ge(s["stsb"], 1)
                    sp.dma_start(p_ssm[0, 0].rearrange("(i h) p n -> (h p) i n", h=2), stail[:])\
                      .then_inc(s["out_done"], 16)
                    sp.wait_ge(s["out_done"], 96)
        prompt.close()

        SR = 8
        sslot = {}
        on_slot = [0] * SR
        for n, (parts, _, _) in enumerate(panels):
            on_slot[n % SR] += sum(KV if part[0] == "kv" else 1 for part in parts)
            sslot[n] = on_slot[n % SR]
        group = whole.enter_context(ExitStack())
        hS = sb("hS", [P, KT, S], scope=group)
        xS = sb("xS", [P, KT, S], scope=group)
        wS = sb("wS", [P, SR, D], scope=group)
        sqS = sb("sqS", [P, KT, S], scope=group)
        sqsS = sb("sqsS", [P, S], scope=group)
        memK = sb("memK", [P, NB, 2, CH * P], scope=group)
        memV = sb("memV", [P, NB, 2, CH * P], scope=group)
        sstream = {n: group.enter_context(nc.semaphore("s_" + n))
                   for n in [f"w_in_slot{r}" for r in range(SR)] + ["lin_out", "mem_in"]}

        def s_load(sp, a, z):
            for n in range(a, min(z, NPAN)):
                if n >= SR:
                    sp.wait_ge(sstream["lin_out"], first_out[n - SR + 1])
                for dst, src in panel_slices(wS[:, n % SR, :], panels[n][0]):
                    sp.dma_start(dst, src).then_inc(sstream[f"w_in_slot{n % SR}"], 16)

        def s_multiply(pe, n, x, free):
            pe.wait_ge(sstream[f"w_in_slot{n % SR}"], 16 * sslot[n])
            kn, outs = panels[n][1], panels[n][2]
            for m in range(outs):
                o = first_out[n] + m
                free(o)
                for k in range(kn):
                    c0 = (k * outs + m) * P
                    last = pe.matmul(L[:, o % 2, 0:S], wS[:, n % SR, c0:c0 + P], x[:, k, :],
                                     start=(k == 0), stop=(k == kn - 1))
                last.then_inc(sstream["lin_out"], 1)

        SNORM = ["sq", "sqs", "tok", "diag", "rb", "x"]

        def s_norm_act(act, s, tag):
            act.activation(sqS[:], hS[:], ACT.Square).then_inc(s[tag + "sq"], 1)

        def s_norm_dve(dve, s, tag, row, out):
            v, r, t = small[0:S, 4, 0:1], small[0:S, 5, 0:1], small[0:S, 6, 0:1]
            dve.wait_ge(s[tag + "sq"], 1)
            dve.tensor_reduce(sqsS[:], sqS[:].rearrange("p k t -> p t k"), AX_X, ALU.add).then_inc(s[tag + "sqs"], 1)
            dve.wait_ge(s[tag + "tok"], 1)
            dve.tensor_scalar(v, G[0:S, 5, 0:1], 1.0 / D, EPS, ALU.mult, ALU.add)
            dve.drain()
            rsqrt(dve, v, r, t)
            dve.tensor_scalar(diag[0:S, 0:S], ident[0:S, 0:S], r, None, ALU.mult).then_inc(s[tag + "diag"], 1)
            dve.wait_ge(s[tag + "rb"], 1)
            dve.tensor_tensor(out[:], hS[:], G[:, 4, 0:S].unsqueeze(1).to_broadcast([P, KT, S]), ALU.mult)
            dve.drain()
            dve.tensor_tensor(out[:], out[:], pv[:, row:row + KT].unsqueeze(2).to_broadcast([P, KT, S]), ALU.mult)\
               .then_inc(s[tag + "x"], 1)

        def s_norm_pe(pe, s, tag):
            pe.wait_ge(s[tag + "sqs"], 1)
            pe.matmul(G[0:S, 5, 0:1], sqsS[:], ones[:, 0:1], start=True, stop=True).then_inc(s[tag + "tok"], 1)
            pe.wait_ge(s[tag + "diag"], 1)
            pe.matmul(G[:, 4, 0:S], ones[0:S, :], diag[0:S, 0:S], start=True, stop=True).then_inc(s[tag + "rb"], 1)

        def s_residual(dve, s, name, o0, n):
            dve.wait_ge(sstream["lin_out"], o0 + n + 1)
            dve.tensor_tensor(hS[:, n, :], L[:, (o0 + n) % 2, 0:S], hS[:, n, :], ALU.add).then_inc(s[name], 1)

        mixer = ExitStack()
        xbcS = sb("xbcS", [P, 8, S], scope=mixer)
        zsS = sb("zsS", [P, 4, S], scope=mixer)
        qS = sb("qS", [P, QJ, S], scope=mixer)
        kS = sb("kS", [P, S], scope=mixer)
        vS = sb("vS", [P, S], scope=mixer)
        dtS = sb("dtS", [S, 10, HS], scope=mixer)
        swK = sb("swK", [P, NB, P], scope=mixer)
        swV = sb("swV", [P, NB, P], scope=mixer)
        stN = sb("stN", [P, NB, 4, P], scope=mixer)
        biasC = sb("biasC", [P, WIN], scope=mixer)
        biasN = sb("biasN", [P, 4, S], scope=mixer)
        snkS = sb("snkS", [P, 1], scope=mixer)
        same = sb("same", [S, NB, TS], scope=mixer)
        leS = sb("leS", [S, S], scope=mixer)
        gtS = sb("gtS", [S, S], scope=mixer)
        in_sems = {n: mixer.enter_context(nc.semaphore("s_" + n)) for n in ("rows_in", "new_in", "swa_in", "ssm_in")}

        with ExitStack() as tmp:
            xin = sb("xinS", [S, D], scope=tmp)
            rawS = sb("rawS", [P, 8, NB, 3 + TS], scope=tmp)
            convS = sb("convS", [P, 8, S], scope=tmp)
            scrow = sb("scrow", [3 * NB, D], scope=tmp)
            lastS = sb("lastS", [P, 8, NB * 3], scope=tmp)
            lrow = sb("lrow", [3 * NB, D], scope=tmp)
            with Phase(["x_in", "sc_in", "xt", "hev", "sct", "scev", "lin_free", "conv", "last", "lt", "ltsb",
                        "dtp", "made", "same", "kill", "out_done"] + ["n1" + n for n in SNORM]) as (b, s):

                @b.sync
                def _(sp):
                    sp.dma_start(xin[:], x_sample.rearrange("b t d -> (b t) d")).then_inc(s["x_in"], 16)
                    sp.dma_start(scrow[:], state_conv[0].rearrange("b k d -> (b k) d")).then_inc(s["sc_in"], 16)
                    s_load(sp, 0, SR)
                    sp.dma_start(swK[:], cache_swa_k[0].rearrange("b t v d -> t b (v d)")).then_inc(in_sems["swa_in"], 16)
                    sp.dma_start(swV[:], cache_swa_v[0].rearrange("b t v d -> t b (v d)")).then_inc(in_sems["swa_in"], 16)
                    for bb in range(NB):
                        sp.dma_start(stN[:, bb], state_ssm[0, bb].rearrange("(i h) p n -> (h p) i n", h=2))\
                          .then_inc(in_sems["ssm_in"], 16)
                    s_load(sp, SR, PAN_OUT + SR)
                    for bb in range(NB):
                        sp.dma_start(memK[:, bb], cache_mem_k[0, bb].rearrange("(c p) h d -> p c (h d)", p=P))\
                          .then_inc(sstream["mem_in"], 16)
                        sp.dma_start(memV[:, bb], cache_mem_v[0, bb].rearrange("(c p) h d -> p c (h d)", p=P))\
                          .then_inc(sstream["mem_in"], 16)
                    sp.wait_ge(s["ltsb"], 1)
                    sp.dma_start(s_conv[0].rearrange("b k d -> (b k) d"), lrow[:]).then_inc(s["out_done"], 16)
                    sp.wait_ge(s["out_done"], 16)

                @b.gpsimd
                def _(pool):
                    pool.memset(same[:], 1.0).then_inc(s["made"], 1)
                    pool.memset(biasN[:], NEG).then_inc(s["kill"], 1)
                    pool.wait_ge(s["made"], 1)
                    pool.affine_select(out=same[:], in_=same[:], compare_op=ALU.is_ge, fill=0.0, base=0,
                                       pattern=[[-TS, NB], [0, TS]], channel_multiplier=1).then_inc(s["made"], 1)
                    pool.wait_ge(s["made"], 2)
                    pool.affine_select(out=same[:], in_=same[:], compare_op=ALU.is_ge, fill=0.0, base=TS - 1,
                                       pattern=[[TS, NB], [0, TS]], channel_multiplier=-1).then_inc(s["same"], 1)

                @b.scalar
                def _(act):
                    act.wait_ge(s["kill"], 1)
                    for b2 in range(2):
                        for t in range(TS):
                            rows = slice(b2 * 64 + t, b2 * 64 + t + 57, TS)
                            act.dma_start(biasC[rows, :],
                                          bass.AP(tensor=bias_rows, offset=127 - t, ap=[[RLEN, HS], [1, WIN]]))\
                               .then_inc(in_sems["rows_in"], 16)
                            for bp in range(4):
                                c0 = (2 * bp + b2) * TS
                                act.dma_start(biasN[rows, bp, c0:c0 + TS],
                                              bass.AP(tensor=bias_rows, offset=127 + WIN - t, ap=[[RLEN, HS], [1, TS]]))\
                                   .then_inc(in_sems["new_in"], 16)
                    for r in range(2):
                        act.dma_start(snkS[64 * r:64 * r + 64, :],
                                      bass.AP(tensor=sinks.tensor, offset=0, ap=[[1, HS], [0, TS], [1, 1]]))\
                           .then_inc(in_sems["rows_in"], 16)
                    act.wait_ge(s["hev"], 1)
                    s_norm_act(act, s, "n1")
                    for o in range(PAN_OUT):
                        act.wait_ge(sstream["lin_out"], o + 1)
                        src = L[:, o % 2, 0:S]
                        if o < PAN_K:
                            dst, f, sc = rawS[:, o, :, 3:], ACT.Copy, 1.0
                            src = src.rearrange("p (b t) -> p b t", t=TS)
                        elif o == PAN_K:
                            dst, f, sc = kS[:], ACT.Copy, 1.0
                        elif o == PAN_V:
                            dst, f, sc = vS[:], ACT.Copy, 1.0
                        elif o < PAN_Z:
                            dst, f, sc = qS[:, o - PAN_Q, :], ACT.Copy, 64 ** -0.5
                        else:
                            dst, f, sc = zsS[:, o - PAN_Z, :], ACT.Silu, 1.0
                        act.activation(dst, src, f, scale=sc).then_inc(s["lin_free"], 1)
                    act.wait_ge(s["conv"], 1)
                    act.activation(xbcS[:], convS[:], ACT.Silu)

                @b.vector
                def _(dve):
                    dve.wait_ge(s["xt"], 1)
                    dve.tensor_copy(hS[:], G[:, 0, :].rearrange("p (k t) -> p k t", t=S)).then_inc(s["hev"], 1)
                    dve.wait_ge(s["sct"], 1)
                    dve.tensor_copy(rawS[:, :, :, 0:3],
                                    G[:, 1, 0:24 * KT].rearrange("p (i b k) -> p i b k", b=NB, k=3))
                    dve.wait_ge(s["hev"], 1)
                    s_norm_dve(dve, s, "n1", PV_MIX, xS)
                    dve.wait_ge(s["same"], 1)
                    sm2 = same[:].rearrange("p b t -> p (b t)")
                    dve.tensor_tensor(leS[:], tri_le[0:S, 0:S], sm2, ALU.mult)
                    dve.tensor_tensor(gtS[:], tri_gt[0:S, 0:S], sm2, ALU.mult)
                    for i in range(8):
                        cv = convS[:, i, :].rearrange("p (b t) -> p b t", t=TS)
                        dve.wait_ge(s["lin_free"], i + 1)
                        dve.tensor_scalar(cv, rawS[:, i, :, 0:TS], g_of(PV_CW, i), g_of(PV_CB, i),
                                          ALU.mult, ALU.add)
                        for k in range(1, 4):
                            dve.drain()
                            last = dve.scalar_tensor_tensor(cv, rawS[:, i, :, k:k + TS], g_of(PV_CW + 8 * k, i), cv,
                                                            ALU.mult, ALU.add)
                    last.then_inc(s["conv"], 1)
                    dve.tensor_copy(lastS[:].rearrange("p i (b k) -> p i b k", k=3), rawS[:, :, :, TS:TS + 3])\
                       .then_inc(s["last"], 1)
                    dve.wait_ge(s["lt"], 1)
                    dve.tensor_copy(lrow[:], G[0:24, 2:4, :].rearrange("p a n -> p (a n)")).then_inc(s["ltsb"], 1)

                @b.tensor
                def _(pe):
                    pe.wait_ge(s["x_in"], 16)
                    for i in range(KT):
                        last = pe.transpose(G[:, 0, i * S:i * S + S], xin[:, i * P:i * P + P], ident[0:S, 0:S])
                    last.then_inc(s["xt"], 1)
                    pe.wait_ge(s["sc_in"], 16)
                    for i in range(KT):
                        last = pe.transpose(G[:, 1, i * 24:i * 24 + 24], scrow[:, i * P:i * P + P], ident[0:24, 0:24])
                    last.then_inc(s["sct"], 1)
                    s_norm_pe(pe, s, "n1")
                    pe.wait_ge(s["n1x"], 1)
                    for n in range(PAN_OUT):
                        s_multiply(pe, n, xS, lambda o: o >= 2 and pe.wait_ge(s["lin_free"], o - 1))
                    for k in range(KT):
                        last = pe.matmul(G[0:S, 5, 0:HS], xS[:, k, :], wdt[:, k, :], start=(k == 0),
                                         stop=(k == KT - 1))
                    last.then_inc(s["dtp"], 1)
                    pe.wait_ge(s["last"], 1)
                    for i in range(KT):
                        last = pe.transpose(G[0:24, 2 + i // 4, (i % 4) * P:(i % 4) * P + P], lastS[:, i, :], ident[:])
                    last.then_inc(s["lt"], 1)

        with ExitStack() as tmp:
            stT = sb("stT", [P, NB, 512], scope=tmp)
            Cz = sb("Cz", [P, NB, 2, S], scope=tmp)
            Bz = sb("Bz", [S, NB, 256], scope=tmp)
            xdtS = sb("xdtS", [S, 512], scope=tmp)
            xddS = sb("xddS", [S, 512], scope=tmp)
            yDS = sb("yDS", [S, 512], scope=tmp)
            yS = sb("yS", [S, 512], scope=tmp)
            btS = sb("btS", [S, 256], scope=tmp)
            rdaS = sb("rdaS", [S, HS * S], scope=tmp)
            ES = sb("ES", [S, HS * S], scope=tmp)
            cbS = sb("cbS", [S, 2 * S], scope=tmp)
            exS = sb("exS", [S, 2 * HS], scope=tmp)
            dab = sb("dab", [S, NB, HS], scope=tmp)
            edS = sb("edS", [P, NB, HS], scope=tmp)
            ssS = sb("ssS", [S, 5, 2], scope=tmp)
            junkS = sb("junkS", [S, 512], scope=tmp)
            Qz = sb("Qz", [P, NB, HS, TS], scope=tmp)
            kcT = sb("kcT", [P, NB, P], scope=tmp)
            ktS = sb("ktS", [S, P], scope=tmp)
            vtS = sb("vtS", [S, P], scope=tmp)
            sS = sb("sS", [P, 4, WIN + S], scope=tmp)
            stat = sb("stat", [P, 8, 4], scope=tmp)
            pcT = sb("pcT", [P, 4, P], scope=tmp)
            pnT = sb("pnT", [S, 4, P], scope=tmp)
            with Phase(["dtr", "dte", "dtu", "dtl", "da", "rda", "cum", "ex", "diff", "E", "xt", "bt", "btev",
                        "cb", "cz", "czero", "bz", "stt", "stev", "yoff", "xdd", "M", "yd", "zt", "y", "ss", "yn",
                        "yt", "ytev", "sn", "snew", "so", "soev", "qz", "qzero", "kct", "kcev", "new_t", "newev",
                        "sc", "nmax", "prob", "pn", "pt", "ptev", "pvs", "mix", "out_done"]) as (b, s):

                @b.sync
                def _(sp):
                    sp.wait_ge(s["newev"], 1)
                    sp.dma_start(s_swa_k[0, :, WIN - TS:WIN].rearrange("b t v d -> b t (v d)"), ktS[:])\
                      .then_inc(s["out_done"], 16)
                    sp.dma_start(s_swa_v[0, :, WIN - TS:WIN].rearrange("b t v d -> b t (v d)"), vtS[:])\
                      .then_inc(s["out_done"], 16)
                    for bb in range(NB):
                        sp.wait_ge(s["soev"], bb + 1)
                        sp.dma_start(s_ssm[0, bb].rearrange("(i h) p n -> (h p) i n", h=2), stN[:, bb])\
                          .then_inc(s["out_done"], 16)
                    sp.wait_ge(s["out_done"], 16 * (2 + NB))

                @b.gpsimd
                def _(pool):
                    pool.memset(Cz[:], 0.0).then_inc(s["czero"], 1)
                    pool.memset(Qz[:], 0.0).then_inc(s["qzero"], 1)

                @b.scalar
                def _(act):
                    act.wait_ge(s["dtr"], 1)
                    act.activation(dtS[:, 3, :], dtS[:, 2, :], ACT.Exp).then_inc(s["dte"], 1)
                    act.wait_ge(s["dtu"], 1)
                    act.activation(dtS[:, 5, :], dtS[:, 4, :], ACT.Ln).then_inc(s["dtl"], 1)
                    act.wait_ge(s["cum"], 1)
                    act.activation(exS[:], G[0:S, 2, 0:2 * HS], ACT.Exp)
                    act.activation(edS[:], G[:, 2, 64:64 + NB * HS].rearrange("p (b h) -> p b h", h=HS), ACT.Exp)\
                       .then_inc(s["ex"], 1)
                    act.wait_ge(s["diff"], 1)
                    act.activation(ES[:], G[0:S, 3, :], ACT.Exp).then_inc(s["E"], 1)
                    for bb in range(NB):
                        act.wait_ge(s["stt"], bb + 1)
                        act.activation(stT[:, bb, :], L[:, bb % 2, :], ACT.Copy).then_inc(s["stev"], 1)
                    act.wait_ge(s["y"], 1)
                    for g in range(2):
                        act.activation(junkS[:, g * 256:g * 256 + 256], yS[:, g * 256:g * 256 + 256], ACT.Square,
                                       accum_out=ssS[:, 0, g:g + 1]).then_inc(s["ss"], 1)
                    act.wait_ge(s["yt"], 1)
                    for i in range(4):
                        last = act.activation(xS[:, i, :], G[:, 0, i * S:i * S + S], ACT.Copy, scale=g_of(PV_SSD, i))
                    last.then_inc(s["ytev"], 1)
                    for bb in range(NB):
                        act.wait_ge(s["so"], bb + 1)
                        act.activation(stN[:, bb], L[:, bb % 2, :].rearrange("p (i n) -> p i n", n=P), ACT.Copy)\
                           .then_inc(s["soev"], 1)
                    for g in range(2):
                        act.wait_ge(s["kct"], g + 1)
                        act.activation(kcT[:, 4 * g:4 * g + 4, :], G[:, g, :].rearrange("p (b t) -> p b t", t=P),
                                       ACT.Copy).then_inc(s["kcev"], 1)
                    act.wait_ge(s["nmax"], 1)
                    for bp in range(4):
                        act.activation(sS[:, bp, :], sS[:, bp, :], ACT.Exp, bias=stat[:, 2, bp:bp + 1],
                                       accum_out=stat[:, 4, bp:bp + 1])
                    act.activation(stat[:, 5, :], stat[:, 3, :], ACT.Exp).then_inc(s["prob"], 1)

                @b.vector
                def _(dve):
                    dt_, d, na, e, u, ln, q, r, da_ = (dtS[:, i, :] for i in range(9))
                    d, dt_ = dtS[:, 1, :], dtS[:, 0, :]
                    dve.tensor_tensor(d, G[0:S, 5, 0:HS], dtb[0:S, :], ALU.add)
                    dve.drain()
                    dve.scalar_tensor_tensor(na, d, -1.0, d, ALU.mult, ALU.min).then_inc(s["dtr"], 1)
                    dve.wait_ge(s["dte"], 1)
                    dve.tensor_scalar(u, e, 1.0, None, ALU.add).then_inc(s["dtu"], 1)
                    dve.wait_ge(s["dtu"], 1)
                    dve.tensor_scalar(q, u, -1.0, None, ALU.add)
                    dve.drain()
                    dve.tensor_scalar(r, q, 1e-30, None, ALU.max)
                    dve.drain()
                    dve.reciprocal(r, r)
                    dve.tensor_scalar(q, q, 0.0, None, ALU.is_equal)
                    dve.wait_ge(s["dtl"], 1)
                    dve.drain()
                    dve.tensor_tensor(r, r, ln, ALU.mult)
                    dve.drain()
                    dve.tensor_tensor(r, r, q, ALU.add)
                    dve.drain()
                    dve.tensor_tensor(r, r, e, ALU.mult)
                    dve.drain()
                    dve.scalar_tensor_tensor(dt_, d, 0.0, r, ALU.max, ALU.add)
                    dve.drain()
                    dve.tensor_tensor(da_, dt_, nega[0:S, :], ALU.mult)
                    dve.drain()
                    sel = same[:, :, 0]
                    bch = lambda t, w: t.unsqueeze(2).to_broadcast([S, t.shape[1], w])
                    v3 = lambda t: t.rearrange("p (h w) -> p h w", h=HS)
                    dve.tensor_tensor(dab[:], bch(sel, HS), da_.unsqueeze(1).to_broadcast([S, NB, HS]), ALU.mult)\
                       .then_inc(s["da"], 1)
                    dve.tensor_tensor(v3(rdaS[:]), leS[:].unsqueeze(1).to_broadcast([S, HS, S]), bch(da_, S),
                                      ALU.mult).then_inc(s["rda"], 1)
                    dve.wait_ge(s["xt"], 1)
                    dve.tensor_tensor(v3(xdtS[:]), v3(G[0:S, 0, :]), bch(dt_, HP), ALU.mult)
                    dve.tensor_tensor(v3(yDS[:]), v3(G[0:S, 0, :]), bch(dsk[0:S, :], HP), ALU.mult)
                    dve.wait_ge(s["ex"], 1)
                    dve.drain()
                    dve.tensor_tensor(v3(xddS[:]), v3(xdtS[:]), bch(exS[:, HS:2 * HS], HP), ALU.mult)\
                       .then_inc(s["xdd"], 1)
                    dve.wait_ge(s["bt"], 1)
                    dve.tensor_copy(btS[:], G[0:S, 1, 0:256]).then_inc(s["btev"], 1)
                    dve.wait_ge(s["btev"], 1)
                    for bb in range(NB):
                        last = dve.tensor_scalar(Bz[:, bb, :], btS[:], same[:, bb, 0:1], None, ALU.mult)
                    last.then_inc(s["bz"], 1)
                    dve.wait_ge(s["czero"], 1)
                    for bb in range(NB):
                        t = slice(bb * TS, bb * TS + TS)
                        last = dve.tensor_copy(Cz[:, bb, :, t], xbcS[:, 6:8, t])
                    last.then_inc(s["cz"], 1)
                    dve.wait_ge(s["cb"], 1)
                    dve.tensor_tensor(cbS[:].rearrange("p (g q) -> p g q", g=2),
                                      G[0:S, 1, 256:256 + 2 * S].rearrange("p (g q) -> p g q", g=2),
                                      leS[:].unsqueeze(1).to_broadcast([S, 2, S]), ALU.mult)
                    dve.wait_ge(s["E"], 1)
                    dve.drain()
                    for g in range(2):
                        eg = ES[:, g * 256:g * 256 + 256].rearrange("p (h q) -> p h q", h=4)
                        last = dve.tensor_tensor(eg, eg, cbS[:, g * S:g * S + S].unsqueeze(1)
                                                 .to_broadcast([S, 4, S]), ALU.mult)
                    last.then_inc(s["M"], 1)
                    dve.wait_ge(s["yoff"], 1)
                    dve.tensor_tensor(v3(yS[:]), v3(G[0:S, 4, :]), bch(exS[:, 0:HS], HP), ALU.mult)
                    dve.drain()
                    dve.tensor_tensor(yS[:], yS[:], yDS[:], ALU.add)
                    dve.drain()
                    dve.wait_ge(s["yd"], 1)
                    dve.tensor_tensor(yS[:], yS[:], G[0:S, 3, :], ALU.add)
                    dve.drain()
                    dve.wait_ge(s["zt"], 1)
                    dve.tensor_tensor(yS[:], yS[:], G[0:S, 0, :], ALU.mult).then_inc(s["y"], 1)
                    dve.wait_ge(s["ss"], 2)
                    dve.tensor_scalar(ssS[:, 1, :], ssS[:, 0, :], 1.0 / 256, EPS, ALU.mult, ALU.add)
                    dve.drain()
                    rsqrt(dve, ssS[:, 1, :], ssS[:, 2, :], ssS[:, 3, :])
                    yv = yS[:].rearrange("p (g w) -> p g w", g=2)
                    dve.tensor_tensor(yv, yv, bch(ssS[:, 2, :], 256), ALU.mult).then_inc(s["yn"], 1)
                    for bb in range(NB):
                        sv = stT[:, bb, :].rearrange("p (h w) -> p h w", h=HS)
                        dve.wait_ge(s["sn"], bb + 1)
                        dve.tensor_tensor(sv, sv, edS[:, bb, :].unsqueeze(2).to_broadcast([P, HS, HP]), ALU.mult)
                        dve.drain()
                        dve.tensor_tensor(stT[:, bb, :], stT[:, bb, :], G[:, 2 + bb % 2, :], ALU.add)\
                           .then_inc(s["snew"], 1)
                    dve.wait_ge(s["qzero"], 1)
                    for j in range(QJ):
                        for v in range(KV):
                            r_ = slice(64 * v, 64 * v + 64)
                            last = dve.tensor_copy(Qz[r_, :, QJ * v + j, :],
                                                   qS[r_, j, :].rearrange("p (b t) -> p b t", t=TS))
                    last.then_inc(s["qz"], 1)
                    dve.wait_ge(s["new_t"], 1)
                    dve.tensor_copy(ktS[:], G[0:S, 4, 0:P])
                    dve.tensor_copy(vtS[:], G[0:S, 4, P:2 * P]).then_inc(s["newev"], 1)
                    dve.wait_ge(s["sc"], 1)
                    dve.wait_ge(in_sems["rows_in"], 16 * (2 * TS + 2))
                    dve.wait_ge(in_sems["new_in"], 16 * 8 * TS)
                    for a in range(2):
                        ps = G[:, 2 + a, 0:2 * (WIN + S)].rearrange("p (c k) -> p c k", c=2)
                        cs2 = slice(2 * a, 2 * a + 2)
                        dve.tensor_tensor(sS[:, cs2, 0:WIN], ps[:, :, 0:WIN],
                                          biasC[:].unsqueeze(1).to_broadcast([P, 2, WIN]), ALU.add)
                        dve.tensor_tensor(sS[:, cs2, WIN:], ps[:, :, WIN:], biasN[:, cs2, :], ALU.add)
                    dve.drain()
                    dve.tensor_reduce(stat[:, 0, :], sS[:], AX_X, ALU.max)
                    dve.drain()
                    dve.tensor_scalar(stat[:, 1, :], stat[:, 0, :], snkS[:], None, ALU.max)
                    dve.drain()
                    dve.tensor_scalar(stat[:, 2, :], stat[:, 1, :], -1.0, None, ALU.mult)
                    dve.tensor_scalar(stat[:, 3, :], stat[:, 1, :], -1.0, snkS[:], ALU.mult, ALU.add)\
                       .then_inc(s["nmax"], 1)
                    dve.wait_ge(s["prob"], 1)
                    dve.tensor_tensor(stat[:, 6, :], stat[:, 4, :], stat[:, 5, :], ALU.add)
                    dve.drain()
                    dve.reciprocal(stat[:, 7, :], stat[:, 6, :])
                    dve.drain()
                    dve.tensor_tensor(sS[:], sS[:], stat[:, 7, :].unsqueeze(2).to_broadcast([P, 4, WIN + S]),
                                      ALU.mult).then_inc(s["pn"], 1)
                    dve.wait_ge(s["pt"], 1)
                    dve.tensor_copy(pcT[:], G[:, 0, :].rearrange("p (b r) -> p b r", r=P))
                    dve.tensor_copy(pnT[:], G[0:S, 1, :].rearrange("p (b r) -> p b r", r=P)).then_inc(s["ptev"], 1)
                    dve.wait_ge(s["pvs"], 1)
                    dve.wait_ge(s["ytev"], 1)
                    for v in range(KV):
                        r_ = slice(64 * v, 64 * v + 64)
                        src = G[r_, 4, :].rearrange("p (b h t) -> p h b t", h=HS, t=TS)
                        last = dve.tensor_copy(xS[r_, 4:8, :].rearrange("p j (b t) -> p j b t", t=TS),
                                               src[:, QJ * v:QJ * v + QJ])
                    last.then_inc(s["mix"], 1)

                @b.tensor
                def _(pe):
                    for i in range(4):
                        last = pe.transpose(G[0:S, 0, i * P:i * P + P], xbcS[:, i, :], ident[:])
                    last.then_inc(s["xt"], 1)
                    for g in range(2):
                        last = pe.transpose(G[0:S, 1, g * P:g * P + P], xbcS[:, 4 + g, :], ident[:])
                    last.then_inc(s["bt"], 1)
                    pe.wait_ge(in_sems["ssm_in"], 16 * NB)
                    for bb in range(NB):
                        if bb >= 2:
                            pe.wait_ge(s["stev"], bb - 1)
                        for i in range(4):
                            last = pe.transpose(L[:, bb % 2, i * P:i * P + P], stN[:, bb, i, :], ident[:])
                        last.then_inc(s["stt"], 1)
                        if bb == 0:
                            pe.wait_ge(s["da"], 1)
                            da_ = dtS[:, 8, :]
                            pe.matmul(G[0:S, 2, 0:HS], leS[:], da_, start=True, stop=True)
                            pe.matmul(G[0:S, 2, HS:2 * HS], gtS[:], da_, start=True, stop=True)
                            pe.matmul(G[:, 2, 64:64 + NB * HS], ones[0:S, :], dab[:], start=True, stop=True)\
                              .then_inc(s["cum"], 1)
                            pe.wait_ge(s["rda"], 1)
                            pe.matmul(G[0:S, 3, :], gtS[:], rdaS[:], start=True, stop=True).then_inc(s["diff"], 1)
                    pe.wait_ge(s["btev"], 1)
                    for g in range(2):
                        last = pe.matmul(G[0:S, 1, 256 + g * S:256 + g * S + S], xbcS[:, 4 + g, :], xbcS[:, 6 + g, :],
                                         start=True, stop=True)
                    last.then_inc(s["cb"], 1)
                    pe.wait_ge(s["stev"], NB)
                    pe.wait_ge(s["cz"], 1)
                    for g in range(2):
                        for bb in range(NB):
                            last = pe.matmul(G[0:S, 4, g * 256:g * 256 + 256], Cz[:, bb, g, :],
                                             stT[:, bb, g * 256:g * 256 + 256], start=(bb == 0), stop=(bb == NB - 1))
                    last.then_inc(s["yoff"], 1)
                    pe.wait_ge(s["M"], 1)
                    for h in range(HS):
                        last = pe.matmul(G[0:S, 3, h * HP:h * HP + HP], ES[:, h * S:h * S + S],
                                         xdtS[:, h * HP:h * HP + HP], start=True, stop=True)
                    last.then_inc(s["yd"], 1)
                    pe.wait_ge(s["xdd"], 1)
                    for i in range(4):
                        last = pe.transpose(G[0:S, 0, i * P:i * P + P], zsS[:, i, :], ident[:])
                    last.then_inc(s["zt"], 1)
                    pe.wait_ge(s["yn"], 1)
                    for i in range(4):
                        last = pe.transpose(G[:, 0, i * S:i * S + S], yS[:, i * P:i * P + P], ident[0:S, 0:S])
                    last.then_inc(s["yt"], 1)

                    def back(bb):
                        pe.wait_ge(s["snew"], bb + 1)
                        if bb >= 2:
                            pe.wait_ge(s["soev"], bb - 1)
                        for i in range(4):
                            last = pe.transpose(L[:, bb % 2, i * P:i * P + P], stT[:, bb, i * P:i * P + P], ident[:])
                        last.then_inc(s["so"], 1)

                    pe.wait_ge(s["bz"], 1)
                    for bb in range(NB):
                        if bb >= 2:
                            pe.wait_ge(s["snew"], bb - 1)
                        for g in range(2):
                            last = pe.matmul(G[:, 2 + bb % 2, g * 256:g * 256 + 256], Bz[:, bb, g * P:g * P + P],
                                             xddS[:, g * 256:g * 256 + 256], start=True, stop=True)
                        last.then_inc(s["sn"], 1)
                        if bb >= 1:
                            back(bb - 1)
                    back(NB - 1)
                    pe.transpose(G[0:S, 4, 0:P], kS[:], ident[:])
                    pe.transpose(G[0:S, 4, P:2 * P], vS[:], ident[:]).then_inc(s["new_t"], 1)
                    pe.wait_ge(in_sems["swa_in"], 32)
                    pe.wait_ge(s["ytev"], 1)
                    for bb in range(NB):
                        last = pe.transpose(G[:, bb // 4, (bb % 4) * P:(bb % 4) * P + P], swK[:, bb, :], ident[:])
                        if bb % 4 == 3:
                            last.then_inc(s["kct"], 1)
                    pe.wait_ge(s["kcev"], 2)
                    pe.wait_ge(s["qz"], 1)
                    for bb in range(NB):
                        r = slice(64 * (bb % 2), 64 * (bb % 2) + 64)
                        bp = bb // 2
                        c0 = (bp % 2) * (WIN + S)
                        lq = Qz[:, bb].rearrange("p h t -> p (h t)")
                        pe.matmul(G[r, 2 + bp // 2, c0:c0 + WIN], lq, kcT[:, bb, :], start=True, stop=True)
                        last = pe.matmul(G[r, 2 + bp // 2, c0 + WIN:c0 + WIN + S], lq, kS[:], start=True, stop=True)
                    last.then_inc(s["sc"], 1)
                    pe.wait_ge(s["pn"], 1)
                    for bp in range(4):
                        pe.transpose(G[:, 0, bp * P:bp * P + P], sS[:, bp, 0:WIN], ident[:])
                    for bp in range(4):
                        last = pe.transpose(G[0:S, 1, bp * P:bp * P + P], sS[:, bp, WIN:], ident[:])
                    last.then_inc(s["pt"], 1)
                    pe.wait_ge(s["ptev"], 1)
                    for bb in range(NB):
                        r = slice(64 * (bb % 2), 64 * (bb % 2) + 64)
                        o = G[:, 4, bb * 64:bb * 64 + 64]
                        pe.matmul(o, swV[:, bb, :], pcT[:, bb // 2, r], start=True, stop=False)
                        last = pe.matmul(o, vtS[:], pnT[:, bb // 2, r], start=False, stop=True)
                    last.then_inc(s["pvs"], 1)
        clear(in_sems.values())
        mixer.close()

        with ExitStack() as tmp:
            kmS = sb("kmS", [P, NB, CH, NMEM], scope=tmp)
            Qc = sb("Qc", [P, NB, CH, CH, TS], scope=tmp)
            sX = sb("sX", [P, 2, NMEM], scope=tmp)
            stx = sb("stx", [P, 4, 2], scope=tmp)
            pxT = sb("pxT", [P, 2, 2, P], scope=tmp)
            oS = sb("oS", [P, CH, S], scope=tmp)
            hid = sb("hid", [P, 8, S], scope=tmp)
            sgS = sb("sgS", [P, 2, S], scope=tmp)
            yoS = sb("yoS", [S, D], scope=tmp)
            O_OUT, O_CQ, O_CO, O_FFN = (first_out[n] for n in (PAN_OUT, PAN_CQ, PAN_CO, PAN_FFN))
            with Phase(["h1", "h2", "h3", "kt", "kev", "qzero", "q", "sc", "cmax", "cexp", "pn", "pt", "ptev",
                        "o", "oev", "gate", "up", "yt", "yev", "out_done"]
                       + [t + n for t in ("n2", "n3", "nf") for n in SNORM]) as (b, s):

                @b.sync
                def _(sp):
                    s_load(sp, PAN_OUT + SR, NPAN)
                    sp.wait_ge(s["yev"], 1)
                    sp.dma_start(y_sample.rearrange("b t d -> (b t) d"), yoS[:]).then_inc(s["out_done"], 16)
                    sp.wait_ge(s["out_done"], 16)

                @b.gpsimd
                def _(pool):
                    pool.memset(Qc[:], 0.0).then_inc(s["qzero"], 1)

                @b.scalar
                def _(act):
                    for n in range(2 * NB):
                        act.wait_ge(s["kt"], n + 1)
                        act.activation(kmS[:, n // 2, :, (n % 2) * P:(n % 2) * P + P],
                                       G[:, n % 2, :].rearrange("p (h m) -> p h m", m=P), ACT.Copy)\
                           .then_inc(s["kev"], 1)
                    act.wait_ge(s["h1"], KT)
                    s_norm_act(act, s, "n2")
                    act.wait_ge(s["cmax"], 1)
                    for g in range(2):
                        act.activation(sX[:, g, :], G[:, 2, g * NMEM:g * NMEM + NMEM], ACT.Exp,
                                       bias=stx[:, 0, g:g + 1], accum_out=stx[:, 1, g:g + 1]).then_inc(s["cexp"], 1)
                    act.wait_ge(s["h2"], KT)
                    s_norm_act(act, s, "n3")
                    for o, (kind, i, g) in enumerate(steps):
                        if kind == "gate":
                            act.wait_ge(sstream["lin_out"], O_FFN + o + 1)
                            if i >= 2:
                                act.wait_ge(s["up"], i - 1)
                            act.activation(sgS[:, i % 2, :], L[:, o % 2, 0:S], ACT.Silu).then_inc(s["gate"], 1)
                    act.wait_ge(s["h3"], KT * len(FGROUPS))
                    s_norm_act(act, s, "nf")

                @b.vector
                def _(dve):
                    for n in range(KT):
                        s_residual(dve, s, "h1", O_OUT, n)
                    s_norm_dve(dve, s, "n2", PV_CROSS, xS)
                    dve.wait_ge(s["qzero"], 1)
                    for h in range(CH):
                        dve.wait_ge(sstream["lin_out"], O_CQ + h + 1)
                        dve.tensor_scalar(Qc[:, :, h, h, :],
                                          L[:, (O_CQ + h) % 2, 0:S].rearrange("p (b t) -> p b t", t=TS),
                                          P ** -0.5, None, ALU.mult).then_inc(s["q"], 1)
                    dve.wait_ge(s["sc"], 1)
                    dve.tensor_reduce(stx[:, 0, :], G[:, 2, :].rearrange("p (g m) -> p g m", g=2), AX_X, ALU.max,
                                      negate=True).then_inc(s["cmax"], 1)
                    dve.wait_ge(s["cexp"], 2)
                    dve.reciprocal(stx[:, 2, :], stx[:, 1, :])
                    dve.drain()
                    dve.tensor_tensor(sX[:], sX[:], stx[:, 2, :].unsqueeze(2).to_broadcast([P, 2, NMEM]), ALU.mult)\
                       .then_inc(s["pn"], 1)
                    dve.wait_ge(s["pt"], 1)
                    dve.tensor_copy(pxT[:], G[:, 3, :].rearrange("p (g m r) -> p g m r", g=2, m=2))\
                       .then_inc(s["ptev"], 1)
                    dve.wait_ge(s["o"], 1)
                    dve.tensor_copy(oS[:], G[:, 0, 0:CH * S].rearrange("p (h t) -> p h t", t=S)).then_inc(s["oev"], 1)
                    for n in range(KT):
                        s_residual(dve, s, "h2", O_CO, n)
                    s_norm_dve(dve, s, "n3", PV_FFN, xS)
                    for o, (kind, i, g) in enumerate(steps):
                        if kind == "up":
                            dve.wait_ge(s["gate"], i + 1)
                            dve.wait_ge(sstream["lin_out"], O_FFN + o + 1)
                            dve.tensor_tensor(hid[:, i % 8, :], sgS[:, i % 2, :], L[:, o % 2, 0:S], ALU.mult)\
                               .then_inc(s["up"], 1)
                        elif kind == "down":
                            if g >= 1:
                                dve.wait_ge(s["h3"], (g - 1) * KT + i + 1)
                            dve.wait_ge(sstream["lin_out"], O_FFN + o + 1)
                            dve.tensor_tensor(hS[:, i, :], L[:, o % 2, 0:S], hS[:, i, :], ALU.add)\
                               .then_inc(s["h3"], 1)
                    s_norm_dve(dve, s, "nf", PV_FINAL, xS)
                    dve.wait_ge(s["yt"], 1)
                    dve.tensor_copy(yoS[:], G[0:S, 0:2, :].rearrange("p a n -> p (a n)")).then_inc(s["yev"], 1)

                @b.tensor
                def _(pe):
                    for n in range(PAN_OUT, PAN_CQ):
                        s_multiply(pe, n, xS, lambda o: o >= O_OUT + 2 and pe.wait_ge(s["h1"], o - O_OUT - 1))
                    pe.wait_ge(sstream["mem_in"], 16 * 2 * NB)
                    for n in range(2 * NB):
                        if n >= 2:
                            pe.wait_ge(s["kev"], n - 1)
                        for h in range(CH):
                            last = pe.transpose(G[:, n % 2, h * P:h * P + P], memK[:, n // 2, n % 2, h * P:h * P + P],
                                                ident[:])
                        last.then_inc(s["kt"], 1)
                    s_norm_pe(pe, s, "n2")
                    pe.wait_ge(s["n2x"], 1)
                    for n in range(CH):
                        s_multiply(pe, PAN_CQ + n, xS, lambda o: o >= O_CQ + 2 and pe.wait_ge(s["q"], o - O_CQ - 1))
                    pe.wait_ge(s["kev"], 2 * NB)
                    pe.wait_ge(s["q"], CH)
                    for bb in range(NB):
                        r = slice(32 * (bb % 4), 32 * (bb % 4) + 32)
                        g = bb // 4
                        for h in range(CH):
                            last = pe.matmul(G[r, 2, g * NMEM:g * NMEM + NMEM],
                                             Qc[:, bb, h].rearrange("p a t -> p (a t)"), kmS[:, bb, h, :],
                                             start=(h == 0), stop=(h == CH - 1), tile_position=(0, 32 * (bb % 4)))
                    last.then_inc(s["sc"], 1)
                    pe.wait_ge(s["pn"], 1)
                    for g in range(2):
                        for m in range(2):
                            i = 2 * g + m
                            last = pe.transpose(G[:, 3, i * P:i * P + P], sX[:, g, m * P:m * P + P], ident[:])
                    last.then_inc(s["pt"], 1)
                    pe.wait_ge(s["ptev"], 1)
                    for h in range(CH):
                        for bb in range(NB):
                            r0 = 32 * (bb % 4) + TS * h
                            for m in range(2):
                                last = pe.matmul(G[:, 0, h * S + bb * TS:h * S + bb * TS + TS],
                                                 memV[:, bb, m, h * P:h * P + P], pxT[:, bb // 4, m, r0:r0 + TS],
                                                 start=(m == 0), stop=(m == 1))
                    last.then_inc(s["o"], 1)
                    pe.wait_ge(s["oev"], 1)
                    for n in range(4):
                        s_multiply(pe, PAN_CO + n, oS, lambda o: o >= O_CO + 2 and pe.wait_ge(s["h2"], o - O_CO - 1))
                    s_norm_pe(pe, s, "n3")
                    pe.wait_ge(s["n3x"], 1)
                    for o, (kind, i, g) in enumerate(steps):
                        f0, f1 = FGROUPS[g]

                        def free(_, o=o):
                            if o < 2:
                                return
                            kind2, i2, g2 = steps[o - 2]
                            if kind2 == "down":
                                pe.wait_ge(s["h3"], g2 * KT + i2 + 1)
                            else:
                                pe.wait_ge(s[kind2], i2 + 1)

                        if kind == "down":
                            if i == 0:
                                pe.wait_ge(s["up"], f1)
                            s_multiply(pe, PAN_FFN + o, hid, free)
                        else:
                            s_multiply(pe, PAN_FFN + o, xS, free)
                    s_norm_pe(pe, s, "nf")
                    pe.wait_ge(s["nfx"], 1)
                    for i in range(KT):
                        last = pe.transpose(G[0:S, i // 4, (i % 4) * P:(i % 4) * P + P], xS[:, i, :], ident[:])
                    last.then_inc(s["yt"], 1)


_INS = ['x_prompt', 'x_sample', 'mem_prompt', 'state_conv', 'state_ssm', 'cache_swa_k', 'cache_swa_v',
        'cache_mem_k', 'cache_mem_v', 'rel_bias', 'g_mix', 'w_in', 'conv_w', 'conv_b', 'dt_bias', 'a_log',
        'd_skip', 'g_ssd_norm', 'sinks', 'w_out', 'g_cross', 'g_mem', 'w_cq', 'w_ck', 'w_cv', 'w_co', 'g_ffn',
        'w_gate', 'w_up', 'w_down', 'g_final']
_OUTS = [(1, 2048, 1024), (8, 8, 1024), (1, 1, 3, 1024), (1, 1, 8, 64, 128), (1, 1, 128, 2, 64),
         (1, 1, 128, 2, 64), (1, 1, 256, 4, 128), (1, 1, 256, 4, 128), (1, 8, 3, 1024), (1, 8, 8, 64, 128),
         (1, 8, 128, 2, 64), (1, 8, 128, 2, 64)]


def shape_tables():
    import math
    import numpy as np

    onehot = np.zeros((32, RLEN), np.float32)
    mask = np.full((HS, RLEN), NEG, np.float32)
    for m in range(RLEN):
        dist = 255 - m
        if not 0 <= dist < WIN:
            continue
        bucket = dist
        if dist >= 16:
            big = np.float32(np.log(np.float32(dist) / np.float32(16)))
            bucket = min(31, 16 + int(np.float32(big / np.float32(math.log(8)) * np.float32(16))))
        onehot[bucket, m] = 1
        mask[:, m] = 0
    return onehot, mask


def kernel(**inputs):
    import numpy as _np
    import concourse.bacc as _bacc
    from concourse import mybir as _mybir
    from concourse.bass_utils import run_bass_kernel_spmd as _run

    nc = _bacc.Bacc("TRN2", target_bir_lowering=False, num_devices=1)
    arrays, args = {}, []
    onehot, mask = shape_tables()
    for name in _INS + ["bucket_onehot", "row_mask"]:
        a = {"bucket_onehot": onehot, "row_mask": mask}[name] if name in ("bucket_onehot", "row_mask") \
            else _np.ascontiguousarray(inputs[name])
        arrays[f"in_{name}_dram"] = a
        args.append(nc.dram_tensor(f"in_{name}_dram", a.shape, _mybir.dt.from_np(a.dtype), kind="ExternalInput").ap())
    for i, shape in enumerate(_OUTS):
        args.append(nc.dram_tensor(f"out_{i}_dram", shape, _mybir.dt.float32, kind="ExternalOutput").ap())
    build(nc, *args)
    r = _run(nc, [arrays], core_ids=[0])
    return tuple(r.results[0][f"out_{i}_dram"] for i in range(len(_OUTS)))
```

```python
from contextlib import ExitStack

import concourse.bass as bass
from concourse import mybir

F32 = mybir.dt.float32
F32R = mybir.dt.float32r
I32 = mybir.dt.int32
ALU = mybir.AluOpType
ACT = mybir.ActivationFunctionType
AX_X = mybir.AxisListType.X

P = 128
D = 1024
KT = D // P
SEQ = 2048
TB = 512
NBLK = SEQ // TB
C = TB // P
NB, TS = 8, 8
S = NB * TS
HS = 8
HP = 64
NST = 128
CONVD = 1024
KV = 2
QJ = 4
WIN = 128
NMEM = 256
CH = 4
DFF = 2816
FT = DFF // P
EPS = 1e-6
NEG = -1e30
COL_Z, COL_X, COL_DT, COL_Q, COL_K, COL_V = 0, 512, 1536, 1544, 2056, 2184
RING = 3
AHEAD = 2
FGROUPS = [(0, 8), (8, 16), (16, 22)]
RLEN = 383

PV_MIX, PV_CROSS, PV_FFN, PV_FINAL, PV_MEM, PV_CB, PV_CW, PV_SSD = 0, 8, 16, 24, 32, 40, 48, 80
PV_ROWS = 84


def weight_panels(w_in, w_out, w_cq, w_co, w_gate, w_up, w_down):
    def cols(w, c, n=P):
        return w[:, c:c + n].rearrange("(k p) n -> p k n", p=P)

    panels = []
    for i in range(8):
        panels.append(([(0, KT, 0, P, cols(w_in, COL_X + i * P))], KT, 1))
    panels.append(([(0, KT, 0, P, cols(w_in, COL_K))], KT, 1))
    panels.append(([(0, KT, 0, P, cols(w_in, COL_V))], KT, 1))
    for j in range(QJ):
        panels.append(([(0, KT, 0, 64, cols(w_in, COL_Q + 64 * j, 64)),
                        (0, KT, 64, 64, cols(w_in, COL_Q + 256 + 64 * j, 64))], KT, 1))
    for i in range(4):
        panels.append(([(0, KT, 0, P, cols(w_in, COL_Z + i * P))], KT, 1))
    for n in range(KT):
        c = slice(n * P, n * P + P)
        top = w_out[0:512, c].rearrange("(k p) n -> p k n", p=P)
        att = w_out[512:1024, c].rearrange("(v j d) n -> v d j n", v=KV, j=QJ)
        panels.append(([(0, 4, 0, P, top), ("kv", att)], KT, 1))
    for n in range(CH):
        panels.append(([(0, KT, 0, P, cols(w_cq, n * P))], KT, 1))
    for n in range(4):
        panels.append(([("wide", w_co[:, n * 256:n * 256 + 256].rearrange("(k p) n -> p k n", p=P))], 4, 2))
    for f0, f1 in FGROUPS:
        for f in range(f0, f1):
            panels.append(([(0, KT, 0, P, cols(w_gate, f * P))], KT, 1))
            panels.append(([(0, KT, 0, P, cols(w_up, f * P))], KT, 1))
        for n in range(KT):
            src = w_down[f0 * P:f1 * P, n * P:n * P + P].rearrange("(k p) n -> p k n", p=P)
            panels.append(([(0, f1 - f0, 0, P, src)], f1 - f0, 1))
    return panels


def panel_slices(slot, parts):
    tiles = slot.rearrange("p (k n) -> p k n", n=P)
    out = []
    for part in parts:
        if part[0] == "kv":
            for v in range(KV):
                out.append((tiles[64 * v:64 * v + 64, 4:8, :], part[1][v]))
        elif part[0] == "wide":
            out.append((slot.rearrange("p (k n) -> p k n", n=256), part[1]))
        else:
            k0, kn, c0, cn, src = part
            out.append((tiles[:, k0:k0 + kn, c0:c0 + cn], src))
    return out


def rsqrt(dve, v, r, t):
    dve.tensor_scalar(r.bitcast(I32), v.bitcast(I32), 1, None, ALU.arith_shift_right)
    dve.drain()
    dve.tensor_scalar(r.bitcast(I32), r.bitcast(I32), -1.0, float(0x5F3759DF), ALU.mult, ALU.add)
    dve.drain()
    for _ in range(3):
        dve.scalar_tensor_tensor(t, r, -0.5, r, ALU.mult, ALU.mult)
        dve.drain()
        dve.tensor_tensor(t, t, v, ALU.mult)
        dve.drain()
        dve.scalar_tensor_tensor(r, t, 1.5, r, ALU.add, ALU.mult)
        dve.drain()


def build(nc, x_prompt, x_sample, mem_prompt, state_conv, state_ssm, cache_swa_k, cache_swa_v,
          cache_mem_k, cache_mem_v, rel_bias, g_mix, w_in, conv_w, conv_b, dt_bias, a_log, d_skip,
          g_ssd_norm, sinks, w_out, g_cross, g_mem, w_cq, w_ck, w_cv, w_co, g_ffn, w_gate, w_up, w_down,
          g_final, bucket_onehot, row_mask,
          y_prompt, y_sample, p_conv, p_ssm, p_swa_k, p_swa_v, p_mem_k, p_mem_v,
          s_conv, s_ssm, s_swa_k, s_swa_v):
    w_in, w_out, w_cq, w_ck, w_cv, w_co = (w[0] for w in (w_in, w_out, w_cq, w_ck, w_cv, w_co))
    w_gate, w_up, w_down = w_gate[0], w_up[0], w_down[0]
    bias_rows = nc.dram_tensor("bias_rows", [HS, RLEN], F32)
    panels = weight_panels(w_in, w_out, w_cq, w_co, w_gate, w_up, w_down)
    NPAN = len(panels)
    first_out = [sum(p[2] for p in panels[:n]) for n in range(NPAN + 1)]
    first_dma = {}
    on_slot = [0] * RING
    for n, (parts, _, _) in enumerate(panels):
        on_slot[n % RING] += sum(KV if part[0] == "kv" else 1 for part in parts)
        first_dma[n] = on_slot[n % RING]
    PAN_XBC, PAN_K, PAN_V, PAN_Q, PAN_Z, PAN_OUT = 0, 8, 9, 10, 14, 18
    PAN_CQ, PAN_CO, PAN_FFN = 26, 30, 34

    with ExitStack() as whole:
        def sb(name, shape, dt=F32, scope=whole):
            return scope.enter_context(nc.sbuf_tensor(name, shape, dt))

        G = whole.enter_context(nc.psum_tensor("G", [P, 6, 512], F32))
        L = whole.enter_context(nc.psum_tensor("L", [P, 2, 512], F32))

        ident = sb("ident", [P, P])
        ones = sb("ones", [P, P])
        tri_le = sb("tri_le", [P, P])
        tri_gt = sb("tri_gt", [P, P])
        pv = sb("pv", [P, PV_ROWS])
        dtb = sb("dtb", [P, HS])
        nega = sb("nega", [P, HS])
        dsk = sb("dsk", [P, HS])
        snk = sb("snk", [P, HS])
        wdt = sb("wdt", [P, KT, HS])
        wdt_h = sb("wdt_h", [P, KT, HS], F32R)
        wdt_l = sb("wdt_l", [P, KT, HS], F32R)
        small = sb("small", [P, 12, 16])
        diag = sb("diag", [P, TB])

        def g_of(row, i):
            return pv[:, row + i:row + i + 1]

        phase_count = [0]

        def clear(sems):
            nums = sorted(x.num for x in sems)
            cuts = [0] + [i for i in range(1, len(nums)) if nums[i] != nums[i - 1] + 1] + [len(nums)]
            runs = [range(nums[a], nums[b - 1] + 1) for a, b in zip(cuts, cuts[1:])]
            for run in runs[:-1]:
                nc.gpsimd.sem_clear(run)
            nc.all_engine_barrier(sems_to_clear=runs[-1])

        class Phase:

            def __init__(self, names):
                phase_count[0] += 1
                self.stack = ExitStack()
                self.names = names

            def __enter__(self):
                tag = f"_{phase_count[0]}"
                sems = [self.stack.enter_context(nc.semaphore(n + tag)) for n in self.names]
                self.sems = sems
                self.of = dict(zip(self.names, sems))
                self.block = nc.Block(no_gpsimd_drain=True)
                self.blk = self.block.__enter__()
                return self.blk, self.of

            def __exit__(self, *exc):
                self.block.__exit__(*exc)
                clear(self.sems)
                self.stack.close()

        prompt = whole.enter_context(ExitStack())
        bias_prev = sb("bias_prev", [P, HS, WIN], scope=prompt)
        bias_first = sb("bias_first", [P, HS, WIN], scope=prompt)
        bias_cur = sb("bias_cur", [P, HS, WIN], scope=prompt)
        km_hi = sb("km_hi", [P, CH, NMEM], F32R, scope=prompt)
        km_lo = sb("km_lo", [P, CH, NMEM], F32R, scope=prompt)
        vm = sb("vm", [P, 2, CH * P], scope=prompt)
        kbuf = sb("kbuf", [P, WIN + TB], scope=prompt)
        vtok = sb("vtok", [P, 1 + C, P], scope=prompt)
        carry = sb("carry", [P, 8, 3], scope=prompt)
        state = sb("state", [P, HS * HP], scope=prompt)

        with ExitStack() as tmp:
            pvrow = sb("pvrow", [PV_ROWS, P], scope=tmp)
            alog = sb("alog", [P, HS], scope=tmp)
            table = sb("table", [32, HS], scope=tmp)
            onehot = sb("onehot", [32, RLEN], scope=tmp)
            rmask = sb("rmask", [HS, RLEN], scope=tmp)
            rrow = sb("rrow", [HS, RLEN], scope=tmp)
            mem = sb("mem", [P, 2, D], scope=tmp)
            memn = sb("memn", [P, 2, D], scope=tmp)
            mnT = sb("mnT", [P, KT, NMEM], scope=tmp)
            wck_sb = sb("wck_sb", [P, KT, CH * P], scope=tmp)
            wcv_sb = sb("wcv_sb", [P, KT, CH * P], scope=tmp)
            kmT = sb("kmT", [P, CH, NMEM], scope=tmp)
            kmtok = sb("kmtok", [P, 2, CH * P], scope=tmp)
            toep = sb("toep", [P, HS, 2 * WIN], scope=tmp)
            flip = sb("flip", [P, P], scope=tmp)
            with Phase(["par_in", "mem_in", "wck_in", "wcv_in", "bias_in", "rows_out", "made", "consts", "km_hi",
                        "params", "ssq", "normed", "mt", "mtsb", "kps", "kev", "vps", "vev", "ktp", "ktev",
                        "rps", "rsb", "out_done", "bias_done", "flipped"]) as (b, s):
                par = 0

                @b.sync
                def _(sp):
                    loads = [(pvrow[PV_MIX:PV_MIX + 8, :], g_mix[0].rearrange("(t p) -> t p", p=P)),
                             (pvrow[PV_CROSS:PV_CROSS + 8, :], g_cross[0].rearrange("(t p) -> t p", p=P)),
                             (pvrow[PV_FFN:PV_FFN + 8, :], g_ffn[0].rearrange("(t p) -> t p", p=P)),
                             (pvrow[PV_FINAL:PV_FINAL + 8, :], g_final.rearrange("(t p) -> t p", p=P)),
                             (pvrow[PV_MEM:PV_MEM + 8, :], g_mem[0].rearrange("(t p) -> t p", p=P)),
                             (pvrow[PV_CB:PV_CB + 8, :], conv_b[0].rearrange("(t p) -> t p", p=P)),
                             (pvrow[PV_CW:PV_CW + 32, :], conv_w[0].rearrange("k (t p) -> (k t) p", p=P)),
                             (pvrow[PV_SSD:PV_SSD + 4, :], g_ssd_norm[0].rearrange("(t p) -> t p", p=P)),
                             (dtb[:], dt_bias.to_broadcast([P, HS])),
                             (alog[:], a_log.to_broadcast([P, HS])),
                             (dsk[:], d_skip.to_broadcast([P, HS])),
                             (snk[:], sinks.to_broadcast([P, HS])),
                             (wdt[:], w_in[:, COL_DT:COL_DT + HS].rearrange("(k p) n -> p k n", p=P)),
                             (table[:], rel_bias), (onehot[:], bucket_onehot), (rmask[:], row_mask)]
                    assert len(loads) == 16
                    for dst, src in loads:
                        sp.dma_start(dst, src).then_inc(s["par_in"], 16)
                    sp.dma_start(wck_sb[:], w_ck.rearrange("(k p) n -> p k n", p=P)).then_inc(s["wck_in"], 16)
                    sp.dma_start(wcv_sb[:], w_cv.rearrange("(k p) n -> p k n", p=P)).then_inc(s["wcv_in"], 16)
                    sp.wait_ge(s["rsb"], 1)
                    sp.dma_start(bias_rows.ap(), rrow[:]).then_inc(s["rows_out"], 16)
                    sp.wait_ge(s["rows_out"], 16)
                    sp.dma_start(toep[:], bass.AP(tensor=bias_rows, offset=0,
                                                  ap=[[1, P], [RLEN, HS], [1, 2 * WIN]])).then_inc(s["bias_in"], 16)
                    sp.wait_ge(s["vev"], 2)
                    sp.dma_start(p_mem_v[0, 0].rearrange("(c p) h d -> p c (h d)", p=P), vm[:])\
                      .then_inc(s["out_done"], 16)
                    sp.wait_ge(s["ktev"], 2)
                    sp.dma_start(p_mem_k[0, 0].rearrange("(c p) h d -> p c (h d)", p=P), kmtok[:])\
                      .then_inc(s["out_done"], 16)
                    sp.wait_ge(s["out_done"], 32)

                @b.gpsimd
                def _(pool):
                    pool.memset(ones[:], 1.0).then_inc(s["made"], 1)
                    pool.memset(ident[:], 0.0).then_inc(s["made"], 1)
                    pool.memset(flip[:], 0.0).then_inc(s["made"], 1)
                    pool.memset(bias_first[:], NEG)
                    pool.memset(kbuf[:, 0:WIN], 0.0)
                    pool.memset(vtok[:, 0, :], 0.0)
                    pool.memset(carry[:], 0.0)
                    pool.memset(state[:], 0.0)
                    pool.wait_ge(s["made"], 3)
                    pool.affine_select(out=ident[:], in_=ident[:], compare_op=ALU.not_equal, fill=1.0, base=0,
                                       pattern=[[-1, P]], channel_multiplier=1)
                    pool.affine_select(out=flip[:], in_=flip[:], compare_op=ALU.not_equal, fill=1.0, base=1 - P,
                                       pattern=[[1, P]], channel_multiplier=1)
                    pool.affine_select(out=tri_le[:], in_=ones[:], compare_op=ALU.is_ge, fill=0.0, base=0,
                                       pattern=[[1, P]], channel_multiplier=-1)
                    pool.affine_select(out=tri_gt[:], in_=ones[:], compare_op=ALU.is_ge, fill=0.0, base=-1,
                                       pattern=[[-1, P]], channel_multiplier=1).then_inc(s["consts"], 1)
                    pool.wait_ge(s["kev"], CH)
                    pool.tensor_copy(km_hi[:], kmT[:]).then_inc(s["km_hi"], 1)
                    pool.wait_ge(s["km_hi"], 1)
                    pool.tensor_tensor(km_lo[:], kmT[:], km_hi[:].bitcast(F32), ALU.subtract)

                @b.scalar
                def _(act):
                    act.dma_start(mem[:], mem_prompt[0].rearrange("(c p) d -> p c d", p=P)).then_inc(s["mem_in"], 16)
                    act.wait_ge(s["mem_in"], 16)
                    for c in range(2):
                        act.activation(memn[:, c, :], mem[:, c, :], ACT.Square, accum_out=small[:, 0, c:c + 1])\
                           .then_inc(s["ssq"], 1)
                    act.wait_ge(s["par_in"], 256)
                    act.activation(alog[:], alog[:], ACT.Exp).then_inc(s["params"], 1)
                    for i in range(KT):
                        act.wait_ge(s["mt"], i + 1)
                        act.activation(mnT[:, i, :], G[:, i % 2, 0:NMEM], ACT.Copy, scale=g_of(PV_MEM, i))\
                           .then_inc(s["mtsb"], 1)
                    for h in range(CH):
                        act.wait_ge(s["kps"], h + 1)
                        act.activation(kmT[:, h, :], G[:, 2 + h % 2, 0:NMEM], ACT.Copy).then_inc(s["kev"], 1)
                    for c in range(2):
                        act.wait_ge(s["vps"], c + 1)
                        act.activation(vm[:, c, :], G[:, 4 + c, :], ACT.Copy).then_inc(s["vev"], 1)

                @b.vector
                def _(dve):
                    dve.wait_ge(s["par_in"], 256)
                    dve.tensor_copy(wdt_h[:], wdt[:])
                    dve.drain()
                    dve.tensor_tensor(wdt_l[:], wdt[:], wdt_h[:].bitcast(F32), ALU.subtract)
                    dve.wait_ge(s["params"], 1)
                    dve.tensor_scalar(nega[:], alog[:], -1.0, None, ALU.mult)
                    dve.wait_ge(s["rps"], 1)
                    dve.tensor_tensor(rrow[:], L[0:HS, 0, 0:RLEN], rmask[:], ALU.add).then_inc(s["rsb"], 1)
                    dve.wait_ge(s["rps"], 2)
                    dve.tensor_copy(pv[:], L[:, 1, 0:PV_ROWS]).then_inc(s["rsb"], 1)
                    dve.wait_ge(s["ssq"], 2)
                    v, r, t = small[:, 1, 0:2], small[:, 2, 0:2], small[:, 3, 0:2]
                    dve.tensor_scalar(v, small[:, 0, 0:2], 1.0 / D, EPS, ALU.mult, ALU.add)
                    dve.drain()
                    rsqrt(dve, v, r, t)
                    for c in range(2):
                        dve.tensor_scalar(memn[:, c, :], mem[:, c, :], r[:, c:c + 1], None, ALU.mult)\
                           .then_inc(s["normed"], 1)
                    for c in range(2):
                        dve.wait_ge(s["ktp"], c + 1)
                        dve.tensor_copy(kmtok[:, c, :], L[:, c, :]).then_inc(s["ktev"], 1)
                    for n in range(4):
                        dve.wait_ge(s["flipped"], n + 1)
                        src = G[:, n % 2, :].rearrange("p (h k) -> p h k", h=2)
                        dve.tensor_copy(bias_prev[:, 2 * n:2 * n + 2, :], src[:, :, 0:WIN])
                        dve.tensor_copy(bias_cur[:, 2 * n:2 * n + 2, :], src[:, :, WIN:2 * WIN])\
                           .then_inc(s["bias_done"], 1)

                @b.tensor
                def _(pe):
                    pe.wait_ge(s["par_in"], 256)
                    pe.wait_ge(s["consts"], 1)
                    pe.matmul(L[0:HS, 0, 0:RLEN], table[:], onehot[:], start=True, stop=True)\
                      .then_inc(s["rps"], 1)
                    pe.transpose(L[:, 1, 0:PV_ROWS], pvrow[:], ident[0:PV_ROWS, 0:PV_ROWS]).then_inc(s["rps"], 1)
                    pe.wait_ge(s["normed"], 2)
                    pe.wait_ge(s["rsb"], 2)
                    for i in range(KT):
                        if i >= 2:
                            pe.wait_ge(s["mtsb"], i - 1)
                        for c in range(2):
                            last = pe.transpose(G[:, i % 2, c * P:c * P + P], memn[:, c, i * P:i * P + P], ident[:])
                        last.then_inc(s["mt"], 1)
                    pe.wait_ge(s["mtsb"], KT)
                    pe.wait_ge(s["wck_in"], 16)
                    for h in range(CH):
                        if h >= 2:
                            pe.wait_ge(s["kev"], h - 1)
                        for k in range(KT):
                            last = pe.matmul(G[:, 2 + h % 2, 0:NMEM], wck_sb[:, k, h * P:h * P + P], mnT[:, k, :],
                                             start=(k == 0), stop=(k == KT - 1))
                        last.then_inc(s["kps"], 1)
                    pe.wait_ge(s["wcv_in"], 16)
                    for c in range(2):
                        for k in range(KT):
                            last = pe.matmul(G[:, 4 + c, :], mnT[:, k, c * P:c * P + P], wcv_sb[:, k, :],
                                             start=(k == 0), stop=(k == KT - 1))
                        last.then_inc(s["vps"], 1)
                    pe.wait_ge(s["kev"], CH)
                    for c in range(2):
                        for h in range(CH):
                            last = pe.transpose(L[:, c, h * P:h * P + P], kmT[:, h, c * P:c * P + P], ident[:])
                        last.then_inc(s["ktp"], 1)
                    pe.wait_ge(s["bias_in"], 16)
                    for n in range(4):
                        if n >= 2:
                            pe.wait_ge(s["bias_done"], n - 1)
                        pe.matmul(G[:, n % 2, :], flip[:], toep[:, 2 * n:2 * n + 2, :], start=True, stop=True)\
                          .then_inc(s["flipped"], 1)

        with nc.Fori(0, NBLK) as blk, ExitStack() as body:
            hT = sb("hT", [P, KT, TB], scope=body)
            xh = sb("xh", [P, KT, TB], F32R, scope=body)
            xl = sb("xl", [P, KT, TB], F32R, scope=body)
            w_raw = sb("w_raw", [P, RING, D], scope=body)
            w_hi = sb("w_hi", [P, RING, D], F32R, scope=body)
            w_lo = sb("w_lo", [P, RING, D], F32R, scope=body)
            ntmp = sb("ntmp", [P, 2, TB], scope=body)
            sq = sb("sq", [P, 2, TB], scope=body)
            sqsum = sb("sqsum", [P, TB], scope=body)

            stream_names = [f"w_in_slot{r}" for r in range(RING)] + ["hi_ready", "lo_ready", "lin_out"]
            stream = {n: body.enter_context(nc.semaphore(n)) for n in stream_names}

            def load_panels(sp, a, z):
                for n in range(a, min(z, NPAN)):
                    if n >= RING:
                        sp.wait_ge(stream["lo_ready"], n - RING + 1)
                    for dst, src in panel_slices(w_raw[:, n % RING, :], panels[n][0]):
                        sp.dma_start(dst, src).then_inc(stream[f"w_in_slot{n % RING}"], 16)

            def panel_width(n):
                return panels[n][1] * panels[n][2] * P

            def round_panel(act, n):
                if n >= NPAN:
                    return
                act.wait_ge(stream[f"w_in_slot{n % RING}"], 16 * first_dma[n])
                if n >= RING:
                    act.wait_ge(stream["lin_out"], first_out[n - RING + 1])
                w = panel_width(n)
                act.activation(w_hi[:, n % RING, 0:w], w_raw[:, n % RING, 0:w], ACT.Copy)\
                   .then_inc(stream["hi_ready"], 1)

            def rest_panels(pool, a, z):
                for n in range(a, min(z, NPAN)):
                    pool.wait_ge(stream["hi_ready"], n + 1)
                    w = panel_width(n)
                    pool.tensor_tensor(w_lo[:, n % RING, 0:w], w_raw[:, n % RING, 0:w],
                                       w_hi[:, n % RING, 0:w].bitcast(F32), ALU.subtract)\
                        .then_inc(stream["lo_ready"], 1)

            def multiply_panel(pe, n, rh, rl, each_k=None, free=None):
                pe.wait_ge(stream["lo_ready"], n + 1)
                kn, outs = panels[n][1], panels[n][2]
                for m in range(outs):
                    o = first_out[n] + m
                    if free:
                        free(o)
                    bank = L[:, o % 2, :]
                    for k in range(kn):
                        if each_k:
                            each_k(k)
                        c0 = (k * outs + m) * P
                        wh = w_hi[:, n % RING, c0:c0 + P]
                        wl = w_lo[:, n % RING, c0:c0 + P]
                        pe.matmul(bank, wh, rh[:, k, :], start=(k == 0), stop=False)
                        pe.matmul(bank, wl, rh[:, k, :], start=False, stop=False)
                        last = pe.matmul(bank, wh, rl[:, k, :], start=False, stop=(k == kn - 1))
                    last.then_inc(stream["lin_out"], 1)

            def norm_rows_dve(dve, s, tag, sums, n=C):
                v, r, t = small[:, 1, 0:n], small[:, 2, 0:n], small[:, 3, 0:n]
                dve.tensor_scalar(v, sums, 1.0 / D, EPS, ALU.mult, ALU.add)
                dve.drain()
                rsqrt(dve, v, r, t)
                for c in range(n):
                    last = dve.tensor_scalar(diag[:, c * P:c * P + P], ident[:], r[:, c:c + 1], None, ALU.mult)
                last.then_inc(s[tag + "diag"], 1)

            def norm_rows_pe(pe, s, tag):
                pe.wait_ge(s[tag + "diag"], 1)
                pe.matmul(G[:, 4, :], ones[:], diag[:], start=True, stop=True).then_inc(s[tag + "rb"], 1)

            RB = diag[:]

            def norm_row_back_dve(dve, s, tag):
                dve.wait_ge(s[tag + "rb"], 1)
                dve.tensor_copy(RB, G[:, 4, :])
                dve.drain()

            def norm_split_dve(dve, s, tag, row):
                def rest(i):
                    dve.wait_ge(s[tag + "xh"], i + 1)
                    dve.tensor_tensor(xl[:, i, :], ntmp[:, i % 2, :], xh[:, i, :].bitcast(F32), ALU.subtract)\
                       .then_inc(s[tag + "xl"], 1)

                for i in range(KT):
                    if i >= 2:
                        dve.wait_ge(s[tag + "xl"], i - 1)
                    dve.tensor_scalar(ntmp[:, i % 2, :], hT[:, i, :], g_of(row, i), None, ALU.mult)\
                       .then_inc(s[tag + "nt"], 1)
                    if i >= 1:
                        rest(i - 1)
                rest(KT - 1)

            def norm_split_act(act, s, tag):
                for i in range(KT):
                    act.wait_ge(s[tag + "nt"], i + 1)
                    act.activation(xh[:, i, :], ntmp[:, i % 2, :], ACT.Copy).then_inc(s[tag + "xh"], 1)

            def residual_dve(dve, s, tag, o0, n, square):
                dve.wait_ge(stream["lin_out"], o0 + n + 1)
                dve.tensor_tensor(hT[:, n, :], L[:, (o0 + n) % 2, :], hT[:, n, :], ALU.add)\
                   .then_inc(s[tag + "h"], 1)
                if square and n >= 1:
                    sum_squares_dve(dve, s, tag, n - 1)

            def sum_squares_dve(dve, s, tag, n):
                dve.wait_ge(s[tag + "sq"], n + 1)
                if n == 0:
                    ins = dve.tensor_copy(sqsum[:], sq[:, 0, :])
                else:
                    dve.wait_ge(s[tag + "sqs"], n)
                    ins = dve.tensor_tensor(sqsum[:], sqsum[:], sq[:, n % 2, :], ALU.add)
                ins.then_inc(s[tag + "sqs"], 1)

            def square_act(act, s, tag, n, done=None):
                act.wait_ge(s[tag + "h"], (n if done is None else done) + 1)
                if n >= 2:
                    act.wait_ge(s[tag + "sqs"], n - 1)
                act.activation(sq[:, n % 2, :], hT[:, n, :], ACT.Square).then_inc(s[tag + "sq"], 1)

            def token_sums_pe(pe, s, tag, wait=True):
                if wait:
                    pe.wait_ge(s[tag + "sqs"], KT)
                for c in range(C):
                    last = pe.matmul(G[:, 5, c:c + 1], sqsum[:, c * P:c * P + P], ones[:, 0:1],
                                     start=True, stop=True)
                last.then_inc(s[tag + "tok"], 1)

            NORM = ["diag", "rb", "nt", "xh", "xl"]
            RESID = ["h", "sq", "sqs", "tok"]

            mixer = ExitStack()
            xbc = sb("xbc", [P, 8, TB], scope=mixer)
            zs = sb("zs", [P, 4, TB], scope=mixer)
            qT = sb("qT", [P, QJ, TB], scope=mixer)
            vT = sb("vT", [P, TB], scope=mixer)

            with ExitStack() as tmp:
                xin = sb("xin", [P, C, D], scope=tmp)
                raw = sb("raw", [P, 2, 3 + TB], scope=tmp)
                cacc = sb("cacc", [P, 2, TB], scope=tmp)
                junk1 = sb("junk1", [P, D], scope=tmp)
                with Phase([f"x_in{c}" for c in range(C)] + ["xt", "hev", "ssq", "lin_free", "raw_ready",
                            "conv_done", "silu_done"] + ["n1" + n for n in NORM]) as (b, s):

                    @b.sync
                    def _(sp):
                        for c in range(C):
                            sp.dma_start(xin[:, c, :], x_prompt[0, bass.ds(blk * TB + c * P, P), :])\
                              .then_inc(s[f"x_in{c}"], 16)
                        load_panels(sp, 0, PAN_OUT + RING)

                    @b.gpsimd
                    def _(pool):
                        rest_panels(pool, 0, PAN_OUT + AHEAD)

                    @b.scalar
                    def _(act):
                        for c in range(C):
                            act.wait_ge(s[f"x_in{c}"], 16)
                            act.activation(junk1[:], xin[:, c, :], ACT.Square, accum_out=small[:, 0, c:c + 1])\
                               .then_inc(s["ssq"], 1)
                            act.drain()
                        for n in range(AHEAD):
                            round_panel(act, n)
                        norm_split_act(act, s, "n1")

                        def silu(i):
                            act.wait_ge(s["conv_done"], i + 1)
                            act.activation(xbc[:, i, :], cacc[:, i % 2, :], ACT.Silu).then_inc(s["silu_done"], 1)

                        def silu_z(i):
                            act.wait_ge(s["lin_free"], PAN_Z + i + 1)
                            act.activation(zs[:, i, :], zs[:, i, :], ACT.Silu)

                        for o in range(PAN_OUT):
                            round_panel(act, o + AHEAD)
                            if 1 <= o <= PAN_K:
                                silu(o - 1)
                            elif o > PAN_Z:
                                silu_z(o - 1 - PAN_Z)
                        silu_z(3)

                    @b.vector
                    def _(dve):
                        for c in range(C):
                            dve.wait_ge(s["xt"], c + 1)
                            g0 = 2 * (c % 2)
                            dve.tensor_copy(hT[:, :, c * P:c * P + P],
                                            G[:, g0:g0 + 2, :].rearrange("p a (i t) -> p (a i) t", t=P))\
                               .then_inc(s["hev"], 1)
                        dve.wait_ge(s["hev"], C)
                        norm_split_dve(dve, s, "n1", PV_MIX)
                        dve.wait_ge(s["ssq"], C)
                        norm_rows_dve(dve, s, "n1", small[:, 0, 0:C])
                        norm_row_back_dve(dve, s, "n1")
                        for i in range(8):
                            sl = i % 2
                            if i >= 2:
                                dve.wait_ge(s["silu_done"], i - 1)
                                dve.wait_ge(s["conv_done"], i - 1)
                            dve.tensor_copy(raw[:, sl, 0:3], carry[:, i, :])
                            dve.wait_ge(stream["lin_out"], i + 1)
                            dve.tensor_tensor(raw[:, sl, 3:3 + TB], L[:, sl, :], RB, ALU.mult)\
                               .then_inc(s["lin_free"], 1)
                            dve.drain()
                            dve.tensor_scalar(cacc[:, sl, :], raw[:, sl, 0:TB], g_of(PV_CW, i), g_of(PV_CB, i),
                                              ALU.mult, ALU.add)
                            for k in range(1, 4):
                                dve.drain()
                                last = dve.scalar_tensor_tensor(cacc[:, sl, :], raw[:, sl, k:k + TB],
                                                                g_of(PV_CW + 8 * k, i), cacc[:, sl, :],
                                                                ALU.mult, ALU.add)
                                if k == 2:
                                    dve.tensor_copy(carry[:, i, :], raw[:, sl, TB:TB + 3])
                            last.then_inc(s["conv_done"], 1)
                        for o in range(PAN_K, PAN_OUT):
                            dve.wait_ge(stream["lin_out"], o + 1)
                            if o == PAN_K:
                                dst, scale = kbuf[:, WIN:WIN + TB], 1.0
                            elif o == PAN_V:
                                dst, scale = vT[:], 1.0
                            elif o < PAN_Z:
                                dst, scale = qT[:, o - PAN_Q, :], 64 ** -0.5
                            else:
                                dst, scale = zs[:, o - PAN_Z, :], 1.0
                            dve.scalar_tensor_tensor(dst, L[:, o % 2, :], scale, RB, ALU.mult, ALU.mult)\
                               .then_inc(s["lin_free"], 1)

                    @b.tensor
                    def _(pe):
                        for c in range(C):
                            pe.wait_ge(s[f"x_in{c}"], 16)
                            if c >= 2:
                                pe.wait_ge(s["hev"], c - 1)
                            for i in range(KT):
                                g = 2 * (c % 2) + i // 4
                                last = pe.transpose(G[:, g, (i % 4) * P:(i % 4) * P + P],
                                                    xin[:, c, i * P:i * P + P], ident[:])
                            last.then_inc(s["xt"], 1)
                        for n in range(PAN_OUT):
                            if n == 2:
                                norm_rows_pe(pe, s, "n1")
                            multiply_panel(
                                pe, n, xh, xl,
                                each_k=(lambda k: pe.wait_ge(s["n1xl"], k + 1)) if n == 0 else None,
                                free=(lambda o: pe.wait_ge(s["lin_free"], o - 1)) if n >= 2 else None)
                        for c in range(C):
                            for k in range(KT):
                                lh = xh[:, k, c * P:c * P + P]
                                ll = xl[:, k, c * P:c * P + P]
                                o = G[:, 5, c * HS:c * HS + HS]
                                pe.matmul(o, lh, wdt_h[:, k, :], start=(k == 0), stop=False)
                                pe.matmul(o, lh, wdt_l[:, k, :], start=False, stop=False)
                                pe.matmul(o, ll, wdt_h[:, k, :], start=False, stop=(k == KT - 1))

            with ExitStack() as tmp:
                ymix = sb("ymix", [P, C, D], scope=tmp)
                CHN = C * HS
                dts = sb("dts", [P, 8, CHN], scope=tmp)
                dt, da = dts[:, 0, :], dts[:, 1, :]
                ex = sb("ex", [P, 3 * CHN], scope=tmp)
                rda = sb("rda", [P, HS * P], scope=tmp)
                E = sb("E", [P, HS * P], scope=tmp)
                M = E
                cbm, btok = sqsum[:, 0:2 * P], sqsum[:, 2 * P:4 * P]
                xdt = sb("xdt", [P, 512], scope=tmp)
                xdd = sb("xdd", [P, 512], scope=tmp)
                yD = sb("yD", [P, 512], scope=tmp)
                yac = sb("yac", [P, 512], scope=tmp)
                ssg = sb("ssg", [P, 5, 8], scope=tmp)
                junk2 = sq[:, 0, 0:256]
                SC = sb("SC", [P, 2, 4, 256], scope=tmp)
                PT = rda
                sm = sb("sm", [P, 3, 8, 4], scope=tmp)
                NU = 2 * C

                def heads(ap, w):
                    return ap.unsqueeze(2).to_broadcast([P, ap.shape[1], w])

                def bank(i):
                    return G[:, i, :] if i < 6 else L[:, i - 6, :]

                with Phase(["dtr", "dte", "dtu", "dtl", "da", "cum", "ex", "rda", "xtok", "btok", "cb", "ztok",
                            "diff", "E", "yoff", "xdd", "st", "M", "yd", "ssd_done", "ssum", "ynorm",
                            "vps", "vev", "scores", "s_free", "nmax", "prob", "pt", "ptsb", "pv", "att",
                            "mixt", "mixh", "mixl", "qk_hi", "qk_split"]) as (b, s):
                    q_hi, q_lo = xh[:, 0:QJ, :], xl[:, 0:QJ, :]
                    k_hi = xh[:, QJ:QJ + 2, :].rearrange("p a n -> p (a n)")[:, 0:WIN + TB]
                    k_lo = xl[:, QJ:QJ + 2, :].rearrange("p a n -> p (a n)")[:, 0:WIN + TB]

                    @b.gpsimd
                    def _(pool):
                        pool.tensor_copy(k_hi, kbuf[:]).then_inc(s["qk_hi"], 1)
                        pool.tensor_copy(q_hi, qT[:]).then_inc(s["qk_hi"], 1)
                        pool.wait_ge(s["qk_hi"], 2)
                        pool.tensor_tensor(k_lo, kbuf[:], k_hi.bitcast(F32), ALU.subtract).then_inc(s["qk_split"], 1)
                        pool.tensor_tensor(q_lo, qT[:], q_hi.bitcast(F32), ALU.subtract).then_inc(s["qk_split"], 1)

                    @b.scalar
                    def _(act):
                        act.wait_ge(s["vps"], 1)
                        act.activation(vtok[:, 1:1 + C, :], bank(7).rearrange("p (c t) -> p c t", t=P), ACT.Copy)\
                           .then_inc(s["vev"], 1)
                        act.wait_ge(s["dtr"], 1)
                        act.activation(dts[:, 3, :], dts[:, 2, :], ACT.Exp).then_inc(s["dte"], 1)
                        act.wait_ge(s["dtu"], 1)
                        act.activation(dts[:, 5, :], dts[:, 4, :], ACT.Ln).then_inc(s["dtl"], 1)
                        act.wait_ge(s["cum"], 1)
                        act.activation(ex[:], bank(4)[:, 0:3 * CHN], ACT.Exp).then_inc(s["ex"], 1)

                        def group_squares(c):
                            act.wait_ge(s["ssd_done"], c + 1)
                            for g in range(2):
                                act.activation(junk2, ymix[:, c, g * 256:g * 256 + 256], ACT.Square,
                                               accum_out=ssg[:, 0, 2 * c + g:2 * c + g + 1]).then_inc(s["ssum"], 1)
                                act.drain()

                        for c in range(C):
                            act.wait_ge(s["xtok"], c + 1)
                            act.activation(btok, bank(1)[:, 0:256], ACT.Copy).then_inc(s["btok"], 1)
                            for g in range(2):
                                act.wait_ge(s["diff"], 2 * c + g + 1)
                                act.activation(E[:, g * 512:g * 512 + 512], bank(2 + g), ACT.Exp)\
                                   .then_inc(s["E"], 1)
                            if c >= 1:
                                group_squares(c - 1)
                        group_squares(C - 1)

                        def transposed(u):
                            act.wait_ge(s["pt"], u + 1)
                            if u >= 1:
                                act.wait_ge(s["pv"], u)
                            act.activation(PT[:], G[:, 2:4, :], ACT.Copy).then_inc(s["ptsb"], 1)

                        for u in range(NU):
                            act.wait_ge(s["nmax"], u + 1)
                            for a in range(4):
                                act.activation(SC[:, u % 2, a, :], SC[:, u % 2, a, :], ACT.Exp,
                                               bias=sm[:, u % 3, 2, a:a + 1],
                                               accum_out=sm[:, u % 3, 4, a:a + 1])
                            act.activation(sm[:, u % 3, 5, :], sm[:, u % 3, 3, :], ACT.Exp).then_inc(s["prob"], 1)
                            if u >= 1:
                                transposed(u - 1)
                        transposed(NU - 1)
                        for i in range(KT):
                            act.wait_ge(s["mixt"], i + 1)
                            scale = g_of(PV_SSD, i) if i < 4 else 1.0
                            act.activation(xh[:, i, :], bank(6 + i % 2), ACT.Copy, scale=scale)\
                               .then_inc(s["mixh"], 1)

                    @b.vector
                    def _(dve):
                        d, na, e, u, ln, q, r = (dts[:, i, :] for i in (1, 2, 3, 4, 5, 6, 7))
                        dch = d.rearrange("p (c h) -> p c h", h=HS)
                        dve.tensor_tensor(dch, bank(5)[:, 0:CHN].rearrange("p (c h) -> p c h", h=HS),
                                          small[:, 2, 0:C].unsqueeze(2).to_broadcast([P, C, HS]), ALU.mult)
                        dve.drain()
                        dve.tensor_tensor(dch, dch,
                                          dtb[:].unsqueeze(1).to_broadcast([P, C, HS]), ALU.add)
                        dve.drain()
                        dve.scalar_tensor_tensor(na, d, -1.0, d, ALU.mult, ALU.min).then_inc(s["dtr"], 1)
                        dve.wait_ge(s["dte"], 1)
                        dve.tensor_scalar(u, e, 1.0, None, ALU.add).then_inc(s["dtu"], 1)
                        dve.wait_ge(s["dtu"], 1)
                        dve.tensor_scalar(q, u, -1.0, None, ALU.add)
                        dve.drain()
                        dve.tensor_scalar(r, q, 1e-30, None, ALU.max)
                        dve.drain()
                        dve.reciprocal(r, r)
                        dve.tensor_scalar(q, q, 0.0, None, ALU.is_equal)
                        dve.wait_ge(s["dtl"], 1)
                        dve.drain()
                        dve.tensor_tensor(r, r, ln, ALU.mult)
                        dve.drain()
                        dve.tensor_tensor(r, r, q, ALU.add)
                        dve.drain()
                        dve.tensor_tensor(r, r, e, ALU.mult)
                        dve.drain()
                        dve.scalar_tensor_tensor(dt, d, 0.0, r, ALU.max, ALU.add)
                        dve.drain()
                        dve.tensor_tensor(da.rearrange("p (c h) -> p c h", h=HS),
                                          dt.rearrange("p (c h) -> p c h", h=HS),
                                          nega[:].unsqueeze(1).to_broadcast([P, C, HS]), ALU.mult)\
                           .then_inc(s["da"], 1)
                        dve.wait_ge(s["da"], 1)
                        v3 = lambda t: t.rearrange("p (h w) -> p h w", h=HS)

                        def decay_factor(c):
                            if c >= 1:
                                dve.wait_ge(s["diff"], 2 * c)
                            dve.tensor_tensor(v3(rda[:]), tri_le[:].unsqueeze(1).to_broadcast([P, HS, P]),
                                              heads(da[:, c * HS:c * HS + HS], P), ALU.mult).then_inc(s["rda"], 1)

                        decay_factor(0)
                        for c in range(C):
                            hc = slice(c * HS, c * HS + HS)
                            dve.wait_ge(s["xtok"], c + 1)
                            if c == 0:
                                dve.wait_ge(s["ex"], 1)
                            dve.tensor_tensor(v3(xdt[:]), v3(bank(0)), heads(dt[:, hc], HP), ALU.mult)
                            if c >= 1:
                                dve.wait_ge(s["ssd_done"], c)
                            dve.tensor_tensor(v3(yD[:]), v3(bank(0)), heads(dsk[:], HP), ALU.mult)
                            dve.drain()
                            dve.tensor_tensor(v3(xdd[:]), v3(xdt[:]),
                                              heads(ex[:, CHN + c * HS:CHN + c * HS + HS], HP), ALU.mult)\
                               .then_inc(s["xdd"], 1)
                            dve.wait_ge(s["cb"], c + 1)
                            dve.tensor_tensor(cbm.rearrange("p (g q) -> p g q", g=2),
                                              bank(1)[:, 256:512].rearrange("p (g q) -> p g q", g=2),
                                              tri_le[:].unsqueeze(1).to_broadcast([P, 2, P]), ALU.mult)
                            dve.drain()
                            for g in range(2):
                                dve.wait_ge(s["E"], 2 * c + g + 1)
                                last = dve.tensor_tensor(
                                    M[:, g * 512:g * 512 + 512].rearrange("p (h q) -> p h q", h=4),
                                    E[:, g * 512:g * 512 + 512].rearrange("p (h q) -> p h q", h=4),
                                    cbm[:, g * P:g * P + P].unsqueeze(1).to_broadcast([P, 4, P]), ALU.mult)
                            last.then_inc(s["M"], 1)
                            if c + 1 < C:
                                decay_factor(c + 1)
                            dve.wait_ge(s["yoff"], c + 1)
                            dve.tensor_tensor(v3(yac[:]), v3(bank(5)), heads(ex[:, hc], HP), ALU.mult)
                            dve.drain()
                            dve.tensor_tensor(yac[:], yac[:], yD[:], ALU.add)
                            dve.wait_ge(s["st"], c + 1)
                            dve.tensor_tensor(v3(state[:]), v3(state[:]),
                                              heads(ex[:, 2 * CHN + c * HS:2 * CHN + c * HS + HS], HP), ALU.mult)
                            dve.drain()
                            dve.tensor_tensor(state[:], state[:], bank(6), ALU.add)
                            dve.wait_ge(s["yd"], c + 1)
                            dve.tensor_tensor(yac[:], yac[:], bank(4), ALU.add)
                            dve.drain()
                            dve.wait_ge(s["ztok"], c + 1)
                            dve.tensor_tensor(ymix[:, c, 0:512], yac[:], bank(7), ALU.mult)\
                               .then_inc(s["ssd_done"], 1)
                        def group_norm():
                            dve.wait_ge(s["ssum"], 2 * C)
                            dve.tensor_scalar(ssg[:, 1, :], ssg[:, 0, :], 1.0 / 256, EPS, ALU.mult, ALU.add)
                            dve.drain()
                            rsqrt(dve, ssg[:, 1, :], ssg[:, 2, :], ssg[:, 3, :])
                            for c in range(C):
                                yv = ymix[:, c, 0:512].rearrange("p (g w) -> p g w", g=2)
                                last = dve.tensor_tensor(yv, yv, heads(ssg[:, 2, 2 * c:2 * c + 2], 256), ALU.mult)
                            last.then_inc(s["ynorm"], 1)

                        def finish(u):
                            c, jp = u // 2, u % 2
                            st = sm[:, u % 3]
                            dve.wait_ge(s["prob"], u + 1)
                            dve.tensor_tensor(st[:, 6, :], st[:, 4, :], st[:, 5, :], ALU.add)
                            dve.drain()
                            dve.reciprocal(st[:, 7, :], st[:, 6, :])
                            dve.drain()
                            dve.wait_ge(s["pv"], u + 1)
                            o = ymix[:, c, 512 + jp * 256:512 + jp * 256 + 256]
                            dve.tensor_tensor(o.rearrange("p (j v d) -> p j v d", j=2, v=KV),
                                              bank(4)[:, 0:256].rearrange("p (j v d) -> p j v d", j=2, v=KV),
                                              st[:, 7, :].rearrange("p (v j) -> p j v", v=KV).unsqueeze(3)
                                              .to_broadcast([P, 2, KV, 64]), ALU.mult).then_inc(s["att"], 1)

                        for u in range(NU):
                            c, jp = u // 2, u % 2
                            st = sm[:, u % 3]
                            sc = SC[:, u % 2].rearrange("p (v j) k -> p v j k", v=KV)
                            ps = (L if u % 2 else G)[:, 0:2, :].rearrange("p v (j k) -> p v j k", j=2)
                            hj = slice(2 * jp, 2 * jp + 2)
                            dve.wait_ge(s["scores"], u + 1)
                            if u >= 2:
                                dve.wait_ge(s["pt"], u - 1)
                            for half, bias in ((0, bias_first if c == 0 else bias_prev), (1, bias_cur)):
                                ks = slice(half * WIN, half * WIN + WIN)
                                bv = bias[:].rearrange("p (v j) k -> p v j k", v=KV)
                                for v in range(KV):
                                    last = dve.tensor_tensor(sc[:, v, :, ks], ps[:, v, :, ks], bv[:, v, hj, :],
                                                             ALU.add)
                            last.then_inc(s["s_free"], 1)
                            dve.wait_ge(s["s_free"], u + 1)
                            dve.tensor_reduce(st[:, 0, :], SC[:, u % 2], AX_X, ALU.max)
                            dve.drain()
                            snk_u = snk[:].rearrange("p (v j) -> p v j", v=KV)[:, :, hj]
                            vj = lambda t: t.rearrange("p (v j) -> p v j", v=KV)
                            dve.tensor_tensor(vj(st[:, 1, :]), vj(st[:, 0, :]), snk_u, ALU.max)
                            dve.drain()
                            dve.tensor_scalar(st[:, 2, :], st[:, 1, :], -1.0, None, ALU.mult)
                            dve.tensor_tensor(vj(st[:, 3, :]), snk_u, vj(st[:, 1, :]), ALU.subtract)\
                               .then_inc(s["nmax"], 1)
                            if u == 1:
                                group_norm()
                            if u >= 2:
                                finish(u - 2)
                        finish(NU - 2)
                        finish(NU - 1)
                        dve.tensor_copy(kbuf[:, 0:WIN], kbuf[:, TB:TB + WIN])
                        dve.tensor_copy(vtok[:, 0, :], vtok[:, C, :])
                        dve.tensor_copy(bias_first[:], bias_prev[:])
                        for i in range(KT):
                            dve.wait_ge(s["mixh"], i + 1)
                            src, hi = bank(6 + i % 2), xh[:, i, :].bitcast(F32)
                            if i < 4:
                                ins = dve.scalar_tensor_tensor(xl[:, i, :], src, g_of(PV_SSD, i), hi,
                                                               ALU.mult, ALU.subtract)
                            else:
                                ins = dve.tensor_tensor(xl[:, i, :], src, hi, ALU.subtract)
                            ins.then_inc(s["mixl"], 1)

                    @b.tensor
                    def _(pe):
                        for c in range(C):
                            last = pe.transpose(bank(7)[:, c * P:c * P + P], vT[:, c * P:c * P + P], ident[:])
                        last.then_inc(s["vps"], 1)
                        pe.wait_ge(s["da"], 1)
                        for i, left in enumerate((tri_le, tri_gt, ones)):
                            last = pe.matmul(bank(4)[:, i * CHN:(i + 1) * CHN], left[:], da, start=True, stop=True)
                        last.then_inc(s["cum"], 1)
                        pe.wait_ge(s["vev"], 1)
                        for c in range(C):
                            t = slice(c * P, c * P + P)
                            if c >= 1:
                                pe.wait_ge(s["M"], c)
                            for i in range(4):
                                pe.transpose(bank(0)[:, i * P:i * P + P], xbc[:, i, t], ident[:])
                            for g in range(2):
                                last = pe.transpose(bank(1)[:, g * P:g * P + P], xbc[:, 4 + g, t], ident[:])
                            last.then_inc(s["xtok"], 1)
                            pe.wait_ge(s["rda"], c + 1)
                            for g in range(2):
                                pe.matmul(bank(2 + g), tri_gt[:], rda[:, g * 512:g * 512 + 512],
                                          start=True, stop=True).then_inc(s["diff"], 1)
                            if c >= 1:
                                pe.wait_ge(s["ssd_done"], c)
                            for g in range(2):
                                last = pe.matmul(bank(5)[:, g * 256:g * 256 + 256], xbc[:, 6 + g, t],
                                                 state[:, g * 256:g * 256 + 256], start=True, stop=True)
                            last.then_inc(s["yoff"], 1)
                            pe.wait_ge(s["btok"], c + 1)
                            for g in range(2):
                                last = pe.matmul(bank(1)[:, 256 + g * P:256 + g * P + P], xbc[:, 4 + g, t],
                                                 xbc[:, 6 + g, t], start=True, stop=True)
                            last.then_inc(s["cb"], 1)
                            pe.wait_ge(s["xdd"], c + 1)
                            for g in range(2):
                                last = pe.matmul(bank(6)[:, g * 256:g * 256 + 256], btok[:, g * P:g * P + P],
                                                 xdd[:, g * 256:g * 256 + 256], start=True, stop=True)
                            last.then_inc(s["st"], 1)
                            for i in range(4):
                                last = pe.transpose(bank(7)[:, i * P:i * P + P], zs[:, i, t], ident[:])
                            last.then_inc(s["ztok"], 1)
                            if c == 0:
                                pe.wait_ge(s["ex"], 1)
                            pe.wait_ge(s["M"], c + 1)
                            for h in range(HS):
                                last = pe.matmul(bank(4)[:, h * HP:h * HP + HP], M[:, h * P:h * P + P],
                                                 xdt[:, h * HP:h * HP + HP], start=True, stop=True)
                            last.then_inc(s["yd"], 1)

                        def scores(u):
                            c, jp = u // 2, u % 2
                            if u >= 2:
                                pe.wait_ge(s["s_free"], u - 1)
                            for v in range(KV):
                                for jj in range(2):
                                    r = slice(64 * v, 64 * v + 64)
                                    o = (L if u % 2 else G)[:, v, jj * 256:jj * 256 + 256]
                                    qh = q_hi[r, 2 * jp + jj, c * P:c * P + P]
                                    ql = q_lo[r, 2 * jp + jj, c * P:c * P + P]
                                    kh, kl = k_hi[r, c * P:c * P + 256], k_lo[r, c * P:c * P + 256]
                                    pe.matmul(o, qh, kh, start=True, stop=False)
                                    pe.matmul(o, qh, kl, start=False, stop=False)
                                    last = pe.matmul(o, ql, kh, start=False, stop=True)
                            last.then_inc(s["scores"], 1)

                        def weigh(u):
                            c = u // 2
                            pe.wait_ge(s["prob"], u + 1)
                            if u >= 1:
                                pe.wait_ge(s["ptsb"], u)
                            for a in range(4):
                                for half in range(2):
                                    i = 2 * a + half
                                    last = pe.transpose(G[:, 2 + i // 4, (i % 4) * P:(i % 4) * P + P],
                                                        SC[:, u % 2, a, half * P:half * P + P], ident[:])
                            last.then_inc(s["pt"], 1)

                        def values(u):
                            c = u // 2
                            pe.wait_ge(s["ptsb"], u + 1)
                            if u >= 1:
                                pe.wait_ge(s["att"], u)
                            for a in range(4):
                                v, jj = a // 2, a % 2
                                for half in range(2):
                                    i = 2 * a + half
                                    last = pe.matmul(bank(4)[:, jj * P + v * 64:jj * P + v * 64 + 64],
                                                     PT[:, i * P:i * P + P], vtok[:, c + half, v * 64:v * 64 + 64],
                                                     start=(half == 0), stop=(half == 1))
                            last.then_inc(s["pv"], 1)

                        pe.wait_ge(s["qk_split"], 2)
                        scores(0)
                        pe.wait_ge(s["ssd_done"], C)
                        for u in range(NU):
                            if u + 1 < NU:
                                scores(u + 1)
                            weigh(u)
                            if u >= 1:
                                values(u - 1)
                        values(NU - 1)
                        pe.wait_ge(s["ynorm"], 1)
                        pe.wait_ge(s["att"], NU)
                        for i in range(KT):
                            if i >= 2:
                                pe.wait_ge(s["mixl"], i - 1)
                            for c in range(C):
                                last = pe.transpose(bank(6 + i % 2)[:, c * P:c * P + P],
                                                    ymix[:, c, i * P:i * P + P], ident[:])
                            last.then_inc(s["mixt"], 1)
            mixer.close()

            with ExitStack() as tmp:
                cq = sb("cq", [P, CH, TB], scope=tmp)
                cq_hi = sb("cq_hi", [P, CH, TB], F32R, scope=tmp)
                cq_lo = sb("cq_lo", [P, CH, TB], F32R, scope=tmp)
                PC = sb("PC", [P, 2, CH, NMEM], scope=tmp)
                PTc = sb("PTc", [P, 2 * CH, TB], scope=tmp)
                cs_ = sb("cs_", [P, 2, 3, CH], scope=tmp)
                O_OUT, O_CQ, O_CO = first_out[PAN_OUT], first_out[PAN_CQ], first_out[PAN_CO]
                with Phase(["r1" + n for n in RESID] + ["n2" + n for n in NORM] + ["r2" + n for n in RESID]
                           + ["cqev", "cq_hi", "cq_lo", "scores", "cmax", "cexp", "cprob", "pt", "ptsb", "ov", "oh", "ol"]) as (b, s):
                    def logits(c):
                        return G[:, 4 * (c % 2):4 * (c % 2) + 2, :]

                    @b.sync
                    def _(sp):
                        load_panels(sp, PAN_OUT + RING, PAN_FFN + RING)

                    @b.gpsimd
                    def _(pool):
                        rest_panels(pool, PAN_OUT + AHEAD, PAN_FFN + AHEAD)

                    @b.scalar
                    def _(act):
                        for n in range(KT):
                            round_panel(act, PAN_OUT + n + AHEAD)
                            if n >= 1:
                                square_act(act, s, "r1", n - 1)
                        square_act(act, s, "r1", KT - 1)
                        norm_split_act(act, s, "n2")
                        for n in range(CH):
                            round_panel(act, PAN_CQ + n + AHEAD)
                            act.wait_ge(s["cqev"], n + 1)
                            act.activation(cq_hi[:, n, :], cq[:, n, :], ACT.Copy).then_inc(s["cq_hi"], 1)

                        def transposed(c):
                            act.wait_ge(s["pt"], c + 1)
                            act.activation(PTc[:, :, c * P:c * P + P],
                                           G[:, 2:4, :].rearrange("p a (i t) -> p (a i) t", t=P), ACT.Copy)\
                               .then_inc(s["ptsb"], 1)

                        for c in range(C):
                            act.wait_ge(s["cmax"], c + 1)
                            for h in range(CH):
                                act.activation(PC[:, c % 2, h, :],
                                                      logits(c)[:, h // 2, (h % 2) * 256:(h % 2) * 256 + 256],
                                                      ACT.Exp,
                                                      bias=cs_[:, c % 2, 0, h:h + 1],
                                                      accum_out=cs_[:, c % 2, 1, h:h + 1]).then_inc(s["cexp"], 1)
                            if c >= 1:
                                transposed(c - 1)
                        transposed(C - 1)
                        for h in range(CH):
                            act.wait_ge(s["ov"], h + 1)
                            act.activation(xh[:, h, :], G[:, 4 + h % 2, :], ACT.Copy).then_inc(s["oh"], 1)
                        for n in range(KT):
                            if n % 2 == 0:
                                round_panel(act, PAN_CO + n // 2 + AHEAD)
                            if n >= 1:
                                square_act(act, s, "r2", n - 1)
                        square_act(act, s, "r2", KT - 1)

                    @b.vector
                    def _(dve):
                        for n in range(KT):
                            residual_dve(dve, s, "r1", O_OUT, n, True)
                        dve.wait_ge(s["r1h"], KT)
                        norm_split_dve(dve, s, "n2", PV_CROSS)
                        sum_squares_dve(dve, s, "r1", KT - 1)
                        dve.wait_ge(s["r1tok"], 1)
                        norm_rows_dve(dve, s, "n2", G[:, 5, 0:C])
                        norm_row_back_dve(dve, s, "n2")

                        def query_rest(n):
                            dve.wait_ge(s["cq_hi"], n + 1)
                            dve.tensor_tensor(cq_lo[:, n, :], cq[:, n, :], cq_hi[:, n, :].bitcast(F32),
                                              ALU.subtract).then_inc(s["cq_lo"], 1)

                        for n in range(CH):
                            dve.wait_ge(stream["lin_out"], O_CQ + n + 1)
                            dve.scalar_tensor_tensor(cq[:, n, :], L[:, (O_CQ + n) % 2, :], P ** -0.5, RB,
                                                     ALU.mult, ALU.mult)\
                               .then_inc(s["cqev"], 1)
                            if n >= 1:
                                query_rest(n - 1)
                        query_rest(CH - 1)

                        def normalise(c):
                            dve.wait_ge(s["cexp"], CH * (c + 1))
                            dve.reciprocal(cs_[:, c % 2, 2, :], cs_[:, c % 2, 1, :])
                            dve.drain()
                            for h in range(CH):
                                last = dve.tensor_scalar(PC[:, c % 2, h, :], PC[:, c % 2, h, :],
                                                         cs_[:, c % 2, 2, h:h + 1], None, ALU.mult)
                            last.then_inc(s["cprob"], 1)

                        for c in range(C):
                            dve.wait_ge(s["scores"], c + 1)
                            dve.tensor_reduce(cs_[:, c % 2, 0, :],
                                              logits(c).rearrange("p a (h m) -> p (a h) m", h=2), AX_X, ALU.max,
                                              negate=True).then_inc(s["cmax"], 1)
                            normalise(c)
                        for h in range(CH):
                            dve.wait_ge(s["oh"], h + 1)
                            dve.tensor_tensor(xl[:, h, :], G[:, 4 + h % 2, :], xh[:, h, :].bitcast(F32),
                                              ALU.subtract).then_inc(s["ol"], 1)
                        for n in range(KT):
                            residual_dve(dve, s, "r2", O_CO, n, True)
                        sum_squares_dve(dve, s, "r2", KT - 1)

                    @b.tensor
                    def _(pe):
                        for n in range(KT):
                            multiply_panel(pe, PAN_OUT + n, xh, xl,
                                           free=(lambda o: pe.wait_ge(s["r1h"], o - O_OUT - 1)) if n >= 2 else None)
                        for n in range(CH):
                            if n == 1:
                                token_sums_pe(pe, s, "r1")
                            elif n == 2:
                                norm_rows_pe(pe, s, "n2")
                            multiply_panel(pe, PAN_CQ + n, xh, xl,
                                           each_k=(lambda k: pe.wait_ge(s["n2xl"], k + 1)) if n == 0 else None,
                                           free=(lambda o: pe.wait_ge(s["cqev"], o - O_CQ - 1)) if n >= 2 else None)

                        def scores(c):
                            if c >= 2:
                                pe.wait_ge(s["cexp"], CH * (c - 1))
                            for h in range(CH):
                                if c == 0:
                                    pe.wait_ge(s["cq_lo"], h + 1)
                                o = logits(c)[:, h // 2, (h % 2) * 256:(h % 2) * 256 + 256]
                                qh, ql = cq_hi[:, h, c * P:c * P + P], cq_lo[:, h, c * P:c * P + P]
                                pe.matmul(o, qh, km_hi[:, h, :], start=True, stop=False)
                                pe.matmul(o, qh, km_lo[:, h, :], start=False, stop=False)
                                last = pe.matmul(o, ql, km_hi[:, h, :], start=False, stop=True)
                            last.then_inc(s["scores"], 1)

                        scores(0)
                        for c in range(C):
                            if c + 1 < C:
                                scores(c + 1)
                            pe.wait_ge(s["cprob"], c + 1)
                            if c >= 1:
                                pe.wait_ge(s["ptsb"], c)
                            for i in range(2 * CH):
                                last = pe.transpose(G[:, 2 + i // 4, (i % 4) * P:(i % 4) * P + P],
                                                    PC[:, c % 2, i // 2, (i % 2) * P:(i % 2) * P + P], ident[:])
                            last.then_inc(s["pt"], 1)
                        pe.wait_ge(s["ptsb"], C)
                        for h in range(CH):
                            if h >= 2:
                                pe.wait_ge(s["ol"], h - 1)
                            for m in range(2):
                                last = pe.matmul(G[:, 4 + h % 2, :], vm[:, m, h * P:h * P + P],
                                                 PTc[:, 2 * h + m, :], start=(m == 0), stop=(m == 1))
                            last.then_inc(s["ov"], 1)
                        pe.wait_ge(s["ol"], CH)
                        for n in range(4):
                            multiply_panel(pe, PAN_CO + n, xh, xl,
                                           free=(lambda o: pe.wait_ge(s["r2h"], o - O_CO - 1)) if n >= 1 else None)

            with ExitStack() as tmp:
                hid_h = sb("hid_h", [P, 8, TB], F32R, scope=tmp)
                hid_l = sb("hid_l", [P, 8, TB], F32R, scope=tmp)
                sg = sb("sg", [P, 2, TB], scope=tmp)
                gu = sb("gu", [P, 2, TB], scope=tmp)
                yout = sb("yout", [P, C, D], scope=tmp)
                steps = []
                for g, (f0, f1) in enumerate(FGROUPS):
                    for f in range(f0, f1):
                        steps += [("gate", f, g), ("up", f, g)]
                    steps += [("down", n, g) for n in range(KT)]
                O_FFN = first_out[PAN_FFN]
                assert O_FFN % 2 == 0 and len(steps) == NPAN - PAN_FFN
                LASTG = len(FGROUPS) - 1
                with Phase(["gate", "up", "hh", "hl"] + ["n3" + n for n in NORM] + ["n3tok", "gm", "gr"] + ["rf" + n for n in RESID]
                           + ["nfnt", "yscaled", "yt", "yev", "out_done"]) as (b, s):

                    @b.sync
                    def _(sp):
                        load_panels(sp, PAN_FFN + RING, NPAN)
                        for c in range(C):
                            sp.wait_ge(s["yscaled"], c + 1)
                            sp.dma_start(y_prompt[0, bass.ds(blk * TB + c * P, P), :], yout[:, c, :])\
                              .then_inc(s["out_done"], 16)
                        sp.wait_ge(s["out_done"], 16 * C)

                    @b.gpsimd
                    def _(pool):
                        rest_panels(pool, PAN_FFN + AHEAD, NPAN)

                    @b.scalar
                    def _(act):
                        def round_hidden(f):
                            act.wait_ge(s["up"], f + 1)
                            act.activation(hid_h[:, f % 8, :], gu[:, f % 2, :], ACT.Copy).then_inc(s["hh"], 1)

                        def to_output(i):
                            act.wait_ge(s["yt"], i + 1)
                            act.activation(yout[:, :, i * P:i * P + P],
                                           G[:, i % 2, :].rearrange("p (c t) -> p c t", t=P), ACT.Copy)\
                               .then_inc(s["yev"], 1)

                        norm_split_act(act, s, "n3")
                        for o, (kind, i, g) in enumerate(steps):
                            round_panel(act, PAN_FFN + o + AHEAD)
                            if kind == "gate":
                                act.wait_ge(s["gm"], i + 1)
                                act.activation(sg[:, i % 2, :], sg[:, i % 2, :], ACT.Silu).then_inc(s["gate"], 1)
                                if i > FGROUPS[g][0]:
                                    round_hidden(i - 1)
                            elif kind == "down":
                                if i == 0:
                                    round_hidden(FGROUPS[g][1] - 1)
                                if g == LASTG and i >= 1:
                                    square_act(act, s, "rf", i - 1, done=g * KT + i - 1)
                                if g == LASTG and i >= 2:
                                    to_output(i - 2)
                        square_act(act, s, "rf", KT - 1, done=LASTG * KT + KT - 1)
                        to_output(KT - 2)
                        to_output(KT - 1)

                    @b.vector
                    def _(dve):
                        def rest_hidden(f):
                            dve.wait_ge(s["hh"], f + 1)
                            dve.tensor_tensor(hid_l[:, f % 8, :], gu[:, f % 2, :], hid_h[:, f % 8, :].bitcast(F32),
                                              ALU.subtract).then_inc(s["hl"], 1)

                        norm_split_dve(dve, s, "n3", PV_FFN)
                        dve.wait_ge(s["n3tok"], 1)
                        norm_rows_dve(dve, s, "n3", G[:, 5, 0:C])
                        norm_row_back_dve(dve, s, "n3")
                        for o, (kind, i, g) in enumerate(steps):
                            if kind == "gate":
                                dve.wait_ge(stream["lin_out"], O_FFN + o + 1)
                                if i >= 2:
                                    dve.wait_ge(s["up"], i - 1)
                                dve.tensor_tensor(sg[:, i % 2, :], L[:, o % 2, :], RB, ALU.mult)\
                                   .then_inc(s["gm"], 1)
                            elif kind == "up":
                                dve.wait_ge(s["gate"], i + 1)
                                dve.tensor_tensor(sg[:, i % 2, :], sg[:, i % 2, :], RB, ALU.mult)\
                                   .then_inc(s["gr"], 1)
                                dve.wait_ge(stream["lin_out"], O_FFN + o + 1)
                                dve.wait_ge(s["gr"], i + 1)
                                if i >= 2:
                                    dve.wait_ge(s["hl"], i - 1)
                                dve.tensor_tensor(gu[:, i % 2, :], sg[:, i % 2, :], L[:, o % 2, :], ALU.mult)\
                                   .then_inc(s["up"], 1)
                                if i > FGROUPS[g][0]:
                                    rest_hidden(i - 1)
                            elif kind == "down":
                                if i == 0:
                                    rest_hidden(FGROUPS[g][1] - 1)
                                dve.wait_ge(stream["lin_out"], O_FFN + o + 1)
                                if g >= 1:
                                    dve.wait_ge(s["rfh"], (g - 1) * KT + i + 1)
                                dve.tensor_tensor(hT[:, i, :], L[:, o % 2, :], hT[:, i, :], ALU.add)\
                                   .then_inc(s["rfh"], 1)
                                if g == LASTG:
                                    if i >= 2:
                                        dve.wait_ge(s["yt"], i - 1)
                                    dve.wait_ge(s["rfh"], g * KT + i + 1)
                                    dve.tensor_scalar(ntmp[:, i % 2, :], hT[:, i, :], g_of(PV_FINAL, i), None,
                                                      ALU.mult).then_inc(s["nfnt"], 1)
                                    if i >= 1:
                                        sum_squares_dve(dve, s, "rf", i - 1)
                        sum_squares_dve(dve, s, "rf", KT - 1)
                        dve.wait_ge(s["rftok"], 1)
                        v, r, t = small[:, 1, 0:C], small[:, 2, 0:C], small[:, 3, 0:C]
                        dve.tensor_scalar(v, G[:, 5, 0:C], 1.0 / D, EPS, ALU.mult, ALU.add)
                        dve.drain()
                        rsqrt(dve, v, r, t)
                        dve.wait_ge(s["yev"], KT)
                        for c in range(C):
                            dve.tensor_scalar(yout[:, c, :], yout[:, c, :], r[:, c:c + 1], None, ALU.mult)\
                               .then_inc(s["yscaled"], 1)

                    @b.tensor
                    def _(pe):
                        def turn(i):
                            pe.wait_ge(s["nfnt"], i + 1)
                            if i >= 2:
                                pe.wait_ge(s["yev"], i - 1)
                            for c in range(C):
                                last = pe.transpose(G[:, i % 2, c * P:c * P + P],
                                                    ntmp[:, i % 2, c * P:c * P + P], ident[:])
                            last.then_inc(s["yt"], 1)

                        for o, (kind, i, g) in enumerate(steps):
                            f0, f1 = FGROUPS[g]

                            def free(_, o=o):
                                if o < 2:
                                    return
                                kind2, i2, g2 = steps[o - 2]
                                if kind2 == "down":
                                    pe.wait_ge(s["rfh"], g2 * KT + i2 + 1)
                                else:
                                    pe.wait_ge(s["gm" if kind2 == "gate" else "up"], i2 + 1)

                            if o == 1:
                                token_sums_pe(pe, s, "n3", wait=False)
                            elif o == 2:
                                norm_rows_pe(pe, s, "n3")
                            if kind == "down":
                                each = (lambda k, f0=f0: pe.wait_ge(s["hl"], f0 + k + 1)) if i == 0 else None
                                multiply_panel(pe, PAN_FFN + o, hid_h, hid_l, each_k=each, free=free)
                                if g == LASTG and i >= 1:
                                    turn(i - 1)
                            else:
                                each = (lambda k: pe.wait_ge(s["n3xl"], k + 1)) if o == 0 else None
                                multiply_panel(pe, PAN_FFN + o, xh, xl, each_k=each, free=free)
                        turn(KT - 1)
                        token_sums_pe(pe, s, "rf")

            clear(stream.values())

        with ExitStack() as tmp:
            ktail = sb("ktail", [P, P], scope=tmp)
            ctail = sb("ctail", [3, D], scope=tmp)
            stail = sb("stail", [P, 4, P], scope=tmp)
            with Phase(["kt", "ct", "stt", "ktsb", "ctsb", "stsb", "out_done"]) as (b, s):

                @b.tensor
                def _(pe):
                    pe.transpose(G[:, 0, 0:P], kbuf[:, 0:P], ident[:]).then_inc(s["kt"], 1)
                    for i in range(KT):
                        last = pe.transpose(G[0:3, 1 + i // 4, (i % 4) * P:(i % 4) * P + P], carry[:, i, :], ident[:])
                    last.then_inc(s["ct"], 1)
                    for i in range(4):
                        last = pe.transpose(G[:, 3, i * P:i * P + P], state[:, i * P:i * P + P], ident[:])
                    last.then_inc(s["stt"], 1)

                @b.vector
                def _(dve):
                    dve.wait_ge(s["kt"], 1)
                    dve.tensor_copy(ktail[:], G[:, 0, 0:P]).then_inc(s["ktsb"], 1)
                    dve.wait_ge(s["ct"], 1)
                    dve.tensor_copy(ctail[:], G[0:3, 1:3, :].rearrange("p a n -> p (a n)")).then_inc(s["ctsb"], 1)
                    dve.wait_ge(s["stt"], 1)
                    dve.tensor_copy(stail[:], G[:, 3, :].rearrange("p (i n) -> p i n", n=P)).then_inc(s["stsb"], 1)

                @b.sync
                def _(sp):
                    sp.dma_start(p_swa_v[0, 0].rearrange("t v d -> t (v d)"), vtok[:, 0, :]).then_inc(s["out_done"], 16)
                    for src, dst in ((cache_swa_k, s_swa_k), (cache_swa_v, s_swa_v)):
                        sp.dma_start(dst[0, :, 0:WIN - TS].rearrange("b t v d -> b (t v d)"),
                                     src[0, :, TS:WIN].rearrange("b t v d -> b (t v d)")).then_inc(s["out_done"], 16)
                    sp.wait_ge(s["ktsb"], 1)
                    sp.dma_start(p_swa_k[0, 0].rearrange("t v d -> t (v d)"), ktail[:]).then_inc(s["out_done"], 16)
                    sp.wait_ge(s["ctsb"], 1)
                    sp.dma_start(p_conv[0, 0], ctail[:]).then_inc(s["out_done"], 16)
                    sp.wait_ge(s["stsb"], 1)
                    sp.dma_start(p_ssm[0, 0].rearrange("(i h) p n -> (h p) i n", h=2), stail[:])\
                      .then_inc(s["out_done"], 16)
                    sp.wait_ge(s["out_done"], 96)
        prompt.close()

        SR = 8
        sslot = {}
        on_slot = [0] * SR
        for n, (parts, _, _) in enumerate(panels):
            on_slot[n % SR] += sum(KV if part[0] == "kv" else 1 for part in parts)
            sslot[n] = on_slot[n % SR]
        group = whole.enter_context(ExitStack())
        hS = sb("hS", [P, KT, S], scope=group)
        xS = sb("xS", [P, KT, S], scope=group)
        wS = sb("wS", [P, SR, D], scope=group)
        sqS = sb("sqS", [P, KT, S], scope=group)
        sqsS = sb("sqsS", [P, S], scope=group)
        memK = sb("memK", [P, NB, 2, CH * P], scope=group)
        memV = sb("memV", [P, NB, 2, CH * P], scope=group)
        sstream = {n: group.enter_context(nc.semaphore("s_" + n))
                   for n in [f"w_in_slot{r}" for r in range(SR)] + ["lin_out", "mem_in"]}

        def s_load(sp, a, z):
            for n in range(a, min(z, NPAN)):
                if n >= SR:
                    sp.wait_ge(sstream["lin_out"], first_out[n - SR + 1])
                for dst, src in panel_slices(wS[:, n % SR, :], panels[n][0]):
                    sp.dma_start(dst, src).then_inc(sstream[f"w_in_slot{n % SR}"], 16)

        def s_multiply(pe, n, x, free):
            pe.wait_ge(sstream[f"w_in_slot{n % SR}"], 16 * sslot[n])
            kn, outs = panels[n][1], panels[n][2]
            for m in range(outs):
                o = first_out[n] + m
                free(o)
                for k in range(kn):
                    c0 = (k * outs + m) * P
                    last = pe.matmul(L[:, o % 2, 0:S], wS[:, n % SR, c0:c0 + P], x[:, k, :],
                                     start=(k == 0), stop=(k == kn - 1))
                last.then_inc(sstream["lin_out"], 1)

        SNORM = ["sq", "sqs", "tok", "diag", "rb", "x"]

        def s_norm_act(act, s, tag):
            act.activation(sqS[:], hS[:], ACT.Square).then_inc(s[tag + "sq"], 1)

        def s_norm_dve(dve, s, tag, row, out):
            v, r, t = small[0:S, 4, 0:1], small[0:S, 5, 0:1], small[0:S, 6, 0:1]
            dve.wait_ge(s[tag + "sq"], 1)
            dve.tensor_reduce(sqsS[:], sqS[:].rearrange("p k t -> p t k"), AX_X, ALU.add).then_inc(s[tag + "sqs"], 1)
            dve.wait_ge(s[tag + "tok"], 1)
            dve.tensor_scalar(v, G[0:S, 5, 0:1], 1.0 / D, EPS, ALU.mult, ALU.add)
            dve.drain()
            rsqrt(dve, v, r, t)
            dve.tensor_scalar(diag[0:S, 0:S], ident[0:S, 0:S], r, None, ALU.mult).then_inc(s[tag + "diag"], 1)
            dve.wait_ge(s[tag + "rb"], 1)
            dve.tensor_tensor(out[:], hS[:], G[:, 4, 0:S].unsqueeze(1).to_broadcast([P, KT, S]), ALU.mult)
            dve.drain()
            dve.tensor_tensor(out[:], out[:], pv[:, row:row + KT].unsqueeze(2).to_broadcast([P, KT, S]), ALU.mult)\
               .then_inc(s[tag + "x"], 1)

        def s_norm_pe(pe, s, tag):
            pe.wait_ge(s[tag + "sqs"], 1)
            pe.matmul(G[0:S, 5, 0:1], sqsS[:], ones[:, 0:1], start=True, stop=True).then_inc(s[tag + "tok"], 1)
            pe.wait_ge(s[tag + "diag"], 1)
            pe.matmul(G[:, 4, 0:S], ones[0:S, :], diag[0:S, 0:S], start=True, stop=True).then_inc(s[tag + "rb"], 1)

        def s_residual(dve, s, name, o0, n):
            dve.wait_ge(sstream["lin_out"], o0 + n + 1)
            dve.tensor_tensor(hS[:, n, :], L[:, (o0 + n) % 2, 0:S], hS[:, n, :], ALU.add).then_inc(s[name], 1)

        mixer = ExitStack()
        xbcS = sb("xbcS", [P, 8, S], scope=mixer)
        zsS = sb("zsS", [P, 4, S], scope=mixer)
        qS = sb("qS", [P, QJ, S], scope=mixer)
        kS = sb("kS", [P, S], scope=mixer)
        vS = sb("vS", [P, S], scope=mixer)
        dtS = sb("dtS", [S, 10, HS], scope=mixer)
        swK = sb("swK", [P, NB, P], scope=mixer)
        swV = sb("swV", [P, NB, P], scope=mixer)
        stN = sb("stN", [P, NB, 4, P], scope=mixer)
        biasC = sb("biasC", [P, WIN], scope=mixer)
        biasN = sb("biasN", [P, 4, S], scope=mixer)
        snkS = sb("snkS", [P, 1], scope=mixer)
        same = sb("same", [S, NB, TS], scope=mixer)
        leS = sb("leS", [S, S], scope=mixer)
        gtS = sb("gtS", [S, S], scope=mixer)
        in_sems = {n: mixer.enter_context(nc.semaphore("s_" + n)) for n in ("rows_in", "new_in", "swa_in", "ssm_in")}

        with ExitStack() as tmp:
            xin = sb("xinS", [S, D], scope=tmp)
            rawS = sb("rawS", [P, 8, NB, 3 + TS], scope=tmp)
            convS = sb("convS", [P, 8, S], scope=tmp)
            scrow = sb("scrow", [3 * NB, D], scope=tmp)
            lastS = sb("lastS", [P, 8, NB * 3], scope=tmp)
            lrow = sb("lrow", [3 * NB, D], scope=tmp)
            with Phase(["x_in", "sc_in", "xt", "hev", "sct", "scev", "lin_free", "conv", "last", "lt", "ltsb",
                        "dtp", "made", "same", "kill", "out_done"] + ["n1" + n for n in SNORM]) as (b, s):

                @b.sync
                def _(sp):
                    sp.dma_start(xin[:], x_sample.rearrange("b t d -> (b t) d")).then_inc(s["x_in"], 16)
                    sp.dma_start(scrow[:], state_conv[0].rearrange("b k d -> (b k) d")).then_inc(s["sc_in"], 16)
                    s_load(sp, 0, SR)
                    sp.dma_start(swK[:], cache_swa_k[0].rearrange("b t v d -> t b (v d)")).then_inc(in_sems["swa_in"], 16)
                    sp.dma_start(swV[:], cache_swa_v[0].rearrange("b t v d -> t b (v d)")).then_inc(in_sems["swa_in"], 16)
                    for bb in range(NB):
                        sp.dma_start(stN[:, bb], state_ssm[0, bb].rearrange("(i h) p n -> (h p) i n", h=2))\
                          .then_inc(in_sems["ssm_in"], 16)
                    s_load(sp, SR, PAN_OUT + SR)
                    sp.wait_ge(s["ltsb"], 1)
                    sp.dma_start(s_conv[0].rearrange("b k d -> (b k) d"), lrow[:]).then_inc(s["out_done"], 16)
                    for bb in range(NB):
                        sp.dma_start(memK[:, bb], cache_mem_k[0, bb].rearrange("(c p) h d -> p c (h d)", p=P))\
                          .then_inc(sstream["mem_in"], 16)
                        sp.dma_start(memV[:, bb], cache_mem_v[0, bb].rearrange("(c p) h d -> p c (h d)", p=P))\
                          .then_inc(sstream["mem_in"], 16)
                    sp.wait_ge(s["out_done"], 16)

                @b.gpsimd
                def _(pool):
                    pool.memset(same[:], 1.0).then_inc(s["made"], 1)
                    pool.memset(biasN[:], NEG).then_inc(s["kill"], 1)
                    pool.wait_ge(s["made"], 1)
                    pool.affine_select(out=same[:], in_=same[:], compare_op=ALU.is_ge, fill=0.0, base=0,
                                       pattern=[[-TS, NB], [0, TS]], channel_multiplier=1).then_inc(s["made"], 1)
                    pool.wait_ge(s["made"], 2)
                    pool.affine_select(out=same[:], in_=same[:], compare_op=ALU.is_ge, fill=0.0, base=TS - 1,
                                       pattern=[[TS, NB], [0, TS]], channel_multiplier=-1).then_inc(s["same"], 1)
                    pool.wait_ge(s["kill"], 1)
                    for b2 in range(2):
                        for t in range(TS):
                            rows = slice(b2 * 64 + t, b2 * 64 + t + 57, TS)
                            pool.dma_start(biasC[rows, :],
                                          bass.AP(tensor=bias_rows, offset=127 - t, ap=[[RLEN, HS], [1, WIN]]))\
                               .then_inc(in_sems["rows_in"], 16)
                            for bp in range(4):
                                c0 = (2 * bp + b2) * TS
                                pool.dma_start(biasN[rows, bp, c0:c0 + TS],
                                              bass.AP(tensor=bias_rows, offset=127 + WIN - t, ap=[[RLEN, HS], [1, TS]]))\
                                   .then_inc(in_sems["new_in"], 16)
                    for r in range(2):
                        pool.dma_start(snkS[64 * r:64 * r + 64, :],
                                      bass.AP(tensor=sinks.tensor, offset=0, ap=[[1, HS], [0, TS], [1, 1]]))\
                           .then_inc(in_sems["rows_in"], 16)

                @b.scalar
                def _(act):
                    act.wait_ge(s["hev"], 1)
                    s_norm_act(act, s, "n1")
                    for o in range(PAN_OUT):
                        act.wait_ge(sstream["lin_out"], o + 1)
                        src = L[:, o % 2, 0:S]
                        if o < PAN_K:
                            dst, f, sc = rawS[:, o, :, 3:], ACT.Copy, 1.0
                            src = src.rearrange("p (b t) -> p b t", t=TS)
                        elif o == PAN_K:
                            dst, f, sc = kS[:], ACT.Copy, 1.0
                        elif o == PAN_V:
                            dst, f, sc = vS[:], ACT.Copy, 1.0
                        elif o < PAN_Z:
                            dst, f, sc = qS[:, o - PAN_Q, :], ACT.Copy, 64 ** -0.5
                        else:
                            dst, f, sc = zsS[:, o - PAN_Z, :], ACT.Silu, 1.0
                        act.activation(dst, src, f, scale=sc).then_inc(s["lin_free"], 1)
                    act.wait_ge(s["conv"], 1)
                    act.activation(xbcS[:], convS[:], ACT.Silu)

                @b.vector
                def _(dve):
                    dve.wait_ge(s["xt"], 1)
                    dve.tensor_copy(hS[:], G[:, 0, :].rearrange("p (k t) -> p k t", t=S)).then_inc(s["hev"], 1)
                    dve.wait_ge(s["sct"], 1)
                    dve.tensor_copy(rawS[:, :, :, 0:3],
                                    G[:, 1, 0:24 * KT].rearrange("p (i b k) -> p i b k", b=NB, k=3))
                    dve.wait_ge(s["hev"], 1)
                    s_norm_dve(dve, s, "n1", PV_MIX, xS)
                    dve.wait_ge(s["same"], 1)
                    sm2 = same[:].rearrange("p b t -> p (b t)")
                    dve.tensor_tensor(leS[:], tri_le[0:S, 0:S], sm2, ALU.mult)
                    dve.tensor_tensor(gtS[:], tri_gt[0:S, 0:S], sm2, ALU.mult)
                    for i in range(8):
                        cv = convS[:, i, :].rearrange("p (b t) -> p b t", t=TS)
                        dve.wait_ge(s["lin_free"], i + 1)
                        dve.tensor_scalar(cv, rawS[:, i, :, 0:TS], g_of(PV_CW, i), g_of(PV_CB, i),
                                          ALU.mult, ALU.add)
                        for k in range(1, 4):
                            dve.drain()
                            last = dve.scalar_tensor_tensor(cv, rawS[:, i, :, k:k + TS], g_of(PV_CW + 8 * k, i), cv,
                                                            ALU.mult, ALU.add)
                    last.then_inc(s["conv"], 1)
                    dve.tensor_copy(lastS[:].rearrange("p i (b k) -> p i b k", k=3), rawS[:, :, :, TS:TS + 3])\
                       .then_inc(s["last"], 1)
                    dve.wait_ge(s["lt"], 1)
                    dve.tensor_copy(lrow[:], G[0:24, 2:4, :].rearrange("p a n -> p (a n)")).then_inc(s["ltsb"], 1)

                @b.tensor
                def _(pe):
                    pe.wait_ge(s["x_in"], 16)
                    for i in range(KT):
                        last = pe.transpose(G[:, 0, i * S:i * S + S], xin[:, i * P:i * P + P], ident[0:S, 0:S])
                    last.then_inc(s["xt"], 1)
                    pe.wait_ge(s["sc_in"], 16)
                    for i in range(KT):
                        last = pe.transpose(G[:, 1, i * 24:i * 24 + 24], scrow[:, i * P:i * P + P], ident[0:24, 0:24])
                    last.then_inc(s["sct"], 1)
                    s_norm_pe(pe, s, "n1")
                    pe.wait_ge(s["n1x"], 1)
                    for n in range(PAN_OUT):
                        s_multiply(pe, n, xS, lambda o: o >= 2 and pe.wait_ge(s["lin_free"], o - 1))
                    for k in range(KT):
                        last = pe.matmul(G[0:S, 5, 0:HS], xS[:, k, :], wdt[:, k, :], start=(k == 0),
                                         stop=(k == KT - 1))
                    last.then_inc(s["dtp"], 1)
                    pe.wait_ge(s["last"], 1)
                    for i in range(KT):
                        last = pe.transpose(G[0:24, 2 + i // 4, (i % 4) * P:(i % 4) * P + P], lastS[:, i, :], ident[:])
                    last.then_inc(s["lt"], 1)

        with ExitStack() as tmp:
            stT = sb("stT", [P, NB, 512], scope=tmp)
            Cz = sb("Cz", [P, NB, 2, S], scope=tmp)
            Bz = sb("Bz", [S, NB, 256], scope=tmp)
            xdtS = sb("xdtS", [S, 512], scope=tmp)
            xddS = sb("xddS", [S, 512], scope=tmp)
            yDS = sb("yDS", [S, 512], scope=tmp)
            yS = sb("yS", [S, 512], scope=tmp)
            btS = sb("btS", [S, 256], scope=tmp)
            rdaS = sb("rdaS", [S, HS * S], scope=tmp)
            ES = sb("ES", [S, HS * S], scope=tmp)
            cbS = sb("cbS", [S, 2 * S], scope=tmp)
            exS = sb("exS", [S, 2 * HS], scope=tmp)
            dab = sb("dab", [S, NB, HS], scope=tmp)
            edS = sb("edS", [P, NB, HS], scope=tmp)
            ssS = sb("ssS", [S, 5, 2], scope=tmp)
            junkS = sb("junkS", [S, 512], scope=tmp)
            Qz = sb("Qz", [P, NB, HS, TS], scope=tmp)
            kcT = sb("kcT", [P, NB, P], scope=tmp)
            ktS = sb("ktS", [S, P], scope=tmp)
            vtS = sb("vtS", [S, P], scope=tmp)
            sS = sb("sS", [P, 4, WIN + S], scope=tmp)
            stat = sb("stat", [P, 8, 4], scope=tmp)
            pcT = sb("pcT", [P, 4, P], scope=tmp)
            pnT = sb("pnT", [S, 4, P], scope=tmp)
            with Phase(["dtr", "dte", "dtu", "dtl", "da", "rda", "cum", "ex", "diff", "E", "xt", "bt", "btev",
                        "cb", "cz", "czero", "bz", "stt", "stev", "yoff", "xdd", "M", "yd", "zt", "y", "ss", "yn",
                        "yt", "ytev", "sn", "snew", "so", "soev", "qz", "qzero", "kct", "kcev", "new_t", "newev",
                        "sc", "nmax", "prob", "pn", "pt", "ptev", "pvs", "mix", "out_done"]) as (b, s):

                @b.sync
                def _(sp):
                    sp.wait_ge(s["newev"], 1)
                    sp.dma_start(s_swa_k[0, :, WIN - TS:WIN].rearrange("b t v d -> b t (v d)"), ktS[:])\
                      .then_inc(s["out_done"], 16)
                    sp.dma_start(s_swa_v[0, :, WIN - TS:WIN].rearrange("b t v d -> b t (v d)"), vtS[:])\
                      .then_inc(s["out_done"], 16)
                    for bb in range(NB):
                        sp.wait_ge(s["soev"], bb + 1)
                        sp.dma_start(s_ssm[0, bb].rearrange("(i h) p n -> (h p) i n", h=2), stN[:, bb])\
                          .then_inc(s["out_done"], 16)
                    sp.wait_ge(s["out_done"], 16 * (2 + NB))

                @b.gpsimd
                def _(pool):
                    pool.memset(Cz[:], 0.0).then_inc(s["czero"], 1)
                    pool.memset(Qz[:], 0.0).then_inc(s["qzero"], 1)

                @b.scalar
                def _(act):
                    act.wait_ge(s["dtr"], 1)
                    act.activation(dtS[:, 3, :], dtS[:, 2, :], ACT.Exp).then_inc(s["dte"], 1)
                    act.wait_ge(s["dtu"], 1)
                    act.activation(dtS[:, 5, :], dtS[:, 4, :], ACT.Ln).then_inc(s["dtl"], 1)
                    act.wait_ge(s["cum"], 1)
                    act.activation(exS[:], G[0:S, 2, 0:2 * HS], ACT.Exp)
                    act.activation(edS[:], G[:, 2, 64:64 + NB * HS].rearrange("p (b h) -> p b h", h=HS), ACT.Exp)\
                       .then_inc(s["ex"], 1)
                    act.wait_ge(s["diff"], 1)
                    act.activation(ES[:], G[0:S, 3, :], ACT.Exp).then_inc(s["E"], 1)
                    for bb in range(NB):
                        act.wait_ge(s["stt"], bb + 1)
                        act.activation(stT[:, bb, :], L[:, bb % 2, :], ACT.Copy).then_inc(s["stev"], 1)
                    act.wait_ge(s["y"], 1)
                    for g in range(2):
                        act.activation(junkS[:, g * 256:g * 256 + 256], yS[:, g * 256:g * 256 + 256], ACT.Square,
                                       accum_out=ssS[:, 0, g:g + 1]).then_inc(s["ss"], 1)
                    act.wait_ge(s["yt"], 1)
                    for i in range(4):
                        last = act.activation(xS[:, i, :], G[:, 0, i * S:i * S + S], ACT.Copy, scale=g_of(PV_SSD, i))
                    last.then_inc(s["ytev"], 1)
                    for bb in range(NB):
                        act.wait_ge(s["so"], bb + 1)
                        act.activation(stN[:, bb], L[:, bb % 2, :].rearrange("p (i n) -> p i n", n=P), ACT.Copy)\
                           .then_inc(s["soev"], 1)
                    for g in range(2):
                        act.wait_ge(s["kct"], g + 1)
                        act.activation(kcT[:, 4 * g:4 * g + 4, :], G[:, g, :].rearrange("p (b t) -> p b t", t=P),
                                       ACT.Copy).then_inc(s["kcev"], 1)
                    act.wait_ge(s["nmax"], 1)
                    for bp in range(4):
                        act.activation(sS[:, bp, :], sS[:, bp, :], ACT.Exp, bias=stat[:, 2, bp:bp + 1],
                                       accum_out=stat[:, 4, bp:bp + 1])
                    act.activation(stat[:, 5, :], stat[:, 3, :], ACT.Exp).then_inc(s["prob"], 1)

                @b.vector
                def _(dve):
                    dt_, d, na, e, u, ln, q, r, da_ = (dtS[:, i, :] for i in range(9))
                    d, dt_ = dtS[:, 1, :], dtS[:, 0, :]
                    dve.tensor_tensor(d, G[0:S, 5, 0:HS], dtb[0:S, :], ALU.add)
                    dve.drain()
                    dve.scalar_tensor_tensor(na, d, -1.0, d, ALU.mult, ALU.min).then_inc(s["dtr"], 1)
                    dve.wait_ge(s["dte"], 1)
                    dve.tensor_scalar(u, e, 1.0, None, ALU.add).then_inc(s["dtu"], 1)
                    dve.wait_ge(s["dtu"], 1)
                    dve.tensor_scalar(q, u, -1.0, None, ALU.add)
                    dve.drain()
                    dve.tensor_scalar(r, q, 1e-30, None, ALU.max)
                    dve.drain()
                    dve.reciprocal(r, r)
                    dve.tensor_scalar(q, q, 0.0, None, ALU.is_equal)
                    dve.wait_ge(s["dtl"], 1)
                    dve.drain()
                    dve.tensor_tensor(r, r, ln, ALU.mult)
                    dve.drain()
                    dve.tensor_tensor(r, r, q, ALU.add)
                    dve.drain()
                    dve.tensor_tensor(r, r, e, ALU.mult)
                    dve.drain()
                    dve.scalar_tensor_tensor(dt_, d, 0.0, r, ALU.max, ALU.add)
                    dve.drain()
                    dve.tensor_tensor(da_, dt_, nega[0:S, :], ALU.mult)
                    dve.drain()
                    sel = same[:, :, 0]
                    bch = lambda t, w: t.unsqueeze(2).to_broadcast([S, t.shape[1], w])
                    v3 = lambda t: t.rearrange("p (h w) -> p h w", h=HS)
                    dve.tensor_tensor(dab[:], bch(sel, HS), da_.unsqueeze(1).to_broadcast([S, NB, HS]), ALU.mult)\
                       .then_inc(s["da"], 1)
                    dve.tensor_tensor(v3(rdaS[:]), leS[:].unsqueeze(1).to_broadcast([S, HS, S]), bch(da_, S),
                                      ALU.mult).then_inc(s["rda"], 1)
                    dve.wait_ge(s["xt"], 1)
                    dve.tensor_tensor(v3(xdtS[:]), v3(G[0:S, 0, :]), bch(dt_, HP), ALU.mult)
                    dve.tensor_tensor(v3(yDS[:]), v3(G[0:S, 0, :]), bch(dsk[0:S, :], HP), ALU.mult)
                    dve.wait_ge(s["ex"], 1)
                    dve.drain()
                    dve.tensor_tensor(v3(xddS[:]), v3(xdtS[:]), bch(exS[:, HS:2 * HS], HP), ALU.mult)\
                       .then_inc(s["xdd"], 1)
                    dve.wait_ge(s["bt"], 1)
                    dve.tensor_copy(btS[:], G[0:S, 1, 0:256]).then_inc(s["btev"], 1)
                    dve.wait_ge(s["btev"], 1)
                    for bb in range(NB):
                        last = dve.tensor_scalar(Bz[:, bb, :], btS[:], same[:, bb, 0:1], None, ALU.mult)
                    last.then_inc(s["bz"], 1)
                    dve.wait_ge(s["czero"], 1)
                    for bb in range(NB):
                        t = slice(bb * TS, bb * TS + TS)
                        last = dve.tensor_copy(Cz[:, bb, :, t], xbcS[:, 6:8, t])
                    last.then_inc(s["cz"], 1)
                    dve.wait_ge(s["cb"], 1)
                    dve.tensor_tensor(cbS[:].rearrange("p (g q) -> p g q", g=2),
                                      G[0:S, 1, 256:256 + 2 * S].rearrange("p (g q) -> p g q", g=2),
                                      leS[:].unsqueeze(1).to_broadcast([S, 2, S]), ALU.mult)
                    dve.wait_ge(s["E"], 1)
                    dve.drain()
                    for g in range(2):
                        eg = ES[:, g * 256:g * 256 + 256].rearrange("p (h q) -> p h q", h=4)
                        last = dve.tensor_tensor(eg, eg, cbS[:, g * S:g * S + S].unsqueeze(1)
                                                 .to_broadcast([S, 4, S]), ALU.mult)
                    last.then_inc(s["M"], 1)
                    dve.wait_ge(s["yoff"], 1)
                    dve.tensor_tensor(v3(yS[:]), v3(G[0:S, 4, :]), bch(exS[:, 0:HS], HP), ALU.mult)
                    dve.drain()
                    dve.tensor_tensor(yS[:], yS[:], yDS[:], ALU.add)
                    dve.drain()
                    dve.wait_ge(s["yd"], 1)
                    dve.tensor_tensor(yS[:], yS[:], G[0:S, 3, :], ALU.add)
                    dve.drain()
                    dve.wait_ge(s["zt"], 1)
                    dve.tensor_tensor(yS[:], yS[:], G[0:S, 0, :], ALU.mult).then_inc(s["y"], 1)
                    dve.wait_ge(s["ss"], 2)
                    dve.tensor_scalar(ssS[:, 1, :], ssS[:, 0, :], 1.0 / 256, EPS, ALU.mult, ALU.add)
                    dve.drain()
                    rsqrt(dve, ssS[:, 1, :], ssS[:, 2, :], ssS[:, 3, :])
                    yv = yS[:].rearrange("p (g w) -> p g w", g=2)
                    dve.tensor_tensor(yv, yv, bch(ssS[:, 2, :], 256), ALU.mult).then_inc(s["yn"], 1)
                    for bb in range(NB):
                        sv = stT[:, bb, :].rearrange("p (h w) -> p h w", h=HS)
                        dve.wait_ge(s["sn"], bb + 1)
                        dve.tensor_tensor(sv, sv, edS[:, bb, :].unsqueeze(2).to_broadcast([P, HS, HP]), ALU.mult)
                        dve.drain()
                        dve.tensor_tensor(stT[:, bb, :], stT[:, bb, :], G[:, 2 + bb % 2, :], ALU.add)\
                           .then_inc(s["snew"], 1)
                    dve.wait_ge(s["qzero"], 1)
                    for j in range(QJ):
                        for v in range(KV):
                            r_ = slice(64 * v, 64 * v + 64)
                            last = dve.tensor_copy(Qz[r_, :, QJ * v + j, :],
                                                   qS[r_, j, :].rearrange("p (b t) -> p b t", t=TS))
                    last.then_inc(s["qz"], 1)
                    dve.wait_ge(s["new_t"], 1)
                    dve.tensor_copy(ktS[:], G[0:S, 4, 0:P])
                    dve.tensor_copy(vtS[:], G[0:S, 4, P:2 * P]).then_inc(s["newev"], 1)
                    dve.wait_ge(s["sc"], 1)
                    dve.wait_ge(in_sems["rows_in"], 16 * (2 * TS + 2))
                    dve.wait_ge(in_sems["new_in"], 16 * 8 * TS)
                    for a in range(2):
                        ps = G[:, 2 + a, 0:2 * (WIN + S)].rearrange("p (c k) -> p c k", c=2)
                        cs2 = slice(2 * a, 2 * a + 2)
                        dve.tensor_tensor(sS[:, cs2, 0:WIN], ps[:, :, 0:WIN],
                                          biasC[:].unsqueeze(1).to_broadcast([P, 2, WIN]), ALU.add)
                        dve.tensor_tensor(sS[:, cs2, WIN:], ps[:, :, WIN:], biasN[:, cs2, :], ALU.add)
                    dve.drain()
                    dve.tensor_reduce(stat[:, 0, :], sS[:], AX_X, ALU.max)
                    dve.drain()
                    dve.tensor_scalar(stat[:, 1, :], stat[:, 0, :], snkS[:], None, ALU.max)
                    dve.drain()
                    dve.tensor_scalar(stat[:, 2, :], stat[:, 1, :], -1.0, None, ALU.mult)
                    dve.tensor_scalar(stat[:, 3, :], stat[:, 1, :], -1.0, snkS[:], ALU.mult, ALU.add)\
                       .then_inc(s["nmax"], 1)
                    dve.wait_ge(s["prob"], 1)
                    dve.tensor_tensor(stat[:, 6, :], stat[:, 4, :], stat[:, 5, :], ALU.add)
                    dve.drain()
                    dve.reciprocal(stat[:, 7, :], stat[:, 6, :])
                    dve.drain()
                    dve.tensor_tensor(sS[:], sS[:], stat[:, 7, :].unsqueeze(2).to_broadcast([P, 4, WIN + S]),
                                      ALU.mult).then_inc(s["pn"], 1)
                    dve.wait_ge(s["pt"], 1)
                    dve.tensor_copy(pcT[:], G[:, 0, :].rearrange("p (b r) -> p b r", r=P))
                    dve.tensor_copy(pnT[:], G[0:S, 1, :].rearrange("p (b r) -> p b r", r=P)).then_inc(s["ptev"], 1)
                    dve.wait_ge(s["pvs"], 1)
                    dve.wait_ge(s["ytev"], 1)
                    for v in range(KV):
                        r_ = slice(64 * v, 64 * v + 64)
                        src = G[r_, 4, :].rearrange("p (b h t) -> p h b t", h=HS, t=TS)
                        last = dve.tensor_copy(xS[r_, 4:8, :].rearrange("p j (b t) -> p j b t", t=TS),
                                               src[:, QJ * v:QJ * v + QJ])
                    last.then_inc(s["mix"], 1)

                @b.tensor
                def _(pe):
                    for i in range(4):
                        last = pe.transpose(G[0:S, 0, i * P:i * P + P], xbcS[:, i, :], ident[:])
                    last.then_inc(s["xt"], 1)
                    for g in range(2):
                        last = pe.transpose(G[0:S, 1, g * P:g * P + P], xbcS[:, 4 + g, :], ident[:])
                    last.then_inc(s["bt"], 1)
                    pe.wait_ge(in_sems["ssm_in"], 16 * NB)
                    for bb in range(NB):
                        if bb >= 2:
                            pe.wait_ge(s["stev"], bb - 1)
                        for i in range(4):
                            last = pe.transpose(L[:, bb % 2, i * P:i * P + P], stN[:, bb, i, :], ident[:])
                        last.then_inc(s["stt"], 1)
                        if bb == 0:
                            pe.wait_ge(s["da"], 1)
                            da_ = dtS[:, 8, :]
                            pe.matmul(G[0:S, 2, 0:HS], leS[:], da_, start=True, stop=True)
                            pe.matmul(G[0:S, 2, HS:2 * HS], gtS[:], da_, start=True, stop=True)
                            pe.matmul(G[:, 2, 64:64 + NB * HS], ones[0:S, :], dab[:], start=True, stop=True)\
                              .then_inc(s["cum"], 1)
                            pe.wait_ge(s["rda"], 1)
                            pe.matmul(G[0:S, 3, :], gtS[:], rdaS[:], start=True, stop=True).then_inc(s["diff"], 1)
                    pe.wait_ge(s["btev"], 1)
                    for g in range(2):
                        last = pe.matmul(G[0:S, 1, 256 + g * S:256 + g * S + S], xbcS[:, 4 + g, :], xbcS[:, 6 + g, :],
                                         start=True, stop=True)
                    last.then_inc(s["cb"], 1)
                    pe.wait_ge(s["stev"], NB)
                    pe.wait_ge(s["cz"], 1)
                    for g in range(2):
                        for bb in range(NB):
                            last = pe.matmul(G[0:S, 4, g * 256:g * 256 + 256], Cz[:, bb, g, :],
                                             stT[:, bb, g * 256:g * 256 + 256], start=(bb == 0), stop=(bb == NB - 1))
                    last.then_inc(s["yoff"], 1)
                    pe.wait_ge(s["M"], 1)
                    for h in range(HS):
                        last = pe.matmul(G[0:S, 3, h * HP:h * HP + HP], ES[:, h * S:h * S + S],
                                         xdtS[:, h * HP:h * HP + HP], start=True, stop=True)
                    last.then_inc(s["yd"], 1)
                    pe.wait_ge(s["xdd"], 1)
                    for i in range(4):
                        last = pe.transpose(G[0:S, 0, i * P:i * P + P], zsS[:, i, :], ident[:])
                    last.then_inc(s["zt"], 1)
                    pe.wait_ge(s["yn"], 1)
                    for i in range(4):
                        last = pe.transpose(G[:, 0, i * S:i * S + S], yS[:, i * P:i * P + P], ident[0:S, 0:S])
                    last.then_inc(s["yt"], 1)

                    def back(bb):
                        pe.wait_ge(s["snew"], bb + 1)
                        if bb >= 2:
                            pe.wait_ge(s["soev"], bb - 1)
                        for i in range(4):
                            last = pe.transpose(L[:, bb % 2, i * P:i * P + P], stT[:, bb, i * P:i * P + P], ident[:])
                        last.then_inc(s["so"], 1)

                    pe.wait_ge(s["bz"], 1)
                    for bb in range(NB):
                        if bb >= 2:
                            pe.wait_ge(s["snew"], bb - 1)
                        for g in range(2):
                            last = pe.matmul(G[:, 2 + bb % 2, g * 256:g * 256 + 256], Bz[:, bb, g * P:g * P + P],
                                             xddS[:, g * 256:g * 256 + 256], start=True, stop=True)
                        last.then_inc(s["sn"], 1)
                        if bb >= 1:
                            back(bb - 1)
                    back(NB - 1)
                    pe.transpose(G[0:S, 4, 0:P], kS[:], ident[:])
                    pe.transpose(G[0:S, 4, P:2 * P], vS[:], ident[:]).then_inc(s["new_t"], 1)
                    pe.wait_ge(in_sems["swa_in"], 32)
                    pe.wait_ge(s["ytev"], 1)
                    for bb in range(NB):
                        last = pe.transpose(G[:, bb // 4, (bb % 4) * P:(bb % 4) * P + P], swK[:, bb, :], ident[:])
                        if bb % 4 == 3:
                            last.then_inc(s["kct"], 1)
                    pe.wait_ge(s["kcev"], 2)
                    pe.wait_ge(s["qz"], 1)
                    for bb in range(NB):
                        r = slice(64 * (bb % 2), 64 * (bb % 2) + 64)
                        bp = bb // 2
                        c0 = (bp % 2) * (WIN + S)
                        lq = Qz[:, bb].rearrange("p h t -> p (h t)")
                        pe.matmul(G[r, 2 + bp // 2, c0:c0 + WIN], lq, kcT[:, bb, :], start=True, stop=True)
                        last = pe.matmul(G[r, 2 + bp // 2, c0 + WIN:c0 + WIN + S], lq, kS[:], start=True, stop=True)
                    last.then_inc(s["sc"], 1)
                    pe.wait_ge(s["pn"], 1)
                    for bp in range(4):
                        pe.transpose(G[:, 0, bp * P:bp * P + P], sS[:, bp, 0:WIN], ident[:])
                    for bp in range(4):
                        last = pe.transpose(G[0:S, 1, bp * P:bp * P + P], sS[:, bp, WIN:], ident[:])
                    last.then_inc(s["pt"], 1)
                    pe.wait_ge(s["ptev"], 1)
                    for bb in range(NB):
                        r = slice(64 * (bb % 2), 64 * (bb % 2) + 64)
                        o = G[:, 4, bb * 64:bb * 64 + 64]
                        pe.matmul(o, swV[:, bb, :], pcT[:, bb // 2, r], start=True, stop=False)
                        last = pe.matmul(o, vtS[:], pnT[:, bb // 2, r], start=False, stop=True)
                    last.then_inc(s["pvs"], 1)
        clear(in_sems.values())
        mixer.close()

        with ExitStack() as tmp:
            kmS = sb("kmS", [P, NB, CH, NMEM], scope=tmp)
            Qc = sb("Qc", [P, NB, CH, CH, TS], scope=tmp)
            sX = sb("sX", [P, 2, NMEM], scope=tmp)
            stx = sb("stx", [P, 4, 2], scope=tmp)
            pxT = sb("pxT", [P, 2, 2, P], scope=tmp)
            oS = sb("oS", [P, CH, S], scope=tmp)
            O_OUT, O_CQ, O_CO = (first_out[n] for n in (PAN_OUT, PAN_CQ, PAN_CO))
            FC = [(c, min(c + 512, DFF)) for c in range(0, DFF, 512)]
            NFC = len(FC)
            hrow = sb("hrow", [S, D], scope=tmp)
            grow = sb("grow", [S, D], scope=tmp)
            sgS = sb("sgS", [S, 2, 512], scope=tmp)
            huS = sb("huS", [S, 2, 512], scope=tmp)
            hid = sb("hid", [P, 2, 4, S], scope=tmp)
            junkF = sb("junkF", [S, D], scope=tmp)
            nrm = sb("nrm", [S, 4], scope=tmp)
            yoS = sb("yoS", [S, D], scope=tmp)
            pieces, piece_of = [], {}

            def add_piece(key, src, k):
                piece_of[key] = len(pieces)
                pieces.append((src, k))

            for c in range(NFC + 1):
                if c < NFC:
                    for kind, w in (("gate", w_gate), ("up", w_up)):
                        for kh in range(2):
                            add_piece((kind, c, kh), w[kh * 512:kh * 512 + 512, FC[c][0]:FC[c][1]]
                                      .rearrange("(k p) n -> p k n", p=P), 4)
                if c >= 1:
                    f0, f1 = FC[c - 1]
                    for fh in range((f1 - f0) // 256):
                        add_piece(("down", c - 1, fh), w_down[f0 + fh * 256:f0 + fh * 256 + 256, :]
                                  .rearrange("(k p) n -> p k n", p=P), 2)

            def through(kind, c):
                return 1 + max(n for (kd, ch, _), n in piece_of.items() if (kd, ch) == (kind, c))

            PR = SR // 2

            def piece_slot(n):
                q = (n + PAN_FFN % SR // 2) % PR
                src, k = pieces[n]
                w = src.shape[2]
                return wS[:, 2 * q:2 * q + 2, :].rearrange("p a n -> p (a n)")[:, 0:k * w]\
                    .rearrange("p (k n) -> p k n", k=k)
            with Phase(["h1", "h2", "h3", "kt", "kev", "qzero", "q", "sc", "cmax", "cexp", "pn", "pt", "ptev",
                        "o", "oev", "ht", "hrow", "sg", "hu", "hut", "hid", "piece_used", "hsum", "fsq",
                        "yev", "grow_in", "out_done"] + [f"piece_in{q}" for q in range(PR)]
                       + [t + n for t in ("n2", "n3") for n in SNORM]) as (b, s):

                @b.sync
                def _(sp):
                    sp.dma_start(grow[:], bass.AP(tensor=g_final.tensor, offset=0, ap=[[0, S], [1, D]]))\
                      .then_inc(s["grow_in"], 16)
                    s_load(sp, PAN_OUT + SR, PAN_FFN)
                    for n in range(len(pieces)):
                        if n < PR:
                            sp.wait_ge(sstream["lin_out"], first_out[PAN_FFN - SR + 2 * n + 2])
                        else:
                            sp.wait_ge(s["piece_used"], n - PR + 1)
                        sp.dma_start(piece_slot(n), pieces[n][0]).then_inc(s[f"piece_in{n % PR}"], 16)
                    sp.wait_ge(s["yev"], 1)
                    sp.dma_start(y_sample.rearrange("b t d -> (b t) d"), yoS[:]).then_inc(s["out_done"], 16)
                    sp.wait_ge(s["out_done"], 16)

                @b.gpsimd
                def _(pool):
                    pool.memset(Qc[:], 0.0).then_inc(s["qzero"], 1)

                @b.scalar
                def _(act):
                    for n in range(2 * NB):
                        act.wait_ge(s["kt"], n + 1)
                        act.activation(kmS[:, n // 2, :, (n % 2) * P:(n % 2) * P + P],
                                       G[:, n % 2, :].rearrange("p (h m) -> p h m", m=P), ACT.Copy)\
                           .then_inc(s["kev"], 1)
                    act.wait_ge(s["h1"], KT)
                    s_norm_act(act, s, "n2")
                    act.wait_ge(s["cmax"], 1)
                    for g in range(2):
                        act.activation(sX[:, g, :], G[:, 2, g * NMEM:g * NMEM + NMEM], ACT.Exp,
                                       bias=stx[:, 0, g:g + 1], accum_out=stx[:, 1, g:g + 1]).then_inc(s["cexp"], 1)
                    act.wait_ge(s["h2"], KT)
                    s_norm_act(act, s, "n3")
                    act.wait_ge(s["ht"], 1)
                    act.activation(hrow[:], G[0:S, 2:4, :].rearrange("p a n -> p (a n)"), ACT.Copy)\
                       .then_inc(s["hrow"], 1)
                    for c in range(NFC):
                        w = FC[c][1] - FC[c][0]
                        act.wait_ge(s["piece_used"], through("gate", c))
                        if c >= 2:
                            act.wait_ge(s["hu"], c - 1)
                        act.activation(sgS[:, c % 2, 0:w], G[0:S, c % 2, 0:w], ACT.Silu).then_inc(s["sg"], 1)
                    act.wait_ge(s["hsum"], 1)
                    act.activation(junkF[:], hrow[:], ACT.Square, accum_out=nrm[:, 0:1]).then_inc(s["fsq"], 1)

                @b.vector
                def _(dve):
                    for n in range(KT):
                        s_residual(dve, s, "h1", O_OUT, n)
                    s_norm_dve(dve, s, "n2", PV_CROSS, xS)
                    dve.wait_ge(s["qzero"], 1)
                    for h in range(CH):
                        dve.wait_ge(sstream["lin_out"], O_CQ + h + 1)
                        dve.tensor_scalar(Qc[:, :, h, h, :],
                                          L[:, (O_CQ + h) % 2, 0:S].rearrange("p (b t) -> p b t", t=TS),
                                          P ** -0.5, None, ALU.mult).then_inc(s["q"], 1)
                    dve.wait_ge(s["sc"], 1)
                    dve.tensor_reduce(stx[:, 0, :], G[:, 2, :].rearrange("p (g m) -> p g m", g=2), AX_X, ALU.max,
                                      negate=True).then_inc(s["cmax"], 1)
                    dve.wait_ge(s["cexp"], 2)
                    dve.reciprocal(stx[:, 2, :], stx[:, 1, :])
                    dve.drain()
                    dve.tensor_tensor(sX[:], sX[:], stx[:, 2, :].unsqueeze(2).to_broadcast([P, 2, NMEM]), ALU.mult)\
                       .then_inc(s["pn"], 1)
                    dve.wait_ge(s["pt"], 1)
                    dve.tensor_copy(pxT[:], G[:, 3, :].rearrange("p (g m r) -> p g m r", g=2, m=2))\
                       .then_inc(s["ptev"], 1)
                    dve.wait_ge(s["o"], 1)
                    dve.tensor_copy(oS[:], G[:, 0, 0:CH * S].rearrange("p (h t) -> p h t", t=S)).then_inc(s["oev"], 1)
                    for n in range(KT):
                        s_residual(dve, s, "h2", O_CO, n)
                    s_norm_dve(dve, s, "n3", PV_FFN, xS)
                    def hidden_back(c):
                        nf = (FC[c][1] - FC[c][0]) // P
                        dve.wait_ge(s["hut"], c + 1)
                        if c >= 2:
                            dve.wait_ge(s["piece_used"], through("down", c - 2))
                        dve.tensor_copy(hid[:, c % 2, 0:nf, :],
                                        G[:, 4 + c % 2, 0:nf * S].rearrange("p (f t) -> p f t", t=S))\
                           .then_inc(s["hid"], 1)

                    for c in range(NFC + 1):
                        if c >= 1:
                            hidden_back(c - 1)
                        if c < NFC:
                            w = FC[c][1] - FC[c][0]
                            dve.wait_ge(s["sg"], c + 1)
                            dve.wait_ge(s["piece_used"], through("up", c))
                            dve.tensor_tensor(huS[:, c % 2, 0:w], sgS[:, c % 2, 0:w], G[0:S, 2 + c % 2, 0:w],
                                              ALU.mult).then_inc(s["hu"], 1)
                    dve.wait_ge(s["piece_used"], len(pieces))
                    dve.wait_ge(s["hrow"], 1)
                    dve.tensor_tensor(hrow[:], L[0:S, 0:2, :].rearrange("p a n -> p (a n)"), hrow[:], ALU.add)\
                       .then_inc(s["hsum"], 1)
                    dve.wait_ge(s["fsq"], 1)
                    dve.tensor_scalar(nrm[:, 1:2], nrm[:, 0:1], 1.0 / D, EPS, ALU.mult, ALU.add)
                    dve.drain()
                    rsqrt(dve, nrm[:, 1:2], nrm[:, 2:3], nrm[:, 3:4])
                    dve.wait_ge(s["grow_in"], 16)
                    dve.scalar_tensor_tensor(yoS[:], hrow[:], nrm[:, 2:3], grow[:], ALU.mult, ALU.mult)\
                       .then_inc(s["yev"], 1)

                @b.tensor
                def _(pe):
                    for n in range(PAN_OUT, PAN_CQ):
                        s_multiply(pe, n, xS, lambda o: o >= O_OUT + 2 and pe.wait_ge(s["h1"], o - O_OUT - 1))
                    pe.wait_ge(sstream["mem_in"], 16 * 2 * NB)
                    for n in range(2 * NB):
                        if n >= 2:
                            pe.wait_ge(s["kev"], n - 1)
                        for h in range(CH):
                            last = pe.transpose(G[:, n % 2, h * P:h * P + P], memK[:, n // 2, n % 2, h * P:h * P + P],
                                                ident[:])
                        last.then_inc(s["kt"], 1)
                    s_norm_pe(pe, s, "n2")
                    pe.wait_ge(s["n2x"], 1)
                    for n in range(CH):
                        s_multiply(pe, PAN_CQ + n, xS, lambda o: o >= O_CQ + 2 and pe.wait_ge(s["q"], o - O_CQ - 1))
                    pe.wait_ge(s["kev"], 2 * NB)
                    pe.wait_ge(s["q"], CH)
                    for bb in range(NB):
                        r = slice(32 * (bb % 4), 32 * (bb % 4) + 32)
                        g = bb // 4
                        for h in range(CH):
                            last = pe.matmul(G[r, 2, g * NMEM:g * NMEM + NMEM],
                                             Qc[:, bb, h].rearrange("p a t -> p (a t)"), kmS[:, bb, h, :],
                                             start=(h == 0), stop=(h == CH - 1), tile_position=(0, 32 * (bb % 4)))
                    last.then_inc(s["sc"], 1)
                    pe.wait_ge(s["pn"], 1)
                    for g in range(2):
                        for m in range(2):
                            i = 2 * g + m
                            last = pe.transpose(G[:, 3, i * P:i * P + P], sX[:, g, m * P:m * P + P], ident[:])
                    last.then_inc(s["pt"], 1)
                    pe.wait_ge(s["ptev"], 1)
                    for h in range(CH):
                        for bb in range(NB):
                            r0 = 32 * (bb % 4) + TS * h
                            for m in range(2):
                                last = pe.matmul(G[:, 0, h * S + bb * TS:h * S + bb * TS + TS],
                                                 memV[:, bb, m, h * P:h * P + P], pxT[:, bb // 4, m, r0:r0 + TS],
                                                 start=(m == 0), stop=(m == 1))
                    last.then_inc(s["o"], 1)
                    pe.wait_ge(s["oev"], 1)
                    for n in range(4):
                        s_multiply(pe, PAN_CO + n, oS, lambda o: o >= O_CO + 2 and pe.wait_ge(s["h2"], o - O_CO - 1))
                    pe.wait_ge(s["h2"], KT)
                    for i in range(KT):
                        last = pe.transpose(G[0:S, 2 + i // 4, (i % 4) * P:(i % 4) * P + P], hS[:, i, :], ident[:])
                    last.then_inc(s["ht"], 1)
                    s_norm_pe(pe, s, "n3")
                    pe.wait_ge(s["n3x"], 1)

                    def take(key):
                        n = piece_of[key]
                        pe.wait_ge(s[f"piece_in{n % PR}"], 16 * (n // PR + 1))
                        return piece_slot(n)

                    def product(kind, c, bank):
                        w = FC[c][1] - FC[c][0]
                        for kh in range(2):
                            piece = take((kind, c, kh))
                            for k in range(4):
                                last = pe.matmul(G[0:S, bank, 0:w], xS[:, 4 * kh + k, :], piece[:, k, :],
                                                 start=(kh + k == 0), stop=(kh == 1 and k == 3))
                            last.then_inc(s["piece_used"], 1)

                    for c in range(NFC + 1):
                        if c < NFC:
                            if c >= 2:
                                pe.wait_ge(s["sg"], c - 1)
                            product("gate", c, c % 2)
                        if c >= 1:
                            pe.wait_ge(s["hu"], c)
                            if c >= 3:
                                pe.wait_ge(s["hid"], c - 2)
                            for f in range((FC[c - 1][1] - FC[c - 1][0]) // P):
                                last = pe.transpose(G[:, 4 + (c - 1) % 2, f * S:f * S + S],
                                                    huS[:, (c - 1) % 2, f * P:f * P + P], ident[0:S, 0:S])
                            last.then_inc(s["hut"], 1)
                        if c < NFC:
                            if c == 0:
                                pe.wait_ge(s["hrow"], 1)
                            if c >= 2:
                                pe.wait_ge(s["hu"], c - 1)
                            product("up", c, 2 + c % 2)
                        if c >= 1:
                            pe.wait_ge(s["hid"], c)
                            nh = (FC[c - 1][1] - FC[c - 1][0]) // 256
                            for fh in range(nh):
                                piece = take(("down", c - 1, fh))
                                for k in range(2):
                                    for half in range(2):
                                        last = pe.matmul(L[0:S, half, :], hid[:, (c - 1) % 2, 2 * fh + k, :],
                                                         piece[:, k, half * 512:half * 512 + 512],
                                                         start=(c == 1 and fh + k == 0),
                                                         stop=(c == NFC and fh == nh - 1 and k == 1))
                                last.then_inc(s["piece_used"], 1)


_INS = ['x_prompt', 'x_sample', 'mem_prompt', 'state_conv', 'state_ssm', 'cache_swa_k', 'cache_swa_v',
        'cache_mem_k', 'cache_mem_v', 'rel_bias', 'g_mix', 'w_in', 'conv_w', 'conv_b', 'dt_bias', 'a_log',
        'd_skip', 'g_ssd_norm', 'sinks', 'w_out', 'g_cross', 'g_mem', 'w_cq', 'w_ck', 'w_cv', 'w_co', 'g_ffn',
        'w_gate', 'w_up', 'w_down', 'g_final']
_OUTS = [(1, 2048, 1024), (8, 8, 1024), (1, 1, 3, 1024), (1, 1, 8, 64, 128), (1, 1, 128, 2, 64),
         (1, 1, 128, 2, 64), (1, 1, 256, 4, 128), (1, 1, 256, 4, 128), (1, 8, 3, 1024), (1, 8, 8, 64, 128),
         (1, 8, 128, 2, 64), (1, 8, 128, 2, 64)]


def shape_tables():
    import math
    import numpy as np

    onehot = np.zeros((32, RLEN), np.float32)
    mask = np.full((HS, RLEN), NEG, np.float32)
    for m in range(RLEN):
        dist = 255 - m
        if not 0 <= dist < WIN:
            continue
        bucket = dist
        if dist >= 16:
            big = np.float32(np.log(np.float32(dist) / np.float32(16)))
            bucket = min(31, 16 + int(np.float32(big / np.float32(math.log(8)) * np.float32(16))))
        onehot[bucket, m] = 1
        mask[:, m] = 0
    return onehot, mask


def kernel(**inputs):
    import numpy as _np
    import concourse.bacc as _bacc
    from concourse import mybir as _mybir
    from concourse.bass_utils import run_bass_kernel_spmd as _run

    nc = _bacc.Bacc("TRN2", target_bir_lowering=False, num_devices=1)
    arrays, args = {}, []
    onehot, mask = shape_tables()
    for name in _INS + ["bucket_onehot", "row_mask"]:
        a = {"bucket_onehot": onehot, "row_mask": mask}[name] if name in ("bucket_onehot", "row_mask") \
            else _np.ascontiguousarray(inputs[name])
        arrays[f"in_{name}_dram"] = a
        args.append(nc.dram_tensor(f"in_{name}_dram", a.shape, _mybir.dt.from_np(a.dtype), kind="ExternalInput").ap())
    for i, shape in enumerate(_OUTS):
        args.append(nc.dram_tensor(f"out_{i}_dram", shape, _mybir.dt.float32, kind="ExternalOutput").ap())
    build(nc, *args)
    r = _run(nc, [arrays], core_ids=[0])
    return tuple(r.results[0][f"out_{i}_dram"] for i in range(len(_OUTS)))
```
